# Optimizing a Trainium2 kernel written in Bass

```python
import math
import jax, jax.numpy as jnp
from jax import lax
import numpy as np

D_MODEL = 2048
BATCH = 1
SEQ = 256
DEPTH = 1

HEAD_DIM = 128
N_HEADS_SB = 8
N_HEADS_DSA = 8
N_IDX_HEADS = 16
IDX_DIM = 64
TOPK_MAX = 256
D_FF = 5632
CONV_WIDTH = 3
N_BUCKETS = 32
MAX_DISTANCE = 128
Q_BLOCK = 128
EPS = 1e-6
W_SB = N_HEADS_SB * HEAD_DIM
W_DSA = N_HEADS_DSA * HEAD_DIM
IN_SIZES = (W_SB, W_SB, W_SB, W_DSA, W_DSA, W_DSA,
            N_IDX_HEADS * IDX_DIM, IDX_DIM, N_IDX_HEADS, D_MODEL, D_MODEL)
P_IN = 3 * W_SB + 3 * W_DSA + N_IDX_HEADS * IDX_DIM + IDX_DIM + N_IDX_HEADS + 2 * D_MODEL


def rms_norm(x, g):
    xf = x.astype(jnp.float32)
    y = xf * lax.rsqrt(jnp.mean(xf * xf, axis=-1, keepdims=True) + EPS)
    return (y * g.astype(jnp.float32)).astype(x.dtype)

def modulate(h, shift, scale):
    return h * (1.0 + scale[:, None, :]) + shift[:, None, :]

def split_columns(z):
    cuts, acc = [], 0
    for s in IN_SIZES[:-1]:
        acc += s
        cuts.append(acc)
    return jnp.split(z, cuts, axis=-1)

def rel_bucket(dist):
    n = jnp.maximum(dist, 0)
    max_exact = N_BUCKETS // 2
    nf = jnp.maximum(n, 1).astype(jnp.float32)
    large = max_exact + (jnp.log(nf / max_exact) / math.log(MAX_DISTANCE / max_exact)
                         * (N_BUCKETS - max_exact)).astype(jnp.int32)
    large = jnp.minimum(large, N_BUCKETS - 1)
    return jnp.where(n < max_exact, n, large)

def stick_breaking_attention(q, k, v):
    B, S, H, Dh = q.shape
    n_blk = S // Q_BLOCK
    kf = k.astype(jnp.float32)
    vf = v.astype(jnp.float32)
    key_pos = jnp.arange(S)
    scale = HEAD_DIM ** -0.5

    def block(i):
        start = i * Q_BLOCK
        qb = lax.dynamic_slice_in_dim(q, start, Q_BLOCK, axis=1).astype(jnp.float32)
        z = jnp.einsum('bqhd,bshd->bhqs', qb, kf) * scale
        q_pos = start + jnp.arange(Q_BLOCK)
        causal = key_pos[None, :] < q_pos[:, None]
        log_beta = jax.nn.log_sigmoid(z)
        log_keep = jnp.where(causal, jax.nn.log_sigmoid(-z), 0.0)
        suffix = lax.cumsum(log_keep, axis=3, reverse=True) - log_keep
        a = jnp.where(causal, jnp.exp(log_beta + suffix), 0.0)
        return jnp.einsum('bhqs,bshd->bqhd', a, vf)

    out = lax.map(block, jnp.arange(n_blk))
    return out.transpose(1, 0, 2, 3, 4).reshape(B, S, H * Dh).astype(q.dtype)

def indexer_sparse_attention(q, k, v, q_idx, k_idx, w_idx, rel_bias):
    B, S, H, Dh = q.shape
    n_blk = S // Q_BLOCK
    n_sel = min(TOPK_MAX, S // 4)
    kf = k.astype(jnp.float32)
    vf = v.astype(jnp.float32)
    kif = k_idx.astype(jnp.float32)
    key_pos = jnp.arange(S)
    scale = HEAD_DIM ** -0.5
    idx_scale = IDX_DIM ** -0.5
    gather = jax.vmap(lambda arr, ix: arr[ix])

    def block(i):
        start = i * Q_BLOCK
        q_pos = start + jnp.arange(Q_BLOCK)
        qi = lax.dynamic_slice_in_dim(q_idx, start, Q_BLOCK, axis=1).astype(jnp.float32)
        wi = lax.dynamic_slice_in_dim(w_idx, start, Q_BLOCK, axis=1).astype(jnp.float32)
        per_head = jax.nn.relu(jnp.einsum('bqhd,bsd->bqhs', qi, kif) * idx_scale)
        score = jnp.einsum('bqh,bqhs->bqs', wi, per_head)
        causal = key_pos[None, :] <= q_pos[:, None]
        score = jnp.where(causal[None], score, -jnp.inf)
        _, sel = lax.top_k(score, n_sel)
        valid = sel <= q_pos[None, :, None]
        k_sel = gather(kf, sel)
        v_sel = gather(vf, sel)
        qb = lax.dynamic_slice_in_dim(q, start, Q_BLOCK, axis=1).astype(jnp.float32)
        logits = jnp.einsum('bqhd,bqkhd->bhqk', qb, k_sel) * scale
        bias = rel_bias.astype(jnp.float32)[rel_bucket(q_pos[None, :, None] - sel)]
        logits = logits + bias.transpose(0, 3, 1, 2)
        logits = jnp.where(valid[:, None], logits, -jnp.inf)
        p = jax.nn.softmax(logits, axis=-1)
        return jnp.einsum('bhqk,bqkhd->bqhd', p, v_sel)

    out = lax.map(block, jnp.arange(n_blk))
    return out.transpose(1, 0, 2, 3, 4).reshape(B, S, H * Dh).astype(q.dtype)

def causal_dwconv(a, w, b):
    S = a.shape[1]
    ap = jnp.pad(a, ((0, 0), (CONV_WIDTH - 1, 0), (0, 0)))
    y = b
    for j in range(CONV_WIDTH):
        y = y + ap[:, j:j + S, :] * w[j]
    return y

def first_inputs(seed: int = 0) -> dict:
    key = jax.random.key(seed)
    ks = jax.random.split(key, 20)
    f32 = jnp.float32

    def nrm(k, shape, fan_in):
        return jax.random.normal(k, shape, f32) * fan_in ** -0.5

    return {
        'x': jax.random.normal(ks[0], (BATCH, SEQ, D_MODEL), f32),
        'c': jax.random.normal(ks[1], (BATCH, D_MODEL), f32),
        'w_ada': 0.5 * nrm(ks[2], (DEPTH, D_MODEL, 6 * D_MODEL), D_MODEL),
        'b_ada': 0.01 * jax.random.normal(ks[3], (DEPTH, 6 * D_MODEL), f32),
        'g_mix': 1.0 + 0.05 * jax.random.normal(ks[4], (DEPTH, D_MODEL), f32),
        'w_in': nrm(ks[5], (DEPTH, D_MODEL, P_IN), D_MODEL),
        'w_o_sb': nrm(ks[6], (DEPTH, W_SB, D_MODEL), W_SB),
        'w_o_dsa': nrm(ks[7], (DEPTH, W_DSA, D_MODEL), W_DSA),
        'w_out': nrm(ks[8], (DEPTH, D_MODEL, D_MODEL), D_MODEL),
        'rel_bias': 0.5 * jax.random.normal(ks[9], (N_BUCKETS, N_HEADS_DSA), f32),
        'g_ffn': 1.0 + 0.05 * jax.random.normal(ks[10], (DEPTH, D_MODEL), f32),
        'w_gate': nrm(ks[11], (DEPTH, D_MODEL, D_FF), D_MODEL),
        'w_up': nrm(ks[12], (DEPTH, D_MODEL, D_FF), D_MODEL),
        'conv_w': nrm(ks[13], (DEPTH, CONV_WIDTH, D_FF), CONV_WIDTH),
        'conv_b': 0.01 * jax.random.normal(ks[14], (DEPTH, D_FF), f32),
        'w_down': nrm(ks[15], (DEPTH, D_FF, D_MODEL), D_FF),
        'g_final': 1.0 + 0.05 * jax.random.normal(ks[16], (D_MODEL,), f32),
    }

def first_block(x, c, w_ada, b_ada, g_mix, w_in, w_o_sb, w_o_dsa, w_out, rel_bias,
              g_ffn, w_gate, w_up, conv_w, conv_b, w_down, g_final):
    B, S, _ = x.shape
    c_act = jax.nn.silu(c)
    for l in range(DEPTH):
        mod = c_act @ w_ada[l] + b_ada[l]
        sh1, sc1, gt1, sh2, sc2, gt2 = jnp.split(mod, 6, axis=-1)

        h = modulate(rms_norm(x, g_mix[l]), sh1, sc1)
        z = h @ w_in[l]
        (q_sb, k_sb, v_sb, q_ds, k_ds, v_ds, q_ix, k_ix, w_ix,
         gate_sb, gate_ds) = split_columns(z)
        hs = (B, S, N_HEADS_SB, HEAD_DIM)
        hd = (B, S, N_HEADS_DSA, HEAD_DIM)
        o_sb = stick_breaking_attention(q_sb.reshape(hs), k_sb.reshape(hs), v_sb.reshape(hs))
        o_ds = indexer_sparse_attention(
            q_ds.reshape(hd), k_ds.reshape(hd), v_ds.reshape(hd),
            q_ix.reshape(B, S, N_IDX_HEADS, IDX_DIM), k_ix,
            w_ix * (N_IDX_HEADS ** -0.5), rel_bias)
        merged = (jax.nn.sigmoid(gate_sb) * (o_sb @ w_o_sb[l])
                  + jax.nn.sigmoid(gate_ds) * (o_ds @ w_o_dsa[l]))
        x = x + gt1[:, None, :] * (merged @ w_out[l])

        h = modulate(rms_norm(x, g_ffn[l]), sh2, sc2)
        a = causal_dwconv(h @ w_gate[l], conv_w[l], conv_b[l])
        y = (jax.nn.silu(a) * (h @ w_up[l])) @ w_down[l]
        x = x + gt2[:, None, :] * y
    return rms_norm(x, g_final)


N_MIXERS = 3

GLA_HEADS = 4
GLA_DK = D_MODEL // 2
GLA_DV = D_MODEL
GLA_HK = GLA_DK // GLA_HEADS
GLA_HV = GLA_DV // GLA_HEADS
GLA_RANK = 16
GLA_TAU = 16.0
GLA_CHUNK = 64
GLA_IN = 2 * GLA_DK + 2 * GLA_DV + GLA_RANK

POOL_WINDOWS = (2, 4, 8, 16)
POOL_GROUPS = 4
POOL_GW = D_MODEL // POOL_GROUPS

DIFF_HEADS = 8
DIFF_HD = D_MODEL // DIFF_HEADS // 2
DIFF_VD = 2 * DIFF_HD
REL_BUCKETS = 32
REL_MAX_DIST = 128

FFN_HIDDEN = ((8 * D_MODEL + 3 * 256 - 1) // (3 * 256)) * 256

N_GLA = (DEPTH + 2) // N_MIXERS
N_POOL = (DEPTH + 1) // N_MIXERS
N_DIFF = DEPTH // N_MIXERS


def rms_norm_2(x, g):
    xf = x.astype(jnp.float32)
    y = xf * lax.rsqrt(jnp.mean(xf * xf, axis=-1, keepdims=True) + EPS)
    return (y * g.astype(jnp.float32)).astype(x.dtype)

def gla_mixer(h, w_in, w_a2, b_a, g_norm, w_out):
    B, S, _ = h.shape
    f32 = jnp.float32
    C = GLA_CHUNK
    nc = S // C
    proj = h @ w_in
    q, k, v, r, a_lr = jnp.split(
        proj, [GLA_DK, 2 * GLA_DK, 2 * GLA_DK + GLA_DV, 2 * GLA_DK + 2 * GLA_DV], axis=-1)
    log_a = jax.nn.log_sigmoid((a_lr @ w_a2 + b_a).astype(f32)) / GLA_TAU

    def to_chunks(t, hd):
        return t.astype(f32).reshape(B, nc, C, GLA_HEADS, hd).transpose(1, 0, 3, 2, 4)

    qc = to_chunks(q, GLA_HK) * (GLA_HK ** -0.5)
    kc = to_chunks(k, GLA_HK)
    vc = to_chunks(v, GLA_HV)
    bc = jnp.cumsum(to_chunks(log_a, GLA_HK), axis=3)
    causal = jnp.tril(jnp.ones((C, C), dtype=bool))[:, :, None]

    def step(state, inp):
        qb, kb, vb, bb = inp
        o_inter = jnp.einsum('bhtd,bhdv->bhtv', qb * jnp.exp(bb), state)
        diff = bb[:, :, :, None, :] - bb[:, :, None, :, :]
        decay = jnp.exp(jnp.where(causal, diff, -jnp.inf))
        scores = jnp.einsum('bhtd,bhsd,bhtsd->bhts', qb, kb, decay)
        o_intra = jnp.einsum('bhts,bhsv->bhtv', scores, vb)
        b_last = bb[:, :, -1:, :]
        k_dec = kb * jnp.exp(b_last - bb)
        state = jnp.exp(b_last[:, :, 0, :, None]) * state + jnp.einsum('bhsd,bhsv->bhdv', k_dec, vb)
        return state, o_inter + o_intra

    s0 = jnp.zeros((B, GLA_HEADS, GLA_HK, GLA_HV), f32)
    _, o = lax.scan(step, s0, (qc, kc, vc, bc))
    o = o.transpose(1, 0, 3, 2, 4).reshape(B, S, GLA_HEADS, GLA_HV)
    o = rms_norm_2(o, g_norm).reshape(B, S, GLA_DV) * jax.nn.silu(r.astype(f32))
    return o.astype(h.dtype) @ w_out

def pool_mixer(h, w_pool, scale):
    B, S, D = h.shape
    f32 = jnp.float32
    hf = h.astype(f32)
    cs = jnp.pad(jnp.cumsum(hf, axis=1), ((0, 0), (1, 0), (0, 0)))
    t = jnp.arange(S)
    outs = []
    for g, w in enumerate(POOL_WINDOWS):
        c = cs[:, :, g * POOL_GW:(g + 1) * POOL_GW]
        start = jnp.maximum(t + 1 - w, 0)
        count = (t + 1 - start).astype(f32)
        pooled = (c[:, 1:] - c[:, start]) / count[None, :, None]
        outs.append(pooled - hf[:, :, g * POOL_GW:(g + 1) * POOL_GW])
    y = jnp.stack(outs, axis=2).astype(h.dtype)
    y = jnp.einsum('bsgc,gcd->bsgd', y, w_pool).reshape(B, S, D)
    return y * scale

def rel_bucket_2(rel):
    n = jnp.maximum(rel, 0)
    max_exact = REL_BUCKETS // 2
    nf = jnp.maximum(n, 1).astype(jnp.float32)
    large = max_exact + (jnp.log(nf / max_exact) / math.log(REL_MAX_DIST / max_exact)
                         * (REL_BUCKETS - max_exact)).astype(jnp.int32)
    large = jnp.minimum(large, REL_BUCKETS - 1)
    return jnp.where(n < max_exact, n, large)

def diff_attn_mixer(h, w_in, q_gain, k_gain, lam_params, sub_gain, w_out, rel_table, layer_idx):
    B, S, D = h.shape
    f32 = jnp.float32
    H2 = 2 * DIFF_HEADS
    proj = h @ w_in
    q, k, v = jnp.split(proj, [D, 2 * D], axis=-1)
    q = rms_norm_2(q.reshape(B, S, H2, DIFF_HD), q_gain).transpose(0, 2, 1, 3)
    k = rms_norm_2(k.reshape(B, S, H2, DIFF_HD), k_gain).transpose(0, 2, 1, 3)
    v = v.reshape(B, S, DIFF_HEADS, DIFF_VD).transpose(0, 2, 1, 3)
    lam_init = 0.8 - 0.6 * math.exp(-0.3 * layer_idx)
    lp = lam_params.astype(f32)
    lam = jnp.exp(jnp.sum(lp[0] * lp[1])) - jnp.exp(jnp.sum(lp[2] * lp[3])) + lam_init
    nb = S // Q_BLOCK
    qb = q.reshape(B, H2, nb, Q_BLOCK, DIFF_HD).transpose(2, 0, 1, 3, 4)
    kpos = jnp.arange(S)
    scale = DIFF_HD ** -0.5

    def block(args):
        qblk, bi = args
        qpos = bi * Q_BLOCK + jnp.arange(Q_BLOCK)
        rel = qpos[:, None] - kpos[None, :]
        bias = rel_table[rel_bucket_2(rel)].astype(f32).transpose(2, 0, 1)
        logits = jnp.einsum('bhqd,bhkd->bhqk', qblk, k).astype(f32) * scale + bias
        logits = jnp.where(rel >= 0, logits, -jnp.inf)
        p = jax.nn.softmax(logits, axis=-1).reshape(B, DIFF_HEADS, 2, Q_BLOCK, S)
        attn = p[:, :, 0] - lam * p[:, :, 1]
        return jnp.einsum('bhqk,bhkd->bhqd', attn.astype(v.dtype), v)

    o = lax.map(block, (qb, jnp.arange(nb)))
    o = o.transpose(1, 0, 3, 2, 4).reshape(B, S, DIFF_HEADS, DIFF_VD)
    o = rms_norm_2(o, sub_gain) * (1.0 - lam_init)
    return o.reshape(B, S, D).astype(h.dtype) @ w_out

def swiglu(h, w_gu, w_down):
    g, u = jnp.split(h @ w_gu, 2, axis=-1)
    return (jax.nn.silu(g) * u) @ w_down

def second_inputs(seed: int = 0) -> dict:
    key = jax.random.key(seed)
    ks = jax.random.split(key, 20)
    D = D_MODEL
    nrm = jax.random.normal
    out_scale = (2 * DEPTH) ** -0.5
    return {
        "x": nrm(ks[0], (BATCH, SEQ, D), jnp.float32),
        "norm_g": 1.0 + 0.02 * nrm(ks[1], (DEPTH, 2, D), jnp.float32),
        "gla_w_in": nrm(ks[2], (N_GLA, D, GLA_IN), jnp.float32) * D ** -0.5,
        "gla_w_a2": nrm(ks[3], (N_GLA, GLA_RANK, GLA_DK), jnp.float32) * GLA_RANK ** -0.5,
        "gla_b_a": 0.1 * nrm(ks[4], (N_GLA, GLA_DK), jnp.float32),
        "gla_g_norm": 1.0 + 0.02 * nrm(ks[5], (N_GLA, GLA_HV), jnp.float32),
        "gla_w_out": nrm(ks[6], (N_GLA, GLA_DV, D), jnp.float32) * GLA_DV ** -0.5 * out_scale,
        "pool_w": nrm(ks[7], (N_POOL, POOL_GROUPS, POOL_GW, POOL_GW), jnp.float32) * POOL_GW ** -0.5,
        "pool_scale": 1.0 + 0.1 * nrm(ks[8], (N_POOL, D), jnp.float32),
        "diff_w_in": nrm(ks[9], (N_DIFF, D, 3 * D), jnp.float32) * D ** -0.5,
        "diff_q_gain": 1.0 + 0.02 * nrm(ks[10], (N_DIFF, DIFF_HD), jnp.float32),
        "diff_k_gain": 1.0 + 0.02 * nrm(ks[11], (N_DIFF, DIFF_HD), jnp.float32),
        "diff_lambda": 0.1 * nrm(ks[12], (N_DIFF, 4, DIFF_HD), jnp.float32),
        "diff_sub_gain": 1.0 + 0.02 * nrm(ks[13], (N_DIFF, DIFF_VD), jnp.float32),
        "diff_w_out": nrm(ks[14], (N_DIFF, D, D), jnp.float32) * D ** -0.5 * out_scale,
        "rel_bias": 0.5 * nrm(ks[15], (REL_BUCKETS, 2 * DIFF_HEADS), jnp.float32),
        "ffn_w_gu": nrm(ks[16], (DEPTH, D, 2 * FFN_HIDDEN), jnp.float32) * D ** -0.5,
        "ffn_w_down": nrm(ks[17], (DEPTH, FFN_HIDDEN, D), jnp.float32) * FFN_HIDDEN ** -0.5 * out_scale,
    }

def second_block(x, norm_g, gla_w_in, gla_w_a2, gla_b_a, gla_g_norm, gla_w_out,
              pool_w, pool_scale, diff_w_in, diff_q_gain, diff_k_gain, diff_lambda,
              diff_sub_gain, diff_w_out, rel_bias, ffn_w_gu, ffn_w_down):
    for i in range(DEPTH):
        kind = i % N_MIXERS
        slot = i // N_MIXERS
        h = rms_norm_2(x, norm_g[i, 0])
        if kind == 0:
            y = gla_mixer(h, gla_w_in[slot], gla_w_a2[slot], gla_b_a[slot],
                          gla_g_norm[slot], gla_w_out[slot])
        elif kind == 1:
            y = pool_mixer(h, pool_w[slot], pool_scale[slot])
        else:
            y = diff_attn_mixer(h, diff_w_in[slot], diff_q_gain[slot], diff_k_gain[slot],
                                diff_lambda[slot], diff_sub_gain[slot], diff_w_out[slot],
                                rel_bias, i)
        x = x + y.astype(x.dtype)
        x = x + swiglu(rms_norm_2(x, norm_g[i, 1]), ffn_w_gu[i], ffn_w_down[i]).astype(x.dtype)
    return x


def setup_inputs(seed=0):
    out = dict(first_inputs(seed))
    for name, value in second_inputs(seed + 1).items():
        if name != "x":
            out[name + "_2"] = value
    return out


def reference(
    x, c, w_ada, b_ada, g_mix, w_in, w_o_sb, w_o_dsa, w_out, rel_bias, g_ffn, w_gate, w_up,
    conv_w, conv_b, w_down, g_final, norm_g_2, gla_w_in_2, gla_w_a2_2, gla_b_a_2, gla_g_norm_2,
    gla_w_out_2, pool_w_2, pool_scale_2, diff_w_in_2, diff_q_gain_2, diff_k_gain_2,
    diff_lambda_2, diff_sub_gain_2, diff_w_out_2, rel_bias_2, ffn_w_gu_2, ffn_w_down_2,
):
    x = first_block(
        x, c, w_ada, b_ada, g_mix, w_in, w_o_sb, w_o_dsa, w_out, rel_bias, g_ffn, w_gate, w_up,
        conv_w, conv_b, w_down, g_final,
    )
    return second_block(
        x, norm_g_2, gla_w_in_2, gla_w_a2_2, gla_b_a_2, gla_g_norm_2, gla_w_out_2, pool_w_2,
        pool_scale_2, diff_w_in_2, diff_q_gain_2, diff_k_gain_2, diff_lambda_2, diff_sub_gain_2,
        diff_w_out_2, rel_bias_2, ffn_w_gu_2, ffn_w_down_2,
    )


_drawn_inputs = setup_inputs


def setup_inputs(seed=0):
    import zlib

    import numpy as np

    out = dict(_drawn_inputs(seed))
    spreads = {}
    factors = {'b_ada': 3.927, 'conv_b': 8.0, 'gla_b_a_2': 3.24, 'gla_g_norm_2': 6.832}
    for name, (base, spread) in spreads.items():
        noise = np.random.default_rng([zlib.crc32(name.encode()), seed]).standard_normal(out[name].shape)
        drawn = base * np.exp(spread * noise) if base else spread * noise
        out[name] = __import__('jax').numpy.asarray(drawn.astype(out[name].dtype))
    for name, factor in factors.items():
        out[name] = (out[name] * factor).astype(out[name].dtype)
    return out
```

```python
import concourse.bass as bass
from concourse import mybir
from contextlib import ExitStack

P = 128
S = 256
TB = S // P
D = 2048
KT = D // P
NB = 512
HD = 128
NH = 8
W = NH * HD
NIX, DIX = 16, 64
TOPK = S // 4
FF = 5632
FB = FF // NB
BUCKETS = 32
EPS = 1e-6
GH, GK, GV, GC, GR = 4, 256, 512, 64, 16
NIXW = DIX + NIX
C_IX = 6 * W + NIX * DIX
C_GATE = C_IX + NIXW
NEG = -1e30
TAKEN = -3e38
SLAB = 4 * NB
HALF = SLAB // 2
RING = 4
DS_T, DS_L, DS_P, DS_O = (0, 3, 6, 8), (2, 5, 8, 10), (5, 8, 11, 13), (7, 10, 13, 15)
AHEAD = 4
LEVELS = (32, 16, 8, 4, 2, 1)
GL_ITEMS = (1, 2, 0, 3, 4, 5, 6)

PHASES = [
    ("A", 3, 16, 2), ("B", 4, 16, 2), ("C1", 2, 16, 2), ("C2", 2, 16, 2), ("O", 2, 16, 4), ("U", 2, 16, 2),
    ("F1p", 1, 16, 2), ("F1", FB - 1, 24, 6), ("F1e", 1, 8, 4),
    ("GQ", 2, 16, 2), ("GV", 2, 16, 2), ("GR", 2, 16, 2), ("GO", 2, 16, 2),
    ("F2p", 1, 16, 2), ("F2", FB - 1, 24, 6), ("F2e", 1, 8, 4),
]
H0, G0 = {}, {}
_h = _g = 0
for _name, _n, _halves, _groups in PHASES:
    H0[_name], G0[_name] = _h, _g
    _h += _n * _halves
    _g += _n * _groups
H0["end"], G0["end"] = _h, _g


def build_program(nc, A, out):
    fp32, fp32r, u32 = mybir.dt.float32, mybir.dt.float32r, mybir.dt.uint32
    ALU, ACT, AX = mybir.AluOpType, mybir.ActivationFunctionType, mybir.AxisListType
    ds = bass.ds
    ctx = ExitStack()

    KB = 1024
    base = (nc.sbuf_base + 31) // 32 * 32
    ARENA, XB, ADA, CONST = 96 * KB, 168 * KB, 184 * KB, 200 * KB


    def at(name, shape, offset, dtype=fp32):
        return nc.alloc_sbuf_tensor_at("sb_" + name, shape, dtype, offset=base + int(offset))

    raw = at("raw", [P, RING, SLAB], 0)
    whi = at("whi", [P, RING * HALF], 32 * KB, fp32r)
    wlo = at("wlo", [P, RING * HALF], 48 * KB, fp32r)
    hi = at("act_hi", [P, KT, S], 64 * KB, fp32r)
    lo = at("act_lo", [P, KT, S], 80 * KB, fp32r)
    junk = at("junk", [P, D], 80 * KB)
    X = at("x", [P, TB, D], XB)
    ada0 = at("ada0", [P, 4, 2 * D], ARENA)
    acc0 = at("acc0", [P, 2 * D], 64 * KB)
    ixw_raw = at("ixw_raw", [P, KT * NIXW], ARENA + 64 * KB)
    ada_in = at("ada_in", [P, 2, D // 2], ADA)
    ada_acc = at("ada_acc", [P, D], ADA + 8 * KB)
    sbz = at("sbz", [P, TB, 3 * W], ARENA)
    dsz = at("dsz", [P, TB, 3 * W], ARENA + 24 * KB)
    qix = at("qix", [P, TB, W], ARENA + 48 * KB)
    oT_sb = at("oT_sb", [P, NH, S], ARENA + 64 * KB)
    oT_ds = at("oT_ds", [P, NH, S], ARENA + 16 * KB)
    gate_sb = at("gate_sb", [P, TB, D], ARENA)
    gate_ds = at("gate_ds", [P, TB, D], ARENA + 48 * KB)
    hank1 = at("hank1", [P, NH, S], XB)
    hank0 = at("hank0", [P, NH, P], XB + 8 * KB)
    selneg = at("selneg", [P, 3 * P], XB + 12 * KB)
    top8 = at("top8", [P, 8], XB + 14 * KB)
    st_sb = at("st_sb", [P, 2, 3, TB, HD], ARENA + 56 * KB)
    qk_sb = at("qk_sb", [P, 2 * S], ARENA + 62 * KB)
    st_ix = at("st_ix", [P, 2, TB, P], ARENA + 56 * KB)
    q_ixT = at("q_ixT", [P, S], ARENA + 58 * KB)
    r_ix = at("r_ix", [P, 2, 3 * P], ARENA + 59 * KB)
    score = at("score", [P, 3 * P], ARENA + 62 * KB)
    stage = at("stage", [P, 2, NB], ARENA + 40 * KB)
    merged = at("merged", [P, TB, D], ARENA + 24 * KB)
    y1 = at("y1", [P, TB, D], ARENA)
    gt_row = at("gt_row", [P, D], ARENA + 49 * KB)
    gt_bias = at("gt_bias", [P, D], ARENA + 57 * KB)
    xs = at("xs", [P, TB, D], ARENA + 24 * KB)
    aff = at("aff", [P, 2, 2 * S], ARENA + 20 * KB)
    yacc = at("yacc", [P, TB, D], ARENA)
    hid_hi = at("hid_hi", [P, 4, S], ARENA + 16 * KB, fp32r)
    hid_lo = at("hid_lo", [P, 4, S], ARENA + 20 * KB, fp32r)
    gbuf = at("gbuf", [P, TB, NB], ARENA + 24 * KB)
    ubuf = at("ubuf", [P, TB, NB], ARENA + 28 * KB)
    gpad = at("gpad", [P, 4, S + 2], ARENA + 32 * KB)
    cacc = at("cacc", [P, 4, S], ARENA + 37 * KB)
    csig = at("csig", [P, 4, S], ARENA + 41 * KB)
    hidf = at("hidf", [P, 4, S], ARENA + 45 * KB)
    dstage = at("dstage", [P, 2, NB], ARENA + 65 * KB)
    gqk = at("gqk", [P, 2 * GH * GK // P, S], ARENA)
    gv = at("gv", [P, TB, D], ARENA + 16 * KB)
    gr = at("gr", [P, TB, D], ARENA + 32 * KB)
    gb = at("gb", [P, 8 * S], ARENA + 48 * KB)
    gu = at("gu", [P, 8 * S], ARENA + 56 * KB)
    gt1 = at("gt1", [P, 8 * S], ARENA + 64 * KB)
    greset = at("greset", [P, 8 * S], ADA)
    gmask = at("gmask", [P, 7, S], ADA + 8 * KB)
    alr_raw = at("alr_raw", [P, KT * GR], ARENA + 69 * KB)
    alr_hi = at("alr_hi", [P, KT * GR], ARENA + 41 * KB, fp32r)
    alr_lo = at("alr_lo", [P, KT * GR], ARENA + 42 * KB, fp32r)
    alr = at("alr", [P, TB, GR], ARENA + 43 * KB)
    alrT = at("alrT", [GR, S], ARENA + 44 * KB)
    wa2 = at("wa2", [GR, GH * GK], CONST + 10 * KB + 512)
    gstage = at("gstage", [P, TB, NB], ARENA + 36 * KB)
    GT = ARENA + 56 * KB
    sts = at("gstates", [P, 3, 2, GV], GT)
    GU = 64 * KB
    ge = at("ge", [P, 4, 2 * S], GU)
    gm = at("gm", [P, 3, 2 * S], GU + 8 * KB)
    gsc = at("gsc", [P, 2, S], GU + 14 * KB)
    geb = at("geb", [P, 2, 2 * S], GU + 16 * KB)
    gkd = at("gkd", [P, 2, 2 * S], GU + 20 * KB)
    gkdT = at("gkdT", [P, TB, GK], GU + 24 * KB)
    gq = at("gq", [P, 2, 3, 2, P], ADA)
    gla_q = lambda h: gqk[:, 2 * h:2 * h + 2, :].rearrange("p e t -> p (e t)")
    gla_k = lambda h: gqk[:, 2 * (GH + h):2 * (GH + h) + 2, :].rearrange("p e t -> p (e t)")
    gla_sums = lambda h: gb[:, h * 2 * S:(h + 1) * 2 * S]
    gla_v = lambda h, tb: gv[:, tb, h * GV:(h + 1) * GV]
    pairs_by = lambda t, m: t.rearrange("p (n e m) -> p n e m", e=2, m=m)
    gfin = at("gfin", [P, D], CONST + 10 * KB + 512)
    gn = at("gn", [P, GV], CONST + 18 * KB + 512)
    gjunk = at("gjunk", [P, GV], GU + 28 * KB)
    gss = at("gss", [P, TB * GH], CONST + 20 * KB + 512)
    con = at("con", [P, 4 * P + 6 * P], CONST)
    ident, flip, ones, later = (con[:, n * P:(n + 1) * P] for n in range(4))
    sbmask, cneg = con[:, 4 * P:7 * P], con[:, 7 * P:10 * P]
    par1 = at("par1", [P, 112], CONST + 5 * KB)
    par2 = at("par2", [P, 120], CONST + 5 * KB + 512)
    par3 = at("par3", [P, 96], CONST + 6 * KB)
    small = at("small", [P, 256], CONST + 6 * KB + 512)
    ixw = at("ixw", [P, TB, NIXW], CONST + 7 * KB + 512)
    kdup = at("kdup", [P, TB, P], CONST + 8 * KB + 256)
    k_ixT = at("k_ixT", [P, S], CONST + 9 * KB + 256)
    wix = at("wix", [P, TB, NIX], CONST + 10 * KB + 256)
    T = CONST + 10 * KB + 512
    onehot = at("onehot", [BUCKETS, 2 * S], T)
    relb = at("relb", [BUCKETS, NH], T + 2 * KB)
    erow = at("erow", [NH, 2 * S], T + 4 * KB)
    parr = at("parr", [P, 3, P], T + 2 * KB + 64)
    az = at("az", [P, 3 * P], T)
    lb = at("lb", [P, 3 * P], T + 1536)
    lk = at("lk", [P, 3 * P], T + 3072)
    st_qk = at("st_qk", [P, 2, 2, TB, HD], T)
    st_v = at("st_v", [P, 2, TB, HD], T + 4 * KB)
    qk_ds = at("qk_ds", [P, 2 * S], T + 6 * KB)
    lg = at("lg", [P, 2, 3 * P], T + 8 * KB)
    PT = at("PT", [P, 3 * P], XB + 14 * KB + 64)

    cact, gs_mix, sh_mix, sc_ffn, sh_ffn, gs_ffn = (small[:, n * KT:(n + 1) * KT] for n in range(6))
    csg = small[:, 96:112]
    ss = small[:, 112:114]
    rstd = small[:, 114:116]
    ssum = small[:, 120:124]
    nmax = small[:, 124:128]
    grs = small[:, 128:136]
    acol = small[:, 136:137]
    c_col, g_mix, g_ffn, g_n0, g_n1, b_sh1, b_sc1 = (par1[:, n * KT:(n + 1) * KT] for n in range(7))
    b_sh2, b_sc2, conv_b, conv_w0 = par2[:, 0:16], par2[:, 16:32], par2[:, 32:76], par2[:, 76:120]
    conv_w1, conv_w2, gla_b = par3[:, 0:44], par3[:, 44:88], par3[:, 88:96]

    lin = [[ctx.enter_context(nc.psum_tensor(f"lin{g}{t}", [P, NB], fp32)) for t in range(TB)] for g in range(2)]
    aux = [ctx.enter_context(nc.psum_tensor(f"aux{n}", [P, NB], fp32)) for n in range(4)]

    tiled = lambda w: w.rearrange("(k p) n -> p k n", p=P)
    w_ada, w_in, w_out = A["w_ada"][0], tiled(A["w_in"][0]), tiled(A["w_out"][0])
    w_o = [tiled(A["w_o_sb"][0]), tiled(A["w_o_dsa"][0])]
    w_ffn = [(tiled(A["w_gate"][0]), 0, tiled(A["w_up"][0]), 0, tiled(A["w_down"][0])),
             (tiled(A["ffn_w_gu_2"][0]), 0, tiled(A["ffn_w_gu_2"][0]), FF, tiled(A["ffn_w_down_2"][0]))]
    w_gla, w_gla_out = tiled(A["gla_w_in_2"][0]), tiled(A["gla_w_out_2"][0])
    tokens = lambda x: x.rearrange("(t p) n -> p t n", p=P)
    rows = lambda v: v.rearrange("(r c) -> r c", c=P)
    e_dram = nc.dram_tensor("bias_by_distance", (NH, 2 * S), fp32, kind="Internal").ap()

    sems = {}

    def sem(name):
        if name not in sems:
            sems[name] = ctx.enter_context(nc.semaphore(name))
        return sems[name]

    slab_in = [sem(f"slab_in{n}") for n in range(RING)]
    hi_made, lo_made = sem("hi_made"), sem("lo_made")
    half_used = sem("half_used")
    free0, free1 = sem("free0"), sem("free1")
    ada_left = sem("ada_left")
    ada_come = [sem(f"ada_come{n}") for n in range(2)]
    block = ctx.enter_context(nc.Block())

    @block.sync
    def _(sp):
        def slab(it, phase, per, s, src):
            if not (phase == "A" and s < RING and isinstance(it, int)):
                sp.wait_ge(lo_made, H0[phase] + it * per + 2 * (s - RING) + 2)
            sp.dma_start(raw[:, s % RING, :].rearrange("p (k n) -> p k n", k=4), src).then_inc(slab_in[s % RING], 16)

        def ada_chunk(n, piece, j):
            if not (isinstance(n, int) and n < 2):
                sp.wait_ge(ada_left, n - 1)
            kt, half = (j // 2, j % 2) if isinstance(j, int) else j
            sp.dma_start(ada_in[:, half, :], w_ada[ds(kt * P, P), piece * D + half * (D // 2):piece * D + (half + 1) * (D // 2)]
                         ).then_inc(ada_come[half], 16)

        sp.dma_start(con[:], A["k_con"]).then_inc(sem("par_in"), 16)
        small_loads = [
            (0, 0, rows(A["c"][0])), (0, 16, rows(A["g_mix"][0])), (0, 32, rows(A["g_ffn"][0])),
            (0, 48, rows(A["norm_g_2"][0, 0])), (0, 64, rows(A["norm_g_2"][0, 1])),
            (0, 80, rows(A["b_ada"][0, 0:2 * D])),
            (1, 0, rows(A["b_ada"][0, 3 * D:5 * D])), (1, 32, rows(A["conv_b"][0])), (1, 76, rows(A["conv_w"][0, 0])),
            (2, 0, rows(A["conv_w"][0, 1])), (2, 44, rows(A["conv_w"][0, 2])), (2, 88, rows(A["gla_b_a_2"][0])),
        ]
        for n, r, src in small_loads:
            sp.dma_start(parr[r:r + src.shape[0], n, :], src).then_inc(sem("par_in"), 16)
        sp.dma_start(X[:], tokens(A["x"][0])).then_inc(sem("x_in"), 16)
        for kt in range(4):
            sp.dma_start(ada0[:, kt, :], w_ada[kt * P:(kt + 1) * P, 0:2 * D]).then_inc(sem(f"ada0_in{kt}"), 16)
        with sp.Fori(1, KT // 4) as it:
            for u in range(4):
                sp.wait_ge(sem("ada0_sum"), 4 * it + u - 2)
                sp.dma_start(ada0[:, u, :], w_ada[ds((4 * it + u) * P, P), 0:2 * D]).then_inc(sem(f"ada0_in{u}"), 16)
        sp.dma_start(ixw_raw[:].rearrange("p (k n) -> p k n", k=KT), w_in[:, :, C_IX:C_IX + NIXW]).then_inc(sem("ixw_in"), 16)
        sp.dma_start(onehot[:], A["k_onehot"]).then_inc(sem("rel_in"), 16)
        sp.dma_start(relb[:], A["rel_bias"]).then_inc(sem("rel_in"), 16)

        def a_body(it):
            for s in range(8):
                slab(it, "A", 16, s, w_in[:, 4 * (s % 4):4 * (s % 4) + 4, ds(it * 2 * NB + s // 4 * NB, NB)])
                ada_chunk(8 * it + s + 8, 4, ((8 * it + s + 8) // 2 if isinstance(it, int) else 4 * it + s // 2 + 4, s % 2))
        for s in range(RING):
            slab(0, "A", 16, s, w_in[:, 4 * s:4 * s + 4, 0:NB])
        for j in range(8):
            ada_chunk(j, 4, j)
        for s in range(8):
            if s >= RING:
                slab(0, "A", 16, s, w_in[:, 4 * (s % 4):4 * (s % 4) + 4, NB:2 * NB])
            ada_chunk(8 + s, 4, 8 + s)
        with sp.Fori(1, 3) as it:
            a_body(it)
        sp.wait_ge(sem("erow_held"), 1)
        sp.dma_start(e_dram, erow[:]).then_inc(sem("e_out"), 16)
        sp.wait_ge(sem("e_out"), 16)
        sp.wait_ge(sem("tt_T"), KT // 2)
        for h in range(NH):
            src = e_dram[h:h + 1, 0:P]
            sp.dma_start(hank1[:, h, :], bass.AP(tensor=src.tensor, offset=src.offset, ap=[[1, P], [1, S]])).then_inc(sem("hank_in"), 16)
            src = e_dram[h:h + 1, P:2 * P]
            sp.dma_start(hank0[:, h, :], bass.AP(tensor=src.tensor, offset=src.offset, ap=[[1, P], [1, P]])).then_inc(sem("hank_in"), 16)

        def cols_body(it, phase, col0, chunk0, piece):
            for s in range(8):
                slab(it, phase, 16, s, w_in[:, 4 * (s % 4):4 * (s % 4) + 4, ds(it * 2 * NB + (col0 + s // 4 * NB), NB)])
                if piece is not None:
                    ada_chunk(chunk0 + 8 * it + s, piece[0], (piece[1] + 4 * it + s // 2, s % 2))
        with sp.Fori(0, 4) as it:
            cols_body(it, "B", 6 * NB, 32, (3, 0))
        with sp.Fori(0, 2) as it:
            cols_body(it, "C1", C_GATE, 64, (2, 0))
        with sp.Fori(0, 2) as it:
            cols_body(it, "C2", C_GATE + D, 80, (2, 8))

        with sp.Fori(0, 2) as it:
            for s in range(8):
                slab(it, "O", 16, s, w_o[s % 4 // 2][:, 4 * (s % 2):4 * (s % 2) + 4, ds(it * 2 * NB + s // 4 * NB, NB)])
        sp.wait_ge(half_used, H0["O"])
        sp.dma_start(X[:], tokens(A["x"][0])).then_inc(sem("x_in"), 16)
        for it in range(2):
            for s in range(8):
                slab(it, "U", 16, s, w_out[:, 4 * (s % 4):4 * (s % 4) + 4, (2 * it + s // 4) * NB:(2 * it + s // 4 + 1) * NB])
                if 8 * it + s >= 4:
                    ada_chunk(96 + 8 * it + s - 4, 5, 8 * it + s - 4)
                if (it, s) == (0, 3):
                    sp.wait_ge(sem("merge_done"), 2)
                    sp.dma_start(gt_bias[:], A["b_ada"][0:1, 2 * D:3 * D].to_broadcast([P, D])).then_inc(sem("gtb_in"), 16)

        def ffn(n):
            w_g, g0, w_u, u0, w_d = w_ffn[n]
            name = f"F{n + 1}"

            def gate_up(it, phase, per, first, j, w, c0):
                for s in range(4):
                    slab(it, phase, per, first + s, w[:, 4 * s:4 * s + 4, ds(j * NB + c0, NB)])

            def down(it, phase, per, first, j):
                for s in range(4):
                    slab(it, phase, per, first + s, w_d[:, ds(4 * j, 4), s * NB:(s + 1) * NB])

            gate_up(0, name + "p", 16, 0, 0, w_g, g0)
            gate_up(0, name + "p", 16, 4, 0, w_u, u0)
            if n == 0:
                sp.wait_ge(sem("gt_used"), 2)
                sp.dma_start(gt_bias[:], A["b_ada"][0:1, 5 * D:6 * D].to_broadcast([P, D])).then_inc(sem("gtb_in"), 16)
                sp.dma_start(gfin[:], A["g_final"].rearrange("(a n) -> a n", a=1).to_broadcast([P, D])).then_inc(sem("late_in"), 16)
                sp.dma_start(gn[:], A["gla_g_norm_2"][0:1, :].to_broadcast([P, GV])).then_inc(sem("late_in"), 16)
                sp.dma_start(alr_raw[:].rearrange("p (k n) -> p k n", k=KT), w_gla[:, :, 2 * D + 2 * GH * GK:]).then_inc(sem("late_in"), 16)
            with sp.Fori(0, FB - 1) as it:
                gate_up(it, name, 24, 0, it + 1, w_g, g0)
                if n == 0:
                    for half in range(2):
                        ada_chunk(108 + 2 * it + half, 5, (6 + it, half))
                down(it, name, 24, 4, it)
                gate_up(it, name, 24, 8, it + 1, w_u, u0)
            down(0, name + "e", 8, 0, FB - 1)

        ffn(0)

        def gla_body(it, phase, col0, w=w_gla):
            for s in range(8):
                slab(it, phase, 16, s, w[:, 4 * (s % 4):4 * (s % 4) + 4, ds(it * 2 * NB + (col0 + s // 4 * NB), NB)])
        for phase, col0 in (("GQ", 0), ("GV", D), ("GR", 2 * D)):
            with sp.Fori(0, 2) as it:
                gla_body(it, phase, col0)
        with sp.Fori(0, 2) as it:
            gla_body(it, "GO", 0, w_gla_out)
        ffn(1)
        sp.wait_ge(sem("y_done"), 2)
        sp.dma_start(tokens(out[0]), X[:]).then_inc(sem("out_done"), 16)
        sp.wait_ge(sem("out_done"), 16)

    @block.tensor
    def _(pe):
        pairs = [0]

        def half(it, phase, per, idx, gi, kt, first, last, x_hi=hi, x_lo=lo, halves_before=0):
            pe.wait_ge(lo_made, H0[phase] + it * per + idx + 1)
            for q in range(2):
                w = slice(idx % RING * HALF + q * NB, idx % RING * HALF + (q + 1) * NB)
                for tb in range(TB):
                    o, t = lin[gi % 2][tb][:], slice(tb * P, (tb + 1) * P)
                    pe.matmul(o, x_hi[:, kt + q, t], whi[:, w], start=first and q == 0, stop=False)
                    pe.matmul(o, x_hi[:, kt + q, t], wlo[:, w], start=False, stop=False)
                    m = pe.matmul(o, x_lo[:, kt + q, t], whi[:, w], start=False, stop=last and q == 1)
            m.then_inc(half_used, 1)

        def group(it, phase, per, gper, idx0, gi, n, hooks, kt0=0, x_hi=hi, x_lo=lo):
            pe.wait_ge(free0, G0[phase] + it * gper + gi + 1)
            pe.wait_ge(free1, G0[phase] + it * gper + gi + 1)
            for i in range(n):
                half(it, phase, per, idx0 + i, gi, kt0 + 2 * i, i == 0, i == n - 1, x_hi, x_lo)
                hooks(idx0 + i)

        def to_features(src):
            for g in range(KT // 2):
                n = pairs[0]
                if n >= 4:
                    pe.wait_ge(sem("tt_free"), n - 3)
                for q in range(2):
                    for tb in range(TB):
                        m = pe.transpose(aux[n % 4][:, q * S + tb * P:q * S + (tb + 1) * P],
                                         src[:, tb, (2 * g + q) * P:(2 * g + q + 1) * P], ident)
                m.then_inc(sem("tt_T"), 1)
                pairs[0] += 1

        def ada_columns(n):
            pe.wait_ge(sem("ada_sum"), 32 * (n + 1))
            for j in range(KT):
                m = pe.matmul(aux[3][:, j:j + 1], ada_acc[:, j * P:(j + 1) * P], ones[:, 0:1], start=True, stop=True)
            m.then_inc(sem("ada_T"), 1)

        def ada_rows(n):
            pe.wait_ge(sem("ada_sum"), 32 * (n + 1))
            for j in range(4):
                m = pe.matmul(aux[j][:], ones, ada_acc[:, j * NB:(j + 1) * NB], start=True, stop=True)
            m.then_inc(sem("ada_T"), 1)

        none = lambda idx: None

        pe.wait_ge(sem("par_in"), 13 * 16)
        for n, rws in enumerate((112, 120, 96)):
            m = pe.transpose(aux[n][:, 0:rws], parr[0:rws, n, :], ident[0:rws, 0:rws])
        m.then_inc(sem("par_T"), 1)
        pe.wait_ge(sem("rel_in"), 32)
        pe.matmul(aux[3][0:NH, :], relb[:], onehot[:], start=True, stop=True).then_inc(sem("erow_T"), 1)
        pe.wait_ge(sem("par_cols"), 1)
        pe.wait_ge(sem("ada0_sum"), KT)
        for j in range(2 * KT):
            m = pe.matmul(aux[0][:, j:j + 1], acc0[:, j * P:(j + 1) * P], ones[:, 0:1], start=True, stop=True)
        m.then_inc(sem("ada0_T"), 1)
        pe.wait_ge(sem("gs_made"), 1)
        pe.wait_ge(sem("erow_held"), 1)
        pe.wait_ge(sem("xs_made"), 2)
        to_features(X)
        pe.wait_ge(sem("tt_lo"), KT // 2)
        pe.wait_ge(sem("ixw_split"), 1)
        for tb in range(TB):
            t = slice(tb * P, (tb + 1) * P)
            for kt in range(KT):
                o, w = lin[0][tb][:, 0:NIXW], slice(kt * NIXW, (kt + 1) * NIXW)
                pe.matmul(o, hi[:, kt, t], whi[:, w], start=kt == 0, stop=False)
                pe.matmul(o, hi[:, kt, t], wlo[:, w], start=False, stop=False)
                m = pe.matmul(o, lo[:, kt, t], whi[:, w], start=False, stop=kt == KT - 1)
        m.then_inc(sem("ixw_done"), 1)

        with pe.Fori(0, 3) as it:
            for k in range(2):
                group(it, "A", 16, 2, 8 * k, k, 8, none)
        pe.wait_ge(sem("kdup_made"), 1)
        for tb in range(TB):
            m = pe.transpose(aux[0][:, tb * P:(tb + 1) * P], kdup[:, tb, :], ident)
        m.then_inc(sem("kix_T"), 1)
        ada_columns(0)

        def sb_turn(h, u):
            pe.wait_ge(sem("sb_staged"), h + 1)
            for w in range(2):
                for tb in range(TB):
                    m = pe.transpose(aux[0][:, w * S + tb * P:w * S + (tb + 1) * P], st_sb[:, u, w, tb, :], ident)
            m.then_inc(sem("sb_T"), 1)

        def sb_scores(h, u):
            pe.wait_ge(sem("sb_qk"), h + 1)
            pe.matmul(aux[1][:, 0:S], qk_sb[:, S:S + P], qk_sb[:, 0:S], start=True, stop=True)
            pe.matmul(aux[1][:, S:S + P], qk_sb[:, S + P:2 * S], qk_sb[:, P:S], start=True, stop=True).then_inc(sem("sb_z"), 1)

        def sb_suffix(h, u):
            pe.wait_ge(sem("sb_lk"), h + 1)
            pe.matmul(aux[2][:, 0:S], later, lk[:, 0:S], start=True, stop=False)
            pe.matmul(aux[2][:, P:S], ones, lk[:, S:S + P], start=False, stop=True)
            pe.matmul(aux[2][:, S:S + P], later, lk[:, S:S + P], start=True, stop=True).then_inc(sem("sb_suf"), 1)

        def sb_values(h, u):
            pe.wait_ge(sem("sb_a"), h + 1)
            pe.wait_ge(sem("sb_out"), h)
            pe.matmul(aux[3][:, 0:S], st_sb[:, u, 2, 0, :], lb[:, 0:S], start=True, stop=False)
            pe.matmul(aux[3][:, P:S], st_sb[:, u, 2, 1, :], lb[:, S:S + P], start=False, stop=True).then_inc(sem("sb_o"), 1)

        def sb_hooks(it):
            def run(idx):
                for off, step in ((0, sb_turn), (2, sb_scores), (5, sb_suffix), (7, sb_values)):
                    if idx % 8 == off:
                        step(2 * it + idx // 8, idx // 8)
            return run
        pe.wait_ge(sem("kix_made"), 1)
        pe.wait_ge(sem("mod_made"), 1)
        def b_body(it):
            for k in range(2):
                group(it, "B", 16, 2, 8 * k, k, 8, sb_hooks(it))
        with pe.Fori(0, 3) as it:
            b_body(it)
        b_body(3)
        pe.wait_ge(sem("sb_out"), NH)
        ada_columns(1)

        def ix_turn(p, u):
            pe.wait_ge(sem("ix_staged"), p + 1)
            for tb in range(TB):
                m = pe.transpose(aux[0][:, tb * P:(tb + 1) * P], st_ix[:, u % 2, tb, :], ident)
            m.then_inc(sem("ix_T"), 1)

        def ix_scores(p, u):
            pe.wait_ge(sem("ix_q"), p + 1)
            pe.wait_ge(sem("ix_relu"), 2 * p)
            for e in range(2):
                r = slice(e * DIX, (e + 1) * DIX)
                pe.matmul(aux[1 + e][:, 0:P], q_ixT[r, 0:P], k_ixT[r, 0:P], start=True, stop=True)
                m = pe.matmul(aux[1 + e][:, P:3 * P], q_ixT[r, P:S], k_ixT[r, :], start=True, stop=True)
            m.then_inc(sem("ix_z"), 1)

        def ix_hooks(it):
            def run(idx):
                if idx % 4 == 0:
                    ix_turn(4 * it + idx // 4, idx // 4)
                if idx % 4 == 2:
                    ix_scores(4 * it + idx // 4, idx // 4)
            return run
        pe.wait_ge(sem("mod_made"), 2)
        with pe.Fori(0, 2) as it:
            for k in range(2):
                group(it, "C1", 16, 2, 8 * k, k, 8, ix_hooks(it))

        def ds_turn(h, u):
            pe.wait_ge(sem("ds_qk_staged"), h + 1)
            for w in range(2):
                for tb in range(TB):
                    m = pe.transpose(aux[0][:, w * S + tb * P:w * S + (tb + 1) * P], st_qk[:, u % 2, w, tb, :], ident)
            m.then_inc(sem("ds_T"), 1)

        def ds_logits(h, u):
            pe.wait_ge(sem("ds_k"), h + 1)
            pe.wait_ge(sem("ds_lg"), h)
            pe.matmul(aux[1][:, 0:P], qk_ds[:, 0:P], qk_ds[:, S:S + P], start=True, stop=False)
            pe.matmul(aux[1][:, 0:P], flip, hank0[:, ds(h, 1), :].rearrange("p a s -> p (a s)"), start=False, stop=True)
            pe.matmul(aux[1][:, P:3 * P], qk_ds[:, P:S], qk_ds[:, S:2 * S], start=True, stop=False)
            pe.matmul(aux[1][:, P:3 * P], flip, hank1[:, ds(h, 1), :].rearrange("p a s -> p (a s)"), start=False, stop=True).then_inc(sem("ds_L"), 1)

        def ds_probs(h, u):
            pe.wait_ge(sem("ds_p"), h + 1)
            for j in range(3):
                m = pe.transpose(aux[2][:, j * P:(j + 1) * P], lg[:, u % 2, j * P:(j + 1) * P], ident)
            m.then_inc(sem("ds_PT"), 1)

        def ds_values(h, u):
            pe.wait_ge(sem("ds_pt"), h + 1)
            pe.wait_ge(sem("ds_v_staged"), h + 1)
            pe.wait_ge(sem("ds_out"), h)
            pe.matmul(aux[3][:, 0:S], st_v[:, u % 2, 0, :], PT[:, 0:S], start=True, stop=False)
            pe.matmul(aux[3][:, P:S], st_v[:, u % 2, 1, :], PT[:, S:3 * P], start=False, stop=True).then_inc(sem("ds_o"), 1)

        def ds_hooks(it):
            def run(idx):
                for step, offs in ((ds_values, DS_O), (ds_probs, DS_P), (ds_logits, DS_L), (ds_turn, DS_T)):
                    if idx in offs:
                        u = offs.index(idx)
                        step(4 * it + u, u)
            return run
        pe.wait_ge(sem("ix_relu"), 2 * NIX // 2)
        pe.wait_ge(sem("hank_in"), 2 * NH * 16)
        with pe.Fori(0, 2) as it:
            for k in range(2):
                group(it, "C2", 16, 2, 8 * k, k, 8, ds_hooks(it))

        pe.wait_ge(sem("oT_split"), 4)
        with pe.Fori(0, 2) as it:
            for gi in range(4):
                group(it, "O", 16, 4, 4 * gi, gi, 4, none, kt0=8 * (gi % 2))
        pe.wait_ge(sem("ds_out"), NH)
        ada_rows(2)
        pe.wait_ge(sem("gt_made"), 1)
        pe.wait_ge(sem("merge_done"), 2)
        to_features(merged)
        pe.wait_ge(sem("tt_lo"), 2 * KT // 2)
        with pe.Fori(0, 2) as it:
            for k in range(2):
                group(it, "U", 16, 2, 8 * k, k, 8, none)

        def ffn(n):
            name = f"F{n + 1}"
            base = n * FB

            def turn_up(j):
                g = G0[name + "p"] + 6 * j + 4
                pe.wait_ge(free0 if n == 0 else sem("up_mul"), g if n == 0 else j + 1)
                pe.wait_ge(free1, g)
                pe.wait_ge(sem("hid_made"), base + j)
                src = ubuf
                for f in range(4):
                    for tb in range(TB):
                        m = pe.transpose(aux[f // 2][:, f % 2 * S + tb * P:f % 2 * S + (tb + 1) * P],
                                         src[:, tb, f * P:(f + 1) * P], ident)
                m.then_inc(sem("up_T"), 1)

            def turn_gate(j):
                g = G0[name + "p"] + (3 if isinstance(j, int) else 6 * j - 1)
                pe.wait_ge(free0, g)
                pe.wait_ge(free1, g)
                pe.wait_ge(sem("gpad_made"), j)
                for f in range(4):
                    for tb in range(TB):
                        m = pe.transpose(aux[2 + f // 2][:, f % 2 * S + tb * P:f % 2 * S + (tb + 1) * P],
                                         gbuf[:, tb, f * P:(f + 1) * P], ident)
                m.then_inc(sem("gate_T"), 1)

            def hooks(j, at_gate, at_up):
                def run(idx):
                    if idx == at_up:
                        turn_up(j - 1)
                    if idx == at_gate and n == 0:
                        turn_gate(j)
                return run

            def down(it, phase, per, gper, idx0, gi, j, run):
                pe.wait_ge(sem("hid_made"), base + j + 1)
                for c in range(4):
                    group(it, phase, per, gper, idx0 + 2 * c, gi + c, 2, run, 0, hid_hi, hid_lo)

            run = hooks(0, 9, -1)
            group(0, name + "p", 16, 2, 0, 0, 8, run)
            group(0, name + "p", 16, 2, 8, 1, 8, run)
            with pe.Fori(0, FB - 1) as it:
                run = hooks(it + 1, 9, 1)
                group(it, name, 24, 6, 0, 0, 8, run)
                down(it, name, 24, 6, 8, 1, it, run)
                group(it, name, 24, 6, 16, 5, 8, run)
            turn_up(FB - 1)
            down(0, name + "e", 8, 4, 0, 0, FB - 1, none)

        pe.wait_ge(sem("xs_made"), 4)
        to_features(xs)
        pe.wait_ge(sem("tt_lo"), 3 * KT // 2)
        ffn(0)
        pe.wait_ge(sem("hid_made"), FB)
        ada_rows(3)
        pe.wait_ge(sem("gt_made"), 2)

        pe.wait_ge(sem("xs_made"), 6)
        to_features(xs)
        pe.wait_ge(sem("tt_lo"), 4 * KT // 2)
        pe.wait_ge(sem("alr_split"), 1)
        for tb in range(TB):
            t = slice(tb * P, (tb + 1) * P)
            for kt in range(KT):
                o, w = aux[tb][:, 0:GR], slice(kt * GR, (kt + 1) * GR)
                pe.matmul(o, hi[:, kt, t], alr_hi[:, w], start=kt == 0, stop=False)
                pe.matmul(o, hi[:, kt, t], alr_lo[:, w], start=False, stop=False)
                m = pe.matmul(o, lo[:, kt, t], alr_hi[:, w], start=False, stop=kt == KT - 1)
        m.then_inc(sem("alr_done"), 1)

        def gq_hooks(it):
            def run(idx):
                if idx in (5, 13):
                    turn_block(2 * it + idx // 8 - 1)
            return run

        def turn_block(b):
            pe.wait_ge(free0, G0["GQ"] + b + 3)
            pe.wait_ge(free1, G0["GQ"] + b + 3)
            pe.wait_ge(sem("gq_turned"), b)
            for f in range(4):
                for tb in range(TB):
                    m = pe.transpose(aux[2 + f // 2][:, f % 2 * S + tb * P:f % 2 * S + (tb + 1) * P],
                                     gstage[:, tb, f * P:(f + 1) * P], ident)
            m.then_inc(sem("gq_T"), 1)

        for k in range(2):
            group(0, "GQ", 16, 2, 8 * k, k, 8, lambda idx: turn_block(0) if idx == 13 else None)
        pe.wait_ge(sem("alr_held"), 2)
        for tb in range(TB):
            m = pe.transpose(aux[0][0:GR, tb * P:(tb + 1) * P], alr[:, tb, :], ident)
        m.then_inc(sem("alr_T"), 1)
        for k in range(2):
            group(1, "GQ", 16, 2, 8 * k, k, 8, gq_hooks(1))
        pe.wait_ge(sem("alrT_made"), 1)
        pe.wait_ge(sem("gla_in"), 32)
        for f in range(8):
            if f >= 2:
                pe.wait_ge(sem("gu_made"), f - 1)
            pe.matmul(aux[f % 2][:, 0:S], wa2[:, f * P:(f + 1) * P], alrT[:], start=True, stop=True).then_inc(sem("gu_T"), 1)
        for k in range(2):
            group(0, "GV", 16, 2, 8 * k, k, 8, lambda idx: turn_block(3) if idx == 5 else None)
        group(1, "GV", 16, 2, 0, 0, 8, none)
        group(1, "GV", 16, 2, 8, 1, 8, none)
        with pe.Fori(0, 2) as it:
            for k in range(2):
                group(it, "GR", 16, 2, 8 * k, k, 8, none)

        pe.wait_ge(sem("gb_made"), 1)
        pe.wait_ge(sem("gq_turned"), 4)
        pe.wait_ge(free0, 2 + G0["GO"])
        pe.wait_ge(free1, 2 + G0["GO"])

        def level(h, lv):
            n = 7 * h + lv
            if lv:
                pe.wait_ge(sem("gl_m"), 7 * h + GL_ITEMS.index(lv) + 1)
            if n >= 2:
                pe.wait_ge(sem("gl_picked"), n - 1)
            j = (6 * h + lv - 1) % 3
            l, r = (gla_k(h), gla_q(h)) if lv == 0 else (gm[:, j, :], gm[:, j, :])
            for tb in range(TB):
                for e in range(2):
                    c = slice(e * S + tb * P, e * S + (tb + 1) * P)
                    m = pe.matmul(aux[n % 2][:, tb * P:(tb + 1) * P], l[:, c], r[:, c], start=e == 0, stop=e == 1)
            m.then_inc(sem("gl_z"), 1)

        def turn_keys(h):
            pe.wait_ge(sem("gk_dec"), h + 1)
            if h:
                pe.wait_ge(sem("go_held"), 2 * h)
            for tb in range(TB):
                for e in range(2):
                    m = pe.transpose(aux[2][:, (2 * tb + e) * P:(2 * tb + e + 1) * P], gkd[:, h % 2, e * S + tb * P:e * S + (tb + 1) * P], ident)
            m.then_inc(sem("gk_T"), 1)

        def state(h, n):
            c, e, i = n // 2, n % 2, 6 * h + n
            pe.wait_ge(sem("gk_turned"), h + 1)
            if i >= 4:
                pe.wait_ge(sem("gs_added"), i - 3)
            r = slice(c % 2 * GC, (c % 2 + 1) * GC)
            pe.matmul(lin[i % 4 // 2][i % 2][:], gkdT[r, c // 2, e * P:(e + 1) * P], gla_v(h, c // 2)[r, :], start=True, stop=True).then_inc(sem("gs_T"), 1)

        def values(h, tb):
            pe.wait_ge(sem("gl_picked"), 7 * h + 7)
            pe.wait_ge(sem("gq_made"), h + 1)
            pe.wait_ge(sem("gs_added"), 6 * h + (2 if tb == 0 else 6))
            if tb == 0 and h:
                pe.wait_ge(sem("go_held"), 2 * h - 1)
            o = aux[3 - tb][:]
            pe.matmul(o, gsc[:, h % 2, tb * P:(tb + 1) * P], gla_v(h, tb), start=True, stop=False)
            cs = (0,) if tb == 0 else (1, 2)
            for c in cs:
                for e in range(2):
                    m = pe.matmul(o, gq[:, h % 2, c, e, :], sts[:, c, e, :], start=False, stop=c == cs[-1] and e == 1)
            m.then_inc(sem("go_T"), 1)

        for h in range(GH + 1):
            for lv in range(7):
                if h < GH:
                    level(h, lv)
                if h:
                    for step, n in {0: [(turn_keys, None)], 1: [(state, 0), (state, 1)], 2: [(state, 2), (state, 3)],
                                    3: [(state, 4), (state, 5)], 4: [(values, 0)], 5: [(values, 1)]}.get(lv, ()):
                        step(h - 1) if n is None else step(h - 1, n)
        pe.wait_ge(sem("go_done"), 2)
        to_features(gv)
        pe.wait_ge(sem("tt_lo"), 5 * KT // 2)
        with pe.Fori(0, 2) as it:
            for k in range(2):
                group(it, "GO", 16, 2, 8 * k, k, 8, none)
        pe.wait_ge(sem("xs_made"), 8)
        to_features(xs)
        pe.wait_ge(sem("tt_lo"), 6 * KT // 2)
        ffn(1)

    @block.scalar
    def _(act):
        pairs, affine = [0], [0]

        def split(it, phase, per, idx):
            act.wait_ge(slab_in[idx // 2 % RING], 2 * (H0[phase] + it * per) + 16 * (idx // 8 + 1))
            if not (phase == "A" and idx < RING):
                act.wait_ge(half_used, H0[phase] + it * per + idx - RING + 1)
            act.activation(whi[:, idx % RING * HALF:(idx % RING + 1) * HALF],
                           raw[:, idx // 2 % RING, idx % 2 * HALF:(idx % 2 + 1) * HALF], ACT.Copy).then_inc(hi_made, 1)

        def body(it, phase, per, hooks, upto=None):
            for idx in range(RING, per + RING if upto is None else upto):
                split(it, phase, per, idx)
                for step in hooks.get(idx, ()):
                    step()

        def drain(it, phase, gper, gi, upto, dst, **how):
            per = dict((p[0], p[2]) for p in PHASES)[phase]
            act.wait_ge(half_used, H0[phase] + it * per + upto)
            act.activation(dst, lin[gi % 2][0][:], ACT.Copy, **how).then_inc(free0, 1)

        def norm_stats(n):
            for tb in range(TB):
                if tb:
                    act.wait_ge(sem("ss_made"), 2 * n + 1)
                act.activation(junk[:], X[:, tb, :], ACT.Square, accum_out=ss[:, tb:tb + 1]).then_inc(sem("ss_made"), 1)
            act.wait_ge(sem("ms_made"), n + 1)
            act.activation(rstd, ss, ACT.Sqrt).then_inc(sem("sd_made"), 1)

        def norm_rows(n, dst):
            act.wait_ge(sem("rstd_made"), n + 1)
            act.activation(dst[:, 0, :], X[:, 0, :], ACT.Copy, scale=rstd[:, 0:1]).then_inc(sem("xs_made"), 1)

        def features(plain):
            for g in range(KT // 2):
                n = pairs[0]
                if plain:
                    act.wait_ge(sem("tt_T"), n + 1)
                    src = aux[n % 4][:]
                else:
                    act.wait_ge(sem("tt_aff"), affine[0] + 1)
                    src = aff[:, n % 2, :]
                    affine[0] += 1
                act.activation(hi[:, 2 * g:2 * g + 2, :].rearrange("p k t -> p (k t)"), src, ACT.Copy).then_inc(sem("tt_hi"), 1)
                pairs[0] += 1

        act.wait_ge(sem("par_cols"), 1)
        act.activation(csg, c_col, ACT.Sigmoid).then_inc(sem("csg_made"), 1)
        act.wait_ge(sem("x_in"), 16)
        norm_stats(0)
        norm_rows(0, X)
        features(False)
        act.wait_ge(sem("ixw_in"), 16)
        act.activation(whi[:, 0:KT * NIXW], ixw_raw[:], ACT.Copy).then_inc(sem("ixw_hi"), 1)
        act.wait_ge(sem("ixw_done"), 1)
        act.activation(ixw[:, 0, :], lin[0][0][:, 0:NIXW], ACT.Copy).then_inc(free0, 1)
        act.wait_ge(free0, 1)
        act.nop().then_inc(free0, 1)
        for idx in range(RING):
            split(0, "A", 16, idx)

        def drains2(it, phase, dst, extra=None):
            hooks = dict(extra or {})
            for k, idx in ((0, 11), (1, 19)):
                hooks[idx] = list(hooks.get(idx, [])) + [lambda k=k: drain(it, phase, 2, k, 8 * (k + 1), dst(k))]
            return hooks

        cols = lambda it, k: ds(it * 2 * NB + k * NB, NB)
        with act.Fori(0, 3) as it:
            body(it, "A", 16, drains2(it, "A", lambda k: sbz[:, 0, cols(it, k)]))
        act.wait_ge(sem("kix_T"), 1)
        act.activation(k_ixT[:], aux[0][:, 0:S], ACT.Copy).then_inc(sem("kix_made"), 1)

        def sb_act(it):
            def hold_qk(u):
                h = 2 * it + u
                act.wait_ge(sem("sb_T"), h + 1)
                act.activation(qk_sb[:], aux[0][:], ACT.Copy).then_inc(sem("sb_qk"), 1)

            def softplus(u):
                h = 2 * it + u
                act.wait_ge(sem("sb_az"), h + 1)
                act.activation(az[:], az[:], ACT.Exp, scale=HD ** -0.5).then_inc(sem("sb_e"), 1)
                act.wait_ge(sem("sb_e"), h + 1)
                act.activation(az[:], az[:], ACT.Ln, bias=1.0).then_inc(sem("sb_L"), 1)

            def weights(u):
                h = 2 * it + u
                act.wait_ge(sem("sb_sm"), h + 1)
                act.activation(lb[:], lb[:], ACT.Exp).then_inc(sem("sb_ex"), 1)

            def hold_out(u):
                h = 2 * it + u
                act.wait_ge(sem("sb_o"), h + 1)
                act.activation(oT_sb[:, ds(h, 1), :].rearrange("p a t -> p (a t)"), aux[3][:, 0:S], ACT.Copy).then_inc(sem("sb_out"), 1)
            hooks = {}
            for u in range(2):
                for off, step in ((4, hold_qk), (6, softplus), (9, weights), (11, hold_out)):
                    hooks.setdefault(8 * u + off, []).append(lambda u=u, step=step: step(u))
            return hooks

        with act.Fori(0, 3) as it:
            body(it, "B", 16, drains2(it, "B", lambda k: dsz[:, 0, cols(it, k)], sb_act(it)))
        body(3, "B", 16, drains2(3, "B", lambda k: qix[:, 0, k * NB:(k + 1) * NB], sb_act(3)))

        def ix_act(it):
            def hold_q(u):
                p = 4 * it + u
                act.wait_ge(sem("ix_T"), p + 1)
                act.activation(q_ixT[:], aux[0][:, 0:S], ACT.Copy).then_inc(sem("ix_q"), 1)

            def relu(u):
                p = 4 * it + u
                act.wait_ge(sem("ix_z"), p + 1)
                act.wait_ge(sem("ix_sum"), 2 * p)
                for e in range(2):
                    act.activation(r_ix[:, e, :], aux[1 + e][:, 0:3 * P], ACT.Relu, scale=DIX ** -0.5).then_inc(sem("ix_relu"), 1)
            hooks = {}
            for u in range(4):
                hooks.setdefault(4 * u + 4, []).append(lambda u=u: hold_q(u))
                hooks.setdefault(4 * u + 6, []).append(lambda u=u: relu(u))
            return hooks
        with act.Fori(0, 2) as it:
            body(it, "C1", 16, drains2(it, "C1", lambda k: gate_sb[:, 0, cols(it, k)], ix_act(it)))

        def ds_act(it):
            def hold_q(u):
                h = 4 * it + u
                act.wait_ge(sem("ds_T"), h + 1)
                act.activation(qk_ds[:, 0:S], aux[0][:, 0:S], ACT.Copy, scale=HD ** -0.5).then_inc(sem("ds_q"), 1)

            def soft(u):
                h = 4 * it + u
                act.wait_ge(sem("ds_mx"), h + 1)
                for tb, c in ((0, slice(0, P)), (1, slice(P, 3 * P))):
                    n = 2 * (u % 2) + tb
                    m = act.activation(lg[:, u % 2, c], lg[:, u % 2, c], ACT.Exp, bias=nmax[:, n:n + 1], accum_out=ssum[:, n:n + 1])
                    m.then_inc(sem("ds_ex"), 1)

            def hold_p(u):
                h = 4 * it + u
                act.wait_ge(sem("ds_PT"), h + 1)
                act.activation(PT[:], aux[2][:, 0:3 * P], ACT.Copy).then_inc(sem("ds_pt"), 1)

            def hold_out(u):
                h = 4 * it + u
                act.wait_ge(sem("ds_o"), h + 1)
                act.activation(oT_ds[:, ds(h, 1), :].rearrange("p a t -> p (a t)"), aux[3][:, 0:S], ACT.Copy).then_inc(sem("ds_out"), 1)
            hooks = {}
            for offs, step in ((DS_O, hold_out), (DS_P, hold_p), (DS_L, soft), (DS_T, hold_q)):
                for u in range(4):
                    hooks.setdefault(offs[u] + AHEAD, []).append(lambda u=u, step=step: step(u))
            return hooks
        act.wait_ge(sem("tk_in"), 1)
        with act.Fori(0, 2) as it:
            body(it, "C2", 16, drains2(it, "C2", lambda k: gate_ds[:, 0, cols(it, k)], ds_act(it)))

        act.wait_ge(half_used, H0["O"])
        act.wait_ge(sem("ds_out"), NH)
        for n in range(4):
            src = (oT_sb, oT_ds)[n // 2][:, n % 2 * 4:n % 2 * 4 + 4, :]
            act.activation(hi[:, 4 * n:4 * n + 4, :], src, ACT.Copy).then_inc(sem("oT_hi"), 1)

        def o_hooks(it):
            hooks = {}

            def gate(gi):
                g = (gate_sb, gate_ds)[gi % 2][:, :, cols(it, gi // 2)]
                act.activation(g, g, ACT.Sigmoid).then_inc(sem("og_sig"), 1)

            def take(gi):
                act.wait_ge(sem("stage_free"), 4 * it + gi + 1)
                drain(it, "O", 4, gi, 4 * (gi + 1), stage[:, gi % 2, :])
            for gi in range(4):
                hooks.setdefault(4 * gi + 5, []).append(lambda gi=gi: gate(gi))
                hooks.setdefault(4 * gi + 7, []).append(lambda gi=gi: take(gi))
            return hooks
        act.wait_ge(free0, G0["O"] + 2)
        act.wait_ge(free1, G0["O"] + 2)
        with act.Fori(0, 2) as it:
            body(it, "O", 16, o_hooks(it))
        act.wait_ge(half_used, H0["U"])
        features(True)
        with act.Fori(0, 2) as it:
            body(it, "U", 16, drains2(it, "U", lambda k: y1[:, 0, cols(it, k)]))

        def ffn(n):
            name = f"F{n + 1}"
            base = n * FB

            def hid_high(j):
                if n == 0:
                    act.wait_ge(sem("hidf_made"), j + 1)
                    act.activation(hid_hi[:], hidf[:], ACT.Copy).then_inc(sem("hid_h"), 1)
                else:
                    act.wait_ge(sem("up_T"), base + j + 1)
                    for e in range(2):
                        act.activation(hid_hi[:, 2 * e:2 * e + 2, :].rearrange("p k t -> p (k t)"), aux[e][:], ACT.Copy).then_inc(sem("hid_h"), 1)

            def gate_pad(j):
                act.wait_ge(sem("gate_T"), j + 1)
                for e in range(2):
                    m = act.activation(gpad[:, 2 * e:2 * e + 2, 2:], aux[2 + e][:].rearrange("p (k t) -> p k t", k=2), ACT.Copy)
                m.then_inc(sem("gpad_made"), 1)

            def sigmoid(j):
                if n == 0:
                    act.wait_ge(sem("conv_made"), 6 * j + 6)
                    act.activation(csig[:], cacc[:], ACT.Sigmoid).then_inc(sem("csig_made"), 1)
                else:
                    g = G0[name + "p"] + (3 if isinstance(j, int) else 6 * j - 1)
                    act.wait_ge(free0, g)
                    act.wait_ge(free1, g)
                    act.activation(csig[:].rearrange("p a t -> p (a t)"), gbuf[:].rearrange("p a t -> p (a t)"), ACT.Sigmoid).then_inc(sem("csig_made"), 1)

            def down(it, phase, gper, gi, c, upto):
                k = (0 if phase == name else 4 * (FB - 1)) + (4 * it + c)
                act.wait_ge(sem("dstage_free"), n * 4 * FB + k + 1)
                drain(it, phase, gper, gi, upto, dstage[:, c % 2, :])

            def hooks(it, phase, gper, j, ups):
                hk = {}
                add = lambda idx, f: hk.setdefault(idx, []).append(f)
                add(11, lambda: drain(it, phase, gper, 0, 8, gbuf[:, 0, :]))
                if n == 0:
                    add(13, lambda: gate_pad(j))
                add(18 if n == 0 else 12, lambda: sigmoid(j))
                if phase == name:
                    add(5, lambda: hid_high(it))
                    for c in range(4):
                        add(13 + 2 * c, lambda c=c: down(it, phase, gper, 1 + c, c, 10 + 2 * c))
                up = 1 if phase != name else 5
                add(ups, lambda: drain(it, phase, gper, up, ups - AHEAD + 1, ubuf[:, 0, :]))
                return hk
            body(0, name + "p", 16, hooks(0, name + "p", 2, 0, 19))
            with act.Fori(0, FB - 1) as it:
                body(it, name, 24, hooks(it, name, 6, it + 1, 27))
            hid_high(FB - 1)
            hk = {5 + 2 * c: [lambda c=c: down(0, name + "e", 4, c, c, 2 * c + 2)] for c in range(4)}
            if n == 0:
                body(0, name + "e", 8, hk)
            else:
                for idx in range(4, 8):
                    split(0, name + "e", 8, idx)
                    for step in hk.get(idx, ()):
                        step()
                for idx in (9, 11):
                    hk[idx][0]()

        act.wait_ge(sem("xcomb"), 2)
        norm_stats(1)
        norm_rows(1, xs)
        features(False)
        ffn(0)

        act.wait_ge(sem("xcomb"), 4)
        norm_stats(2)
        act.wait_ge(sem("xfin"), 2)
        act.dma_start(wa2[:], A["gla_w_a2_2"][0]).then_inc(sem("gla_in"), 16)
        act.dma_start(gmask[:], A["k_levels"]).then_inc(sem("gla_in"), 16)
        norm_stats(3)
        norm_rows(3, xs)
        act.wait_ge(sem("late_in"), 48)
        act.activation(alr_hi[:], alr_raw[:], ACT.Copy).then_inc(sem("alr_hi_made"), 1)
        features(False)
        act.wait_ge(sem("alr_done"), 1)
        act.activation(alr[:, 0, :], aux[0][:, 0:GR], ACT.Copy).then_inc(sem("alr_held"), 1)

        def turned(b):
            scale = GK ** -0.5 if b < 2 else 1.0
            act.wait_ge(sem("gq_T"), b + 1)
            for e in range(2):
                m = act.activation(gqk[:, 4 * b + 2 * e:4 * b + 2 * e + 2, :].rearrange("p k t -> p (k t)"), aux[2 + e][:], ACT.Copy, scale=scale)
            m.then_inc(sem("gq_turned"), 1)

        def gq_drain(b):
            if b:
                act.wait_ge(sem("gq_T"), b)
            drain(b // 2, "GQ", 2, b % 2, 8 * (b % 2 + 1), gstage[:, 0, :])
        body(0, "GQ", 16, {11: [lambda: gq_drain(0)], 17: [lambda: turned(0)], 19: [lambda: gq_drain(1)]})
        act.wait_ge(sem("alr_T"), 1)
        act.activation(alrT[:], aux[0][0:GR, 0:S], ACT.Copy).then_inc(sem("alrT_made"), 1)
        body(1, "GQ", 16, {9: [lambda: turned(1)], 11: [lambda: gq_drain(2)], 17: [lambda: turned(2)], 19: [lambda: gq_drain(3)]})
        gvd = lambda it: drains2(it, "GV", lambda k: gv[:, 0, cols(it, k)])
        hk = gvd(0)
        hk.setdefault(9, []).append(lambda: turned(3))
        body(0, "GV", 16, hk)
        act.wait_ge(sem("gabs"), 1)
        act.activation(gt1[:], gt1[:], ACT.Exp).then_inc(sem("gexp"), 1)
        act.wait_ge(sem("gexp"), 1)
        act.activation(gt1[:], gt1[:], ACT.Ln, bias=1.0).then_inc(sem("gln"), 1)
        body(1, "GV", 16, gvd(1))
        with act.Fori(0, 2) as it:
            body(it, "GR", 16, drains2(it, "GR", lambda k: gr[:, 0, cols(it, k)]))
        def decays(h, i):
            n = 7 * h + i
            act.wait_ge(sem("gl_d"), n + 1)
            act.activation(ge[:, n % 4, :], ge[:, n % 4, :], ACT.Exp).then_inc(sem("gl_e"), 1)
            if GL_ITEMS[i] == 0:
                if h >= 2:
                    act.wait_ge(sem("gs_added"), 6 * (h - 1))
                act.activation(geb[:, h % 2, :], gla_sums(h), ACT.Exp).then_inc(sem("geb_made"), 1)

        for h in range(GH + 1):
            for i in range(7):
                if h < GH:
                    decays(h, i)
                if i == 1 and h:
                    act.wait_ge(sem("gk_T"), h)
                    act.activation(gkdT[:].rearrange("p a t -> p (a t)"), aux[2][:], ACT.Copy).then_inc(sem("gk_turned"), 1)
            for tb in range(TB if h else 0):
                act.wait_ge(sem("go_T"), 2 * (h - 1) + tb + 1)
                act.activation(gla_v(h - 1, tb), aux[3 - tb][:], ACT.Copy).then_inc(sem("go_held"), 1)
        act.wait_ge(sem("go_held"), 2 * GH)
        for n in range(TB * GH):
            if n:
                act.wait_ge(sem("gss_made"), n)
            act.activation(gjunk[:], gv[:, n // GH, n % GH * GV:(n % GH + 1) * GV], ACT.Square, accum_out=gss[:, n:n + 1]).then_inc(sem("gss_made"), 1)
        act.wait_ge(sem("gms_made"), 1)
        act.activation(grs, gss[:], ACT.Sqrt).then_inc(sem("gsd_made"), 1)
        act.wait_ge(sem("gr_in"), 1)
        for tb in range(TB):
            act.activation(y1[:, tb, :], gr[:, tb, :], ACT.Sigmoid).then_inc(sem("gsig_made"), 1)
        act.wait_ge(half_used, H0["GO"])
        act.wait_ge(sem("go_done"), 2)
        features(True)
        with act.Fori(0, 2) as it:
            body(it, "GO", 16, drains2(it, "GO", lambda k: y1[:, 0, cols(it, k)]))
        act.wait_ge(sem("xcomb"), 6)
        norm_stats(4)
        norm_rows(4, xs)
        features(False)
        ffn(1)

    @block.vector
    def _(dve):
        pairs, affine, links = [0], [0], [0]

        def link(op):
            links[0] += 1
            op.then_inc(sem("dve_link"), 1)
            dve.wait_ge(sem("dve_link"), links[0])

        def split(it, phase, per, idx):
            dve.wait_ge(hi_made, H0[phase] + it * per + idx + 1)
            c = slice(idx % RING * HALF, (idx % RING + 1) * HALF)
            dve.tensor_tensor(wlo[:, c], raw[:, idx // 2 % RING, idx % 2 * HALF:(idx % 2 + 1) * HALF],
                              whi[:, c].bitcast(fp32), ALU.subtract).then_inc(lo_made, 1)

        def body(it, phase, per, hooks, upto=None):
            for idx in range(RING, per + RING if upto is None else upto):
                split(it, phase, per, idx)
                for step in hooks.get(idx, ()):
                    step()

        pers = dict((p[0], p[2]) for p in PHASES)

        def drained(it, phase, upto):
            dve.wait_ge(half_used, H0[phase] + it * pers[phase] + upto)

        def drain(it, phase, gi, upto, dst):
            drained(it, phase, upto)
            dve.tensor_copy(dst, lin[gi % 2][1][:]).then_inc(free1, 1)

        def norm_stats(n):
            dve.wait_ge(sem("ss_made"), 2 * (n + 1))
            dve.tensor_scalar(ss, ss, 1.0 / D, EPS, ALU.mult, ALU.add).then_inc(sem("ms_made"), 1)
            dve.wait_ge(sem("sd_made"), n + 1)
            dve.reciprocal(rstd, rstd).then_inc(sem("rstd_made"), 1)
            dve.wait_ge(sem("rstd_made"), n + 1)

        def norm_rows(dst):
            dve.tensor_scalar(dst[:, 1, :], X[:, 1, :], rstd[:, 1:2], None, ALU.mult).then_inc(sem("xs_made"), 1)

        def features(plain, scale=None, shift=None):
            def low(g, n):
                dve.wait_ge(sem("tt_hi"), n + 1)
                src = aux[n % 4][:] if plain else aff[:, n % 2, :]
                m = dve.tensor_tensor(lo[:, 2 * g:2 * g + 2, :].rearrange("p k t -> p (k t)"), src,
                                      hi[:, 2 * g:2 * g + 2, :].rearrange("p k t -> p (k t)").bitcast(fp32), ALU.subtract)
                m.then_inc(sem("tt_lo"), 1)
            for g in range(KT // 2):
                n = pairs[0]
                if plain:
                    low(g, n)
                    dve.wait_ge(sem("tt_lo"), n + 1)
                    dve.nop().then_inc(sem("tt_free"), 1)
                else:
                    dve.wait_ge(sem("tt_T"), n + 1)
                    if affine[0] >= 2:
                        dve.wait_ge(sem("tt_lo"), n - 1)
                    for q in range(2):
                        kt = 2 * g + q
                        m = dve.tensor_scalar(aff[:, n % 2, q * S:(q + 1) * S], aux[n % 4][:, q * S:(q + 1) * S], scale[:, kt:kt + 1],
                                              None if shift is None else shift[:, kt:kt + 1], ALU.mult,
                                              ALU.bypass if shift is None else ALU.add)
                    m.then_inc(sem("tt_aff"), 1)
                    affine[0] += 1
                    dve.wait_ge(sem("tt_aff"), affine[0])
                    dve.nop().then_inc(sem("tt_free"), 1)
                    if g:
                        low(g - 1, n - 1)
                pairs[0] += 1
            if not plain:
                low(KT // 2 - 1, pairs[0] - 1)

        link(dve.memset(acc0[:], 0.0))
        dve.wait_ge(sem("par_T"), 1)
        dve.tensor_copy(par2[:], aux[1][:, 0:120])
        dve.tensor_copy(par3[:], aux[2][:, 0:96])
        dve.tensor_copy(par1[:], aux[0][:, 0:112]).then_inc(sem("par_cols"), 1)
        dve.wait_ge(sem("par_cols"), 1)
        dve.wait_ge(sem("csg_made"), 1)
        dve.tensor_tensor(cact, c_col, csg, ALU.mult).then_inc(sem("cact_made"), 1)
        dve.wait_ge(sem("cact_made"), 1)
        norm_stats(0)
        norm_rows(X)
        with dve.Fori(0, KT // 4) as it:
            for u in range(4):
                dve.wait_ge(sem(f"ada0_in{u}"), 16 * it + 16)
                dve.wait_ge(sem("ada0_sum"), 4 * it + u)
                dve.scalar_tensor_tensor(acc0[:], ada0[:, u, :], cact[:, ds(4 * it + u, 1)], acc0[:], ALU.mult, ALU.add).then_inc(sem("ada0_sum"), 1)
        dve.wait_ge(sem("ada0_T"), 1)
        link(dve.tensor_tensor(sh_mix, aux[0][:, 0:KT], b_sh1, ALU.add))
        link(dve.tensor_tensor(gs_mix, aux[0][:, KT:2 * KT], b_sc1, ALU.add))
        dve.scalar_tensor_tensor(gs_mix, gs_mix, 1.0, g_mix, ALU.add, ALU.mult).then_inc(sem("gs_made"), 1)
        dve.wait_ge(sem("erow_T"), 1)
        dve.tensor_copy(erow[:], aux[3][0:NH, :]).then_inc(sem("erow_held"), 1)
        dve.wait_ge(sem("gs_made"), 1)
        features(False, gs_mix, sh_mix)
        dve.wait_ge(sem("ixw_hi"), 1)
        dve.tensor_tensor(wlo[:, 0:KT * NIXW], ixw_raw[:], whi[:, 0:KT * NIXW].bitcast(fp32), ALU.subtract).then_inc(sem("ixw_split"), 1)
        dve.wait_ge(sem("ixw_done"), 1)
        dve.tensor_copy(ixw[:, 1, :], lin[0][1][:, 0:NIXW]).then_inc(free1, 1)
        dve.wait_ge(free1, 1)
        dve.nop().then_inc(free1, 1)
        dve.wait_ge(free0, 1)
        dve.tensor_copy(kdup[:, :, 0:DIX], ixw[:, :, 0:DIX])
        dve.tensor_copy(kdup[:, :, DIX:P], ixw[:, :, 0:DIX]).then_inc(sem("kdup_made"), 1)
        link(dve.tensor_scalar(wix[:], ixw[:, :, DIX:NIXW], NIX ** -0.5, None, ALU.mult))
        for idx in range(RING):
            split(0, "A", 16, idx)

        cols = lambda it, k: ds(it * 2 * NB + k * NB, NB)

        def drains2(it, phase, dst, extra=None):
            hooks = dict(extra or {})
            for k, idx in ((0, 11), (1, 19)):
                hooks[idx] = list(hooks.get(idx, [])) + [lambda k=k: drain(it, phase, k, 8 * (k + 1), dst(k))]
            return hooks
        with dve.Fori(0, 3) as it:
            body(it, "A", 16, drains2(it, "A", lambda k: sbz[:, 1, cols(it, k)]))
        dve.wait_ge(sem("ada_T"), 1)
        link(dve.tensor_tensor(sc_ffn, aux[3][:, 0:KT], b_sc2, ALU.add))
        link(dve.scalar_tensor_tensor(gs_ffn, sc_ffn, 1.0, g_ffn, ALU.add, ALU.mult))
        dve.nop().then_inc(sem("mod_made"), 1)

        SC = HD ** -0.5

        def sb_dve(it):
            def log_keep(u):
                h = 2 * it + u
                z = aux[1][:, 0:3 * P]
                dve.wait_ge(sem("sb_z"), h + 1)
                dve.tensor_scalar(lb[:], z, SC, 0.0, ALU.mult, ALU.min).then_inc(sem("sb_own"), 1)
                dve.wait_ge(sem("sb_own"), 3 * h + 1)
                dve.scalar_tensor_tensor(az[:], lb[:], 2.0 / SC, z, ALU.mult, ALU.subtract).then_inc(sem("sb_az"), 1)
                dve.wait_ge(sem("sb_L"), h + 1)
                dve.tensor_tensor(lb[:], lb[:], az[:], ALU.subtract).then_inc(sem("sb_own"), 1)
                dve.wait_ge(sem("sb_own"), 3 * h + 2)
                dve.scalar_tensor_tensor(lk[:], z, -SC, lb[:], ALU.mult, ALU.add).then_inc(sem("sb_own"), 1)
                dve.wait_ge(sem("sb_own"), 3 * h + 3)
                dve.tensor_tensor(lk[:], lk[:], sbmask, ALU.mult).then_inc(sem("sb_lk"), 1)

            def weights(u):
                h = 2 * it + u
                dve.wait_ge(sem("sb_suf"), h + 1)
                dve.tensor_tensor(lb[:], lb[:], aux[2][:, 0:3 * P], ALU.add).then_inc(sem("sb_sm"), 1)
                dve.wait_ge(sem("sb_ex"), h + 1)
                dve.tensor_tensor(lb[:], lb[:], sbmask, ALU.mult).then_inc(sem("sb_a"), 1)
            hooks = {}
            for u in range(2):
                hooks.setdefault(8 * u + 6, []).append(lambda u=u: log_keep(u))
                hooks.setdefault(8 * u + 9, []).append(lambda u=u: weights(u))
            return hooks
        with dve.Fori(0, 3) as it:
            body(it, "B", 16, drains2(it, "B", lambda k: dsz[:, 1, cols(it, k)], sb_dve(it)))
        body(3, "B", 16, drains2(3, "B", lambda k: qix[:, 1, k * NB:(k + 1) * NB], sb_dve(3)))
        dve.wait_ge(sem("ada_T"), 2)
        link(dve.tensor_tensor(sh_ffn, aux[3][:, 0:KT], b_sh2, ALU.add))
        dve.nop().then_inc(sem("mod_made"), 1)

        link(dve.memset(score[:], 0.0))

        def ix_dve(it):
            def add(u):
                p = 4 * it + u
                for e in range(2):
                    dve.wait_ge(sem("ix_relu"), 2 * p + e + 1)
                    dve.wait_ge(sem("ix_sum"), 2 * p + e)
                    for tb, c in ((0, slice(0, P)), (1, slice(P, 3 * P))):
                        m = dve.scalar_tensor_tensor(score[:, c], r_ix[:, e, c], wix[:, tb, ds(2 * p + e, 1)], score[:, c], ALU.mult, ALU.add)
                    m.then_inc(sem("ix_sum"), 1)
            return {4 * u + 6: [lambda u=u: add(u)] for u in range(4)}
        with dve.Fori(0, 2) as it:
            body(it, "C1", 16, drains2(it, "C1", lambda k: gate_sb[:, 1, cols(it, k)], ix_dve(it)))
        dve.wait_ge(sem("ix_sum"), NIX)
        dve.tensor_tensor(selneg[:], score[:], cneg, ALU.add).then_inc(sem("tk_in"), 1)
        dve.wait_ge(sem("tk_in"), 1)
        for r in range(TOPK // 8):
            for tb, c in ((0, slice(0, P)), (1, slice(P, 3 * P))):
                link(dve.max(top8[:], selneg[:, c]))
                link(dve.match_replace(selneg[:, c], top8[:], selneg[:, c], TAKEN))
        link(dve.tensor_scalar(selneg[:], selneg[:], TAKEN / 2, NEG, ALU.is_gt, ALU.mult))
        link(dve.tensor_tensor(selneg[:], selneg[:], cneg, ALU.add))

        def ds_dve(it):
            def hold_k(u):
                h = 4 * it + u
                dve.wait_ge(sem("ds_q"), h + 1)
                dve.tensor_copy(qk_ds[:, S:2 * S], aux[0][:, S:2 * S]).then_inc(sem("ds_k"), 1)

            def soft(u):
                h = 4 * it + u
                s = u % 2
                dve.wait_ge(sem("ds_L"), h + 1)
                dve.tensor_tensor(lg[:, s, :], aux[1][:, 0:3 * P], selneg[:], ALU.add).then_inc(sem("ds_lg"), 1)
                dve.wait_ge(sem("ds_lg"), h + 1)
                parts = ((0, slice(0, P)), (1, slice(P, 3 * P)))
                for tb, c in parts:
                    m = dve.tensor_reduce(nmax[:, 2 * s + tb:2 * s + tb + 1], lg[:, s, c], AX.X, ALU.max, negate=True)
                m.then_inc(sem("ds_mx"), 1)
                dve.wait_ge(sem("ds_ex"), 2 * h + 2)
                dve.reciprocal(ssum[:, 2 * s:2 * s + 2], ssum[:, 2 * s:2 * s + 2]).then_inc(sem("ds_rs"), 1)
                dve.wait_ge(sem("ds_rs"), h + 1)
                for tb, c in parts:
                    m = dve.tensor_scalar(lg[:, s, c], lg[:, s, c], ssum[:, 2 * s + tb:2 * s + tb + 1], None, ALU.mult)
                m.then_inc(sem("ds_p"), 1)
            hooks = {}
            for offs, step in ((DS_L, soft), (DS_T, hold_k)):
                for u in range(4):
                    hooks.setdefault(offs[u] + AHEAD, []).append(lambda u=u, step=step: step(u))
            return hooks
        with dve.Fori(0, 2) as it:
            body(it, "C2", 16, drains2(it, "C2", lambda k: gate_ds[:, 1, cols(it, k)], ds_dve(it)))

        for n in range(4):
            dve.wait_ge(sem("oT_hi"), n + 1)
            src = (oT_sb, oT_ds)[n // 2][:, n % 2 * 4:n % 2 * 4 + 4, :]
            dve.tensor_tensor(lo[:, 4 * n:4 * n + 4, :], src, hi[:, 4 * n:4 * n + 4, :].bitcast(fp32), ALU.subtract).then_inc(sem("oT_split"), 1)

        def o_hooks(it):
            def take(gi):
                c = cols(it, gi // 2)
                drained(it, "O", 4 * (gi + 1))
                dve.wait_ge(sem("og_sig"), 4 * it + gi + 1)
                if gi % 2 == 0:
                    dve.tensor_tensor(merged[:, 1, c], lin[gi % 2][1][:], gate_sb[:, 1, c], ALU.mult).then_inc(free1, 1)
                else:
                    dve.tensor_tensor(gate_ds[:, 1, c], lin[gi % 2][1][:], gate_ds[:, 1, c], ALU.mult).then_inc(free1, 1)
                    dve.wait_ge(free1, 2 + G0["O"] + 4 * it + gi + 1)
                    dve.tensor_tensor(merged[:, 1, c], merged[:, 1, c], gate_ds[:, 1, c], ALU.add).then_inc(sem("og_add1"), 1)
            return {4 * gi + 7: [lambda gi=gi: take(gi)] for gi in range(4)}
        with dve.Fori(0, 2) as it:
            body(it, "O", 16, o_hooks(it))
        dve.wait_ge(sem("og_add1"), 4)
        dve.nop().then_inc(sem("merge_done"), 1)

        def modulation_row(n):
            dve.wait_ge(sem("ada_T"), n + 3)
            dve.wait_ge(sem("gtb_in"), 16 * (n + 1))
            for j in range(4):
                c = slice(j * NB, (j + 1) * NB)
                m = dve.tensor_tensor(gt_row[:, c], aux[j][:], gt_bias[:, c], ALU.add)
            m.then_inc(sem("gt_made"), 1)

        dve.wait_ge(sem("merge_done"), 2)
        modulation_row(0)
        features(True)
        with dve.Fori(0, 2) as it:
            body(it, "U", 16, drains2(it, "U", lambda k: y1[:, 1, cols(it, k)]))

        def combine(y, phase, n, row):
            dve.wait_ge(free1, 2 + G0[phase])
            if row is not None:
                dve.wait_ge(sem("gt_made"), row + 1)
                link(dve.tensor_tensor(y[:, 1, :], y[:, 1, :], gt_row[:], ALU.mult))
            dve.tensor_tensor(X[:, 1, :], X[:, 1, :], y[:, 1, :], ALU.add).then_inc(sem("xcomb"), 1)
            dve.wait_ge(sem("xcomb"), n)
        dve.wait_ge(sem("x_in"), 32)
        combine(y1, "F1p", 2, 0)
        dve.nop().then_inc(sem("gt_used"), 1)

        def ffn(n, y):
            name = f"F{n + 1}"
            base = n * FB
            flat = lambda t: t[:].rearrange("p a t -> p (a t)")

            def hidden(j):
                dve.wait_ge(sem("up_T"), base + j + 1)
                if n == 0:
                    dve.wait_ge(sem("act_made"), j + 1)
                    for e in range(2):
                        m = dve.tensor_tensor(hidf[:, 2 * e:2 * e + 2, :].rearrange("p k t -> p (k t)"), aux[e][:],
                                              cacc[:, 2 * e:2 * e + 2, :].rearrange("p k t -> p (k t)"), ALU.mult)
                    m.then_inc(sem("hidf_made"), 1)
                    dve.wait_ge(sem("hid_h"), j + 1)
                    dve.tensor_tensor(hid_lo[:], hidf[:], hid_hi[:].bitcast(fp32), ALU.subtract).then_inc(sem("hid_made"), 1)
                else:
                    dve.wait_ge(sem("hid_h"), FB + 2 * j + 2)
                    for e in range(2):
                        m = dve.tensor_tensor(hid_lo[:, 2 * e:2 * e + 2, :].rearrange("p k t -> p (k t)"), aux[e][:],
                                              hid_hi[:, 2 * e:2 * e + 2, :].rearrange("p k t -> p (k t)").bitcast(fp32), ALU.subtract)
                    m.then_inc(sem("hid_made"), 1)

            def conv(j, e):
                if e == 0:
                    dve.wait_ge(sem("gpad_made"), j + 1)
                fs = (2 * e, 2 * e + 1)
                col = lambda w, f: w[:, ds(4 * j + f, 1)]
                for f in fs:
                    m = dve.tensor_scalar(cacc[:, f, :], gpad[:, f, 2:], col(conv_w2, f), col(conv_b, f), ALU.mult, ALU.add)
                m.then_inc(sem("conv_made"), 1)
                for k, w in ((1, conv_w1), (2, conv_w0)):
                    dve.wait_ge(sem("conv_made"), 6 * j + 3 * e + k)
                    for f in fs:
                        m = dve.scalar_tensor_tensor(cacc[:, f, :], gpad[:, f, 2 - k:2 - k + S], col(w, f), cacc[:, f, :], ALU.mult, ALU.add)
                    m.then_inc(sem("conv_made"), 1)

            def activate(j):
                dve.wait_ge(sem("csig_made"), base + j + 1)
                g = cacc if n == 0 else gbuf
                dve.tensor_tensor(flat(cacc), flat(g), flat(csig), ALU.mult).then_inc(sem("act_made"), 1)

            def up(it, phase, gi, upto, j):
                if n == 0:
                    drain(it, phase, gi, upto, ubuf[:, 1, :])
                else:
                    drained(it, phase, upto)
                    dve.wait_ge(sem("act_made"), base + j + 1)
                    dve.tensor_tensor(ubuf[:, 1, :], lin[gi % 2][1][:], flat(cacc)[:, NB:2 * NB], ALU.mult).then_inc(free1, 1)

            def down(it, phase, gper, gi, c, upto):
                drained(it, phase, upto)
                dve.wait_ge(free1, 2 + G0[phase] + it * gper + gi)
                s = slice(c * NB, (c + 1) * NB)
                dve.tensor_tensor(y[:, 1, s], y[:, 1, s], lin[gi % 2][1][:], ALU.add).then_inc(free1, 1)

            def hooks(it, phase, gper, j, ups):
                hk = {}
                add = lambda idx, f: hk.setdefault(idx, []).append(f)
                add(11, lambda: drain(it, phase, 0, 8, gbuf[:, 1, :]))
                if n == 0:
                    add(14, lambda: conv(j, 0))
                    add(16, lambda: conv(j, 1))
                add(18 if n == 0 else 16, lambda: activate(j))
                if phase == name:
                    add(5, lambda: hidden(it))
                    for c in range(4):
                        add(13 + 2 * c, lambda c=c: down(it, phase, gper, 1 + c, c, 10 + 2 * c))
                add(ups, lambda: up(it, phase, 1 if phase != name else 5, ups - AHEAD + 1, j))
                return hk
            body(0, name + "p", 16, hooks(0, name + "p", 2, 0, 19))
            with dve.Fori(0, FB - 1) as it:
                body(it, name, 24, hooks(it, name, 6, it + 1, 27))
            hidden(FB - 1)
            hk = {5 + 2 * c: [lambda c=c: down(0, name + "e", 4, c, c, 2 * c + 2)] for c in range(4)}
            if n == 0:
                body(0, name + "e", 8, hk)
            else:
                for idx in range(4, 8):
                    split(0, name + "e", 8, idx)
                    for step in hk.get(idx, ()):
                        step()
                for idx in (9, 11):
                    hk[idx][0]()

        norm_stats(1)
        norm_rows(xs)
        features(False, gs_ffn, sh_ffn)
        link(dve.memset(gpad[:, :, 0:2], 0.0))
        link(dve.memset(yacc[:, 1, :], 0.0))
        ffn(0, yacc)
        modulation_row(1)
        combine(yacc, "GQ", 4, 1)

        norm_stats(2)
        dve.wait_ge(sem("late_in"), 48)
        dve.wait_ge(sem("xcomb"), 4)
        for tb in range(TB):
            dve.scalar_tensor_tensor(X[:, tb, :], X[:, tb, :], rstd[:, tb:tb + 1], gfin[:], ALU.mult, ALU.mult).then_inc(sem("xfin"), 1)
        dve.wait_ge(sem("xfin"), 2)
        norm_stats(3)
        norm_rows(xs)
        dve.wait_ge(sem("alr_hi_made"), 1)
        dve.tensor_tensor(alr_lo[:], alr_raw[:], alr_hi[:].bitcast(fp32), ALU.subtract).then_inc(sem("alr_split"), 1)
        features(False, g_n0)
        link(dve.memset(greset[:], 1.0))
        link(dve.memset(greset[:].rearrange("p (c t) -> p c t", t=GC)[:, :, 0:1], 0.0))
        dve.wait_ge(sem("alr_done"), 1)
        dve.tensor_copy(alr[:, 1, :], aux[1][:, 0:GR]).then_inc(sem("alr_held"), 1)

        def gq_drain(b):
            if b:
                dve.wait_ge(sem("gq_T"), b)
            drain(b // 2, "GQ", b % 2, 8 * (b % 2 + 1), gstage[:, 1, :])
        body(0, "GQ", 16, {11: [lambda: gq_drain(0)], 19: [lambda: gq_drain(1)]})
        body(1, "GQ", 16, {11: [lambda: gq_drain(2)], 19: [lambda: gq_drain(3)]})
        for f in range(8):
            dve.wait_ge(sem("gu_T"), f + 1)
            dve.tensor_scalar(gu[:, f * S:(f + 1) * S], aux[f % 2][:, 0:S], gla_b[:, f:f + 1], None, ALU.add).then_inc(sem("gu_made"), 1)
        dve.wait_ge(sem("gu_made"), 8)
        dve.scalar_tensor_tensor(gt1[:], gu[:], -1.0, gu[:], ALU.mult, ALU.min).then_inc(sem("gabs"), 1)
        link(dve.tensor_scalar(gu[:], gu[:], 0.0, 1.0 / 16, ALU.min, ALU.mult))
        gvd = lambda it: drains2(it, "GV", lambda k: gv[:, 1, cols(it, k)])
        body(0, "GV", 16, gvd(0))
        dve.wait_ge(sem("gln"), 1)
        link(dve.scalar_tensor_tensor(gu[:], gt1[:], -1.0 / 16, gu[:], ALU.mult, ALU.add))
        dve.tensor_tensor_scan(gb[:], greset[:], gu[:], 0.0, ALU.mult, ALU.add).then_inc(sem("gb_made"), 1)
        body(1, "GV", 16, gvd(1))
        with dve.Fori(0, 2) as it:
            body(it, "GR", 16, drains2(it, "GR", lambda k: gr[:, 1, cols(it, k)]))
        dve.wait_ge(half_used, H0["GO"])
        dve.wait_ge(free0, 2 + G0["GO"])
        dve.wait_ge(free1, 2 + G0["GO"])
        link(dve.memset(gq[:], 0.0))

        def zero(h):
            if h >= 2:
                dve.wait_ge(sem("go_T"), 2 * (h - 1))
            dve.memset(gsc[:, h % 2, :], 0.0).then_inc(sem("gsc_zero"), 1)

        def pick(h, lv):
            n = 7 * h + lv
            if lv == 0:
                dve.wait_ge(sem("gla_in"), 32)
                dve.wait_ge(sem("gsc_zero"), h + 1)
            dve.wait_ge(sem("gl_z"), n + 1)
            dve.wait_ge(sem("gl_picked"), n)
            dve.copy_predicated(gsc[:, h % 2, :], gmask[:, lv, :].bitcast(u32), aux[n % 2][:, 0:S]).then_inc(sem("gl_picked"), 1)

        def decayed(h, i):
            n, lv = 7 * h + i, GL_ITEMS[i]
            dve.wait_ge(sem("gl_e"), n + 1)
            if lv == 0:
                if h >= 2:
                    dve.wait_ge(sem("gk_T"), h - 1)
                dve.tensor_tensor(gkd[:, h % 2, :], gla_k(h), ge[:, n % 4, :], ALU.mult).then_inc(sem("gk_dec"), 1)
                dve.wait_ge(sem("gk_dec"), h + 1)
                dve.nop().then_inc(sem("gl_m"), 1)
                return
            j = 6 * h + lv - 1
            if j >= 3:
                dve.wait_ge(sem("gl_z"), 7 * ((j - 3) // 6) + (j - 3) % 6 + 2)
            m = LEVELS[lv - 1]
            e, o = pairs_by(ge[:, n % 4, :], m), pairs_by(gm[:, j % 3, :], m)
            dve.tensor_tensor(o[:, :, 1, :], pairs_by(gla_q(h), m)[:, :, 1, :], e[:, :, 1, :], ALU.mult)
            dve.tensor_tensor(o[:, :, 0, :], pairs_by(gla_k(h), m)[:, :, 0, :], e[:, :, 0, :], ALU.mult).then_inc(sem("gl_m"), 1)

        def queries(h):
            dve.wait_ge(sem("geb_made"), h + 1)
            if h >= 2:
                dve.wait_ge(sem("go_T"), 2 * (h - 1))
            q3, e3 = (t.rearrange("p (e t) -> p e t", e=2) for t in (gla_q(h), geb[:, h % 2, :]))
            for c in range(3):
                t, o = slice((c + 1) * GC, (c + 2) * GC), (c + 1) % 2 * GC
                m = dve.tensor_tensor(gq[:, h % 2, c, :, o:o + GC], q3[:, :, t], e3[:, :, t], ALU.mult)
            m.then_inc(sem("gq_made"), 1)

        def state(h, n):
            c, e, i = n // 2, n % 2, 6 * h + n
            dve.wait_ge(sem("gs_T"), i + 1)
            bank = lin[i % 4 // 2][i % 2][:]
            if c == 0:
                if h and e == 0:
                    dve.wait_ge(sem("go_T"), 2 * h)
                dve.tensor_copy(sts[:, 0, e, :], bank).then_inc(sem("gs_added"), 1)
            else:
                dve.wait_ge(sem("gs_added"), i - 1)
                last = e * S + (c + 1) * GC - 1
                dve.scalar_tensor_tensor(sts[:, c, e, :], sts[:, c - 1, e, :], geb[:, h % 2, last:last + 1], bank,
                                         ALU.mult, ALU.add).then_inc(sem("gs_added"), 1)

        for h in range(GH + 1):
            for i in range(7):
                if h < GH:
                    if i == 0:
                        zero(h)
                    decayed(h, i)
                    lv = GL_ITEMS[i]
                    if lv:
                        pick(h, lv - 1)
                    if i == 3:
                        queries(h)
                    if i == 6:
                        pick(h, 6)
                if h and i in (1, 3, 4):
                    for e in range(2):
                        state(h - 1, 2 * (1, 3, 4).index(i) + e)
        dve.nop().then_inc(sem("gr_in"), 1)
        dve.wait_ge(sem("gss_made"), TB * GH)
        dve.tensor_scalar(gss[:], gss[:], 1.0 / GV, EPS, ALU.mult, ALU.add).then_inc(sem("gms_made"), 1)
        dve.wait_ge(sem("gsd_made"), 1)
        link(dve.reciprocal(grs, grs))
        dve.wait_ge(sem("late_in"), 48)
        for tb in range(TB):
            dve.wait_ge(sem("gsig_made"), tb + 1)
            link(dve.tensor_tensor(gr[:, tb, :], gr[:, tb, :], y1[:, tb, :], ALU.mult))
            link(dve.tensor_tensor(gr[:, tb, :].rearrange("p (h v) -> p h v", h=GH), gr[:, tb, :].rearrange("p (h v) -> p h v", h=GH),
                                   gn[:].rearrange("p (a v) -> p a v", a=1).to_broadcast([P, GH, GV]), ALU.mult))
            for h in range(GH):
                c, n = slice(h * GV, (h + 1) * GV), tb * GH + h
                m = dve.scalar_tensor_tensor(gv[:, tb, c], gv[:, tb, c], grs[:, n:n + 1], gr[:, tb, c], ALU.mult, ALU.mult)
            m.then_inc(sem("go_done"), 1)
        features(True)
        with dve.Fori(0, 2) as it:
            body(it, "GO", 16, drains2(it, "GO", lambda k: y1[:, 1, cols(it, k)]))
        combine(y1, "F2p", 6, None)
        norm_stats(4)
        norm_rows(xs)
        features(False, g_n1)
        ffn(1, X)
        dve.wait_ge(free1, 2 + G0["end"])
        dve.nop().then_inc(sem("y_done"), 1)

    @block.gpsimd
    def _(pool):
        steps = [0]

        def link(op):
            steps[0] += 1
            op.then_inc(sem("pool_link"), 1)
            pool.wait_ge(sem("pool_link"), steps[0])

        def ada(n, kt, half, col):
            c = slice(half * (D // 2), (half + 1) * (D // 2))
            pool.wait_ge(ada_come[half], 8 * (n - half) + 16)
            pool.tensor_tensor(ada_in[:, half, :], ada_in[:, half, :], col.to_broadcast([P, D // 2]), ALU.mult).then_inc(sem("ada_mul"), 1)
            pool.wait_ge(sem("ada_mul"), n + 1)
            pool.wait_ge(sem("ada_sum"), n)
            pool.tensor_tensor(ada_acc[:, c], ada_acc[:, c], ada_in[:, half, :], ALU.add).then_inc(sem("ada_sum"), 1)
            pool.wait_ge(sem("ada_sum"), n + 1)
            pool.nop().then_inc(ada_left, 1)

        def pairs_of(n, kt, count):
            pool.tensor_copy(acol, cact[:, ds(kt, 1)]).then_inc(sem("acol_made"), 1)
            pool.wait_ge(sem("acol_made"), count + 1)
            for half in range(2):
                ada(n + half, kt, half, acol)

        def clear(piece):
            if piece:
                pool.wait_ge(sem("ada_T"), piece)
            link(pool.memset(ada_acc[:], 0.0))

        pool.wait_ge(sem("cact_made"), 1)
        clear(0)
        for k in range(8):
            pairs_of(2 * k, k, k)
        with pool.Fori(0, 2) as it:
            for k in range(4):
                pairs_of(8 * it + 2 * k + 16, 4 * it + k + 8, 4 * it + k + 8)

        def sb_stage(h, u):
            pool.tensor_copy(st_sb[:, u, :, :, :],
                             sbz[:].rearrange("p t (w h d) -> p w t h d", w=3, h=NH)[:, :, :, ds(h, 1), :].rearrange("p w t a d -> p w t (a d)")).then_inc(sem("sb_staged"), 1)
        pool.wait_ge(free0, 2 + G0["B"])
        pool.wait_ge(free1, 2 + G0["B"])
        sb_stage(0, 0)
        sb_stage(1, 1)
        clear(1)

        def b_pool(it, more):
            for u in range(2):
                for k in range(2):
                    kk = 4 * it + 2 * u + k
                    pairs_of(32 + 2 * kk, kk, 16 + kk)
                if more:
                    pool.wait_ge(sem("sb_o"), 2 * it + u + 1)
                    sb_stage(2 * it + u + 2, u)
        with pool.Fori(0, 3) as it:
            b_pool(it, True)
        b_pool(3, False)

        def ix_stage(p, u):
            pool.tensor_copy(st_ix[:, u % 2, :, :], qix[:, :, ds(p * P, P)]).then_inc(sem("ix_staged"), 1)
        pool.wait_ge(free0, 2 + G0["C1"])
        pool.wait_ge(free1, 2 + G0["C1"])
        pool.wait_ge(sem("sb_o"), NH)
        ix_stage(0, 0)
        ix_stage(1, 1)
        clear(2)

        def c_pool(it, n0, k0, stages):
            for u in range(4):
                kk = 4 * it + u + k0
                pairs_of(64 + 2 * kk, kk, 32 + kk)
                for st in stages[u]:
                    st()

        def ix_next(it, u):
            pool.wait_ge(sem("ix_T"), 4 * it + u + 1)
            ix_stage(4 * it + u + 2, u)
        c_pool(0, 64, 0, [[lambda u=u: ix_next(0, u)] for u in range(4)])
        c_pool(1, 64, 0, [[lambda u=u: ix_next(1, u)] if u < 2 else [] for u in range(4)])

        def qk_stage(h, u):
            src = dsz[:].rearrange("p t (w h d) -> p w t h d", w=3, h=NH)[:, 0:2, :, ds(h, 1), :].rearrange("p w t a d -> p w t (a d)")
            pool.tensor_copy(st_qk[:, u % 2, :, :, :], src).then_inc(sem("ds_qk_staged"), 1)

        def v_stage(h, u):
            pool.tensor_copy(st_v[:, u % 2, :, :], dsz[:, :, ds(h * HD + 2 * W, HD)]).then_inc(sem("ds_v_staged"), 1)

        for u in range(2):
            qk_stage(u, u)
            v_stage(u, u)

        def qk_next(it, u):
            pool.wait_ge(sem("ds_T"), 4 * it + u - 1)
            qk_stage(4 * it + u, u)

        def v_next(it, u):
            pool.wait_ge(sem("ds_o"), 4 * it + u - 1)
            v_stage(4 * it + u, u)

        def ds_pool(it, more):
            q, v = (lambda u: lambda: qk_next(it, u)), (lambda u: lambda: v_next(it, u))
            after = [[q(2), q(3)], [v(2)], [q(4), q(5)] if more else [], [v(3)] + ([v(4), v(5)] if more else [])]
            if more:
                after = [[q(2), q(3)], [v(2), q(4)], [q(5), v(3)], [v(4), v(5)]]
            c_pool(it, 64, 8, after)
        ds_pool(0, True)
        ds_pool(1, False)

        pool.nop().then_inc(sem("stage_free"), 1)
        pool.nop().then_inc(sem("stage_free"), 1)
        for it in range(2):
            for gi in range(4):
                g = 4 * it + gi
                c = ds(it * 2 * NB + gi // 2 * NB, NB)
                pool.wait_ge(free0, 2 + G0["O"] + g + 1)
                pool.wait_ge(sem("og_sig"), g + 1)
                if gi % 2 == 0:
                    pool.tensor_tensor(merged[:, 0, c], stage[:, 0, :], gate_sb[:, 0, c], ALU.mult).then_inc(sem("stage_free"), 1)
                else:
                    pool.tensor_tensor(gate_ds[:, 0, c], stage[:, 1, :], gate_ds[:, 0, c], ALU.mult).then_inc(sem("stage_free"), 1)
                    pool.wait_ge(sem("stage_free"), 2 + g + 1)
                    link(pool.tensor_tensor(merged[:, 0, c], merged[:, 0, c], gate_ds[:, 0, c], ALU.add))
        pool.nop().then_inc(sem("merge_done"), 1)

        def combine(y, phase, n, row):
            pool.wait_ge(free0, 2 + G0[phase])
            if row is not None:
                pool.wait_ge(sem("gt_made"), row + 1)
                link(pool.tensor_tensor(y[:, 0, :], y[:, 0, :], gt_row[:], ALU.mult))
            pool.tensor_tensor(X[:, 0, :], X[:, 0, :], y[:, 0, :], ALU.add).then_inc(sem("xcomb"), 1)
            pool.wait_ge(sem("xcomb"), n)
        clear(3)
        for k in range(6):
            pairs_of(96 + 2 * k, k, 48 + k)
        pool.wait_ge(sem("x_in"), 32)
        combine(y1, "F1p", 2, 0)
        pool.nop().then_inc(sem("gt_used"), 1)

        def ffn(n, y):
            name = f"F{n + 1}"
            base = n * FB

            def down(it, phase, gper, gi, c):
                k = n * 4 * FB + (0 if phase == name else 4 * (FB - 1)) + 4 * it + c
                pool.wait_ge(free0, 2 + G0[phase] + it * gper + gi + 1)
                pool.wait_ge(sem("dstage_free"), 2 + k)
                s = slice(c * NB, (c + 1) * NB)
                pool.tensor_tensor(y[:, 0, s], y[:, 0, s], dstage[:, c % 2, :], ALU.add).then_inc(sem("dstage_free"), 1)

            def up(g, j):
                if n == 1:
                    pool.wait_ge(free0, g)
                    pool.wait_ge(sem("act_made"), base + j + 1)
                    pool.tensor_tensor(ubuf[:, 0, :], ubuf[:, 0, :], cacc[:].rearrange("p a t -> p (a t)")[:, 0:NB], ALU.mult).then_inc(sem("up_mul"), 1)

            up(2 + G0[name + "p"] + 2, 0)
            with pool.Fori(0, FB - 1) as it:
                if n == 0:
                    pairs_of(108 + 2 * it, 6 + it, 54 + it)
                for c in range(4):
                    down(it, name, 6, 1 + c, c)
                up(2 + G0[name] + 6 * it + 6, it + 1)
            for c in range(4):
                down(0, name + "e", 4, c, c)

        link(pool.memset(yacc[:, 0, :], 0.0))
        pool.nop().then_inc(sem("dstage_free"), 1)
        pool.nop().then_inc(sem("dstage_free"), 1)
        ffn(0, yacc)
        pool.wait_ge(sem("dstage_free"), 2 + 4 * FB)
        combine(yacc, "GQ", 4, 1)
        pool.wait_ge(sem("gb_made"), 1)
        pool.wait_ge(half_used, H0["GO"])
        for h in range(GH):
            for i, lv in enumerate(GL_ITEMS):
                n = 7 * h + i
                if n >= 4:
                    pool.wait_ge(sem("gl_m"), n - 3)
                if lv:
                    m = LEVELS[lv - 1]
                    b, e = pairs_by(gla_sums(h), m), pairs_by(ge[:, n % 4, :], m)
                    ref = b[:, :, 0, m - 1:m].to_broadcast([P, 2 * S // (2 * m), m])
                    pool.tensor_tensor(e[:, :, 1, :], b[:, :, 1, :], ref, ALU.subtract)
                    pool.tensor_tensor(e[:, :, 0, :], ref, b[:, :, 0, :], ALU.subtract).then_inc(sem("gl_d"), 1)
                else:
                    b, e = (t.rearrange("p (c t) -> p c t", t=GC) for t in (gla_sums(h), ge[:, n % 4, :]))
                    pool.tensor_tensor(e, b[:, :, GC - 1:GC].to_broadcast([P, 8, GC]), b, ALU.subtract).then_inc(sem("gl_d"), 1)
        combine(y1, "F2p", 6, None)
        ffn(1, X)
        pool.wait_ge(sem("dstage_free"), 2 + 8 * FB)
        pool.nop().then_inc(sem("y_done"), 1)

    ctx.close()


INPUTS = ("x", "c", "w_ada", "b_ada", "g_mix", "w_in", "w_o_sb", "w_o_dsa", "w_out", "rel_bias", "g_ffn", "w_gate", "w_up",
          "conv_w", "conv_b", "w_down", "g_final", "norm_g_2", "gla_w_in_2", "gla_w_a2_2", "gla_b_a_2", "gla_g_norm_2",
          "gla_w_out_2", "ffn_w_gu_2", "ffn_w_down_2")


def constants():
    import numpy as np
    i = np.arange(P)
    key, query = i[:, None], i[None, :]
    con = np.zeros((P, 10, P), np.float32)
    con[:, 0] = key == query
    con[:, 1] = key + query == P - 1
    con[:, 2] = 1
    con[:, 3] = key > query
    con[:, 4] = con[:, 6] = key < query
    con[:, 5] = 1
    con[:, 7] = con[:, 9] = np.where(query > key, NEG, 0)
    dist = np.maximum(S - 1 - np.arange(2 * S), 0)
    exact = BUCKETS // 2
    far = exact + (np.log(np.maximum(dist, 1).astype(np.float32) / np.float32(exact))
                   / np.float32(np.log(128 / exact)) * np.float32(BUCKETS - exact)).astype(np.int32)
    bucket = np.where(dist < exact, dist, np.minimum(far, BUCKETS - 1))
    onehot = (np.arange(BUCKETS)[:, None] == bucket[None, :]).astype(np.float32)
    levels = np.zeros((P, 7, TB, P), np.float32)
    levels[:, 0] = (key == query)[:, None]
    for n, m in enumerate(LEVELS):
        levels[:, n + 1] = ((key // (2 * m) == query // (2 * m)) & (key // m < query // m))[:, None]
    return {"k_con": con.reshape(P, 10 * P), "k_onehot": onehot, "k_levels": levels.reshape(P, 7, S)}


def kernel(**inputs):
    import numpy as np
    import concourse.bacc as bacc
    from concourse.bass_utils import run_bass_kernel_spmd

    nc = bacc.Bacc("TRN2", target_bir_lowering=False, num_devices=1, dynamic_dma_scratch_size=1024)
    arrays, A = {}, {}
    given = {name: np.ascontiguousarray(inputs[name]) for name in INPUTS}
    for name, a in list(given.items()) + list(constants().items()):
        arrays[f"in_{name}_dram"] = a
        A[name] = nc.dram_tensor(f"in_{name}_dram", a.shape, mybir.dt.from_np(a.dtype), kind="ExternalInput").ap()
    out = nc.dram_tensor("out_0_dram", (1, S, D), mybir.dt.float32, kind="ExternalOutput").ap()
    build_program(nc, A, out)
    r = run_bass_kernel_spmd(nc, [arrays], core_ids=[0])
    return r.results[0]["out_0_dram"]
```

```python
import concourse.bass as bass
from concourse import mybir
from contextlib import ExitStack

P = 128
S = 256
TB = S // P
D = 2048
KT = D // P
NB = 512
HD = 128
NH = 8
W = NH * HD
NIX, DIX = 16, 64
TOPK = S // 4
FF = 5632
FB = FF // NB
BUCKETS = 32
EPS = 1e-6
GH, GK, GV, GC, GR = 4, 256, 512, 64, 16
NIXW = DIX + NIX
C_IX = 6 * W + NIX * DIX
C_GATE = C_IX + NIXW
NEG = -1e30
TAKEN = -3e38
SLAB = 4 * NB
HALF = SLAB // 2
RING = 4
DS_T, DS_L, DS_P, DS_O = (0, 3, 6, 8), (2, 5, 8, 10), (5, 8, 11, 13), (7, 10, 13, 15)
AHEAD = 4
LEVELS = (32, 16, 8, 4, 2, 1)
GL_ITEMS = (1, 2, 0, 3, 4, 5, 6)

PHASES = [
    ("A", 3, 16, 2), ("B", 4, 16, 2), ("C1", 2, 16, 2), ("C2", 2, 16, 2), ("O", 2, 16, 4), ("U", 2, 16, 2),
    ("F1p", 1, 16, 2), ("F1", FB - 1, 24, 6), ("F1e", 1, 8, 4),
    ("GQ", 2, 16, 2), ("GV", 2, 16, 2), ("GR", 2, 16, 2), ("GO", 2, 16, 2),
    ("F2p", 1, 16, 2), ("F2", FB - 1, 24, 6), ("F2e", 1, 8, 4),
]
H0, G0 = {}, {}
_h = _g = 0
for _name, _n, _halves, _groups in PHASES:
    H0[_name], G0[_name] = _h, _g
    _h += _n * _halves
    _g += _n * _groups
H0["end"], G0["end"] = _h, _g


def build_program(nc, A, out):
    fp32, fp32r, u32 = mybir.dt.float32, mybir.dt.float32r, mybir.dt.uint32
    ALU, ACT, AX = mybir.AluOpType, mybir.ActivationFunctionType, mybir.AxisListType
    ds = bass.ds
    ctx = ExitStack()

    KB = 1024
    base = (nc.sbuf_base + 31) // 32 * 32
    ARENA, XB, ADA, CONST = 96 * KB, 168 * KB, 184 * KB, 200 * KB


    def at(name, shape, offset, dtype=fp32):
        return nc.alloc_sbuf_tensor_at("sb_" + name, shape, dtype, offset=base + int(offset))

    raw = at("raw", [P, RING, SLAB], 0)
    whi = at("whi", [P, RING * HALF], 32 * KB, fp32r)
    wlo = at("wlo", [P, RING * HALF], 48 * KB, fp32r)
    hi = at("act_hi", [P, KT, S], 64 * KB, fp32r)
    lo = at("act_lo", [P, KT, S], 80 * KB, fp32r)
    junk = at("junk", [P, D], 80 * KB)
    X = at("x", [P, TB, D], XB)
    ada0 = at("ada0", [P, 4, 2 * D], ARENA)
    acc0 = at("acc0", [P, 2 * D], 64 * KB)
    ixw_raw = at("ixw_raw", [P, KT * NIXW], ARENA + 64 * KB)
    ixw_hi = at("ixw_hi", [P, KT * NIXW], ARENA + 24 * KB, fp32r)
    ixw_lo = at("ixw_lo", [P, KT * NIXW], ARENA + 32 * KB, fp32r)
    ada_in = at("ada_in", [P, 2, D // 2], ADA)
    ada_acc = at("ada_acc", [P, D], ADA + 8 * KB)
    sbz = at("sbz", [P, TB, 3 * W], ARENA)
    dsz = at("dsz", [P, TB, 3 * W], ARENA + 24 * KB)
    qix = at("qix", [P, TB, W], ARENA + 48 * KB)
    oT_sb = at("oT_sb", [P, NH, S], ARENA + 64 * KB)
    oT_ds = at("oT_ds", [P, NH, S], ARENA + 16 * KB)
    gate_sb = at("gate_sb", [P, TB, D], ARENA)
    gate_ds = at("gate_ds", [P, TB, D], ARENA + 48 * KB)
    hank1 = at("hank1", [P, NH, S], XB)
    hank0 = at("hank0", [P, NH, P], XB + 8 * KB)
    selneg = at("selneg", [P, 3 * P], XB + 12 * KB)
    top8 = at("top8", [P, 8], XB + 14 * KB)
    st_sb = at("st_sb", [P, 2, 3, TB, HD], ARENA + 56 * KB)
    qk_sb = at("qk_sb", [P, 2 * S], ARENA + 62 * KB)
    st_ix = at("st_ix", [P, 2, TB, P], ARENA + 56 * KB)
    q_ixT = at("q_ixT", [P, S], ARENA + 58 * KB)
    r_ix = at("r_ix", [P, 2, 3 * P], ARENA + 59 * KB)
    score = at("score", [P, 3 * P], ARENA + 62 * KB)
    merged = at("merged", [P, TB, D], ARENA + 24 * KB)
    y1 = at("y1", [P, TB, D], ARENA)
    gt_row = at("gt_row", [P, D], ARENA + 49 * KB)
    gt_bias = at("gt_bias", [P, D], ARENA + 57 * KB)
    xs = at("xs", [P, TB, D], ARENA + 24 * KB)
    aff = at("aff", [P, 2, 2 * S], ARENA + 20 * KB)
    yacc = at("yacc", [P, TB, D], ARENA)
    hid_hi = at("hid_hi", [P, 4, S], ARENA + 16 * KB, fp32r)
    hid_lo = at("hid_lo", [P, 4, S], ARENA + 20 * KB, fp32r)
    gbuf = at("gbuf", [P, TB, NB], ARENA + 24 * KB)
    ubuf = at("ubuf", [P, TB, NB], ARENA + 28 * KB)
    gpad = at("gpad", [P, 4, S + 2], ARENA + 32 * KB)
    cacc = at("cacc", [P, 4, S], ARENA + 37 * KB)
    csig = at("csig", [P, 4, S], ARENA + 41 * KB)
    hidf = at("hidf", [P, 4, S], ARENA + 45 * KB)
    dstage = at("dstage", [P, 2, NB], ARENA + 65 * KB)
    gqk = at("gqk", [P, 2 * GH * GK // P, S], ARENA)
    gv = at("gv", [P, TB, D], ARENA + 16 * KB)
    gr = at("gr", [P, TB, D], ARENA + 32 * KB)
    gb = at("gb", [P, 8 * S], ARENA + 48 * KB)
    gu = at("gu", [P, 8 * S], ARENA + 56 * KB)
    gt1 = at("gt1", [P, 8 * S], ARENA + 64 * KB)
    greset = at("greset", [P, 8 * S], ADA)
    gmask = at("gmask", [P, 7, S], ADA + 8 * KB)
    alr_raw = at("alr_raw", [P, KT * GR], ARENA + 69 * KB)
    alr_hi = at("alr_hi", [P, KT * GR], ARENA + 41 * KB, fp32r)
    alr_lo = at("alr_lo", [P, KT * GR], ARENA + 42 * KB, fp32r)
    alrT = at("alrT", [GR, S], ARENA + 44 * KB)
    wa2 = at("wa2", [GR, GH * GK], CONST + 10 * KB + 512)
    gstage = at("gstage", [P, TB, NB], ARENA + 36 * KB)
    GT = ARENA + 56 * KB
    sts = at("gstates", [P, 3, 2, GV], GT)
    GU = 64 * KB
    ge = at("ge", [P, 4, 2 * S], GU)
    gm = at("gm", [P, 3, 2 * S], GU + 8 * KB)
    gsc = at("gsc", [P, 2, S], GU + 14 * KB)
    geb = at("geb", [P, 2, 2 * S], GU + 16 * KB)
    gkd = at("gkd", [P, 2, 2 * S], GU + 20 * KB)
    gkdT = at("gkdT", [P, TB, GK], GU + 24 * KB)
    gq = at("gq", [P, 2, 3, 2, P], ADA)
    gla_q = lambda h: gqk[:, 2 * h:2 * h + 2, :].rearrange("p e t -> p (e t)")
    gla_k = lambda h: gqk[:, 2 * (GH + h):2 * (GH + h) + 2, :].rearrange("p e t -> p (e t)")
    gla_sums = lambda h: gb[:, h * 2 * S:(h + 1) * 2 * S]
    gla_v = lambda h, tb: gv[:, tb, h * GV:(h + 1) * GV]
    pairs_by = lambda t, m: t.rearrange("p (n e m) -> p n e m", e=2, m=m)
    gfin = at("gfin", [P, D], CONST + 10 * KB + 512)
    gsig = at("gsig", [P, TB, NB], ARENA + 68 * KB)
    gn = at("gn", [P, GV], CONST + 18 * KB + 512)
    gjunk = at("gjunk", [P, GV], GU + 28 * KB)
    gss = at("gss", [P, TB * GH], CONST + 20 * KB + 512)
    con = at("con", [P, 4 * P + 6 * P], CONST)
    ident, flip, ones, later = (con[:, n * P:(n + 1) * P] for n in range(4))
    sbmask, cneg = con[:, 4 * P:7 * P], con[:, 7 * P:10 * P]
    par1 = at("par1", [P, 112], CONST + 5 * KB)
    par2 = at("par2", [P, 120], CONST + 5 * KB + 512)
    par3 = at("par3", [P, 96], CONST + 6 * KB)
    small = at("small", [P, 256], CONST + 6 * KB + 512)
    ixw = at("ixw", [P, TB, NIXW], CONST + 7 * KB + 512)
    kdup = at("kdup", [P, TB, P], CONST + 8 * KB + 256)
    k_ixT = at("k_ixT", [P, S], CONST + 9 * KB + 256)
    wix = at("wix", [P, TB, NIX], CONST + 10 * KB + 256)
    T = CONST + 10 * KB + 512
    onehot = at("onehot", [BUCKETS, 2 * S], T)
    relb = at("relb", [BUCKETS, NH], T + 2 * KB)
    erow = at("erow", [NH, 2 * S], T + 4 * KB)
    parr = at("parr", [P, 3, P], T + 2 * KB + 64)
    az = at("az", [P, 3 * P], T)
    lb = at("lb", [P, 3 * P], T + 1536)
    lk = at("lk", [P, 3 * P], T + 3072)
    st_qk = at("st_qk", [P, 2, 2, TB, HD], T)
    st_v = at("st_v", [P, 2, TB, HD], T + 4 * KB)
    qk_ds = at("qk_ds", [P, 2 * S], T + 6 * KB)
    lg = at("lg", [P, 2, 3 * P], T + 8 * KB)
    PT = at("PT", [P, 3 * P], XB + 14 * KB + 64)

    cact, gs_mix, sh_mix, sc_ffn, sh_ffn, gs_ffn = (small[:, n * KT:(n + 1) * KT] for n in range(6))
    csg = small[:, 96:112]
    ss, ssy = small[:, 112:114], small[:, 114:116]
    rstd, rstdy = small[:, 116:118], small[:, 118:120]
    ry = small[:, 138:140]
    ssum = small[:, 120:124]
    nmax = small[:, 124:128]
    grs = small[:, 128:136]
    acol = small[:, 136:137]
    c_col, g_mix, g_ffn, g_n0, g_n1, b_sh1, b_sc1 = (par1[:, n * KT:(n + 1) * KT] for n in range(7))
    b_sh2, b_sc2, conv_b, conv_w0 = par2[:, 0:16], par2[:, 16:32], par2[:, 32:76], par2[:, 76:120]
    conv_w1, conv_w2, gla_b = par3[:, 0:44], par3[:, 44:88], par3[:, 88:96]

    lin = [[ctx.enter_context(nc.psum_tensor(f"lin{g}{t}", [P, NB], fp32)) for t in range(TB)] for g in range(2)]
    aux = [ctx.enter_context(nc.psum_tensor(f"aux{n}", [P, NB], fp32)) for n in range(4)]

    tiled = lambda w: w.rearrange("(k p) n -> p k n", p=P)
    w_ada, w_in, w_out = A["w_ada"][0], tiled(A["w_in"][0]), tiled(A["w_out"][0])
    w_o = [tiled(A["w_o_sb"][0]), tiled(A["w_o_dsa"][0])]
    w_ffn = [(tiled(A["w_gate"][0]), 0, tiled(A["w_up"][0]), 0, tiled(A["w_down"][0])),
             (tiled(A["ffn_w_gu_2"][0]), 0, tiled(A["ffn_w_gu_2"][0]), FF, tiled(A["ffn_w_down_2"][0]))]
    w_gla, w_gla_out = tiled(A["gla_w_in_2"][0]), tiled(A["gla_w_out_2"][0])
    tokens = lambda x: x.rearrange("(t p) n -> p t n", p=P)
    rows = lambda v: v.rearrange("(r c) -> r c", c=P)
    e_dram = nc.dram_tensor("bias_by_distance", (NH, 2 * S), fp32, kind="Internal").ap()

    sems = {}

    def sem(name):
        if name not in sems:
            sems[name] = ctx.enter_context(nc.semaphore(name))
        return sems[name]

    slab_in = [sem(f"slab_in{n}") for n in range(RING)]
    hi_made, lo_made = sem("hi_made"), sem("lo_made")
    half_used = sem("half_used")
    free0, free1 = sem("free0"), sem("free1")
    ada_left = sem("ada_left")
    ada_come = [sem(f"ada_come{n}") for n in range(2)]
    block = ctx.enter_context(nc.Block())

    @block.sync
    def _(sp):
        def slab(it, phase, per, s, src):
            if not (phase == "A" and s < RING and isinstance(it, int)):
                sp.wait_ge(lo_made, H0[phase] + it * per + 2 * (s - RING) + 2)
            sp.dma_start(raw[:, s % RING, :].rearrange("p (k n) -> p k n", k=4), src).then_inc(slab_in[s % RING], 16)

        def ada_chunk(n, piece, j):
            if not (isinstance(n, int) and n < 2):
                sp.wait_ge(ada_left, n - 1)
            kt, half = (j // 2, j % 2) if isinstance(j, int) else j
            sp.dma_start(ada_in[:, half, :], w_ada[ds(kt * P, P), piece * D + half * (D // 2):piece * D + (half + 1) * (D // 2)]
                         ).then_inc(ada_come[half], 16)

        sp.dma_start(con[:], A["k_con"]).then_inc(sem("par_in"), 16)
        small_loads = [
            (0, 0, rows(A["c"][0])), (0, 16, rows(A["g_mix"][0])), (0, 32, rows(A["g_ffn"][0])),
            (0, 48, rows(A["norm_g_2"][0, 0])), (0, 64, rows(A["norm_g_2"][0, 1])),
            (0, 80, rows(A["b_ada"][0, 0:2 * D])),
            (1, 0, rows(A["b_ada"][0, 3 * D:5 * D])), (1, 32, rows(A["conv_b"][0])), (1, 76, rows(A["conv_w"][0, 0])),
            (2, 0, rows(A["conv_w"][0, 1])), (2, 44, rows(A["conv_w"][0, 2])), (2, 88, rows(A["gla_b_a_2"][0])),
        ]
        for n, r, src in small_loads:
            sp.dma_start(parr[r:r + src.shape[0], n, :], src).then_inc(sem("par_in"), 16)
        sp.dma_start(X[:], tokens(A["x"][0])).then_inc(sem("x_in"), 16)
        for kt in range(4):
            sp.dma_start(ada0[:, kt, :], w_ada[kt * P:(kt + 1) * P, 0:2 * D]).then_inc(sem(f"ada0_in{kt}"), 16)
        with sp.Fori(1, KT // 4) as it:
            for u in range(4):
                sp.wait_ge(sem("ada0_sum"), 4 * it + u - 2)
                sp.dma_start(ada0[:, u, :], w_ada[ds((4 * it + u) * P, P), 0:2 * D]).then_inc(sem(f"ada0_in{u}"), 16)
        sp.dma_start(ixw_raw[:].rearrange("p (k n) -> p k n", k=KT), w_in[:, :, C_IX:C_IX + NIXW]).then_inc(sem("ixw_in"), 16)
        sp.dma_start(onehot[:], A["k_onehot"]).then_inc(sem("rel_in"), 16)
        sp.dma_start(relb[:], A["rel_bias"]).then_inc(sem("rel_in"), 16)

        def a_body(it):
            for s in range(8):
                slab(it, "A", 16, s, w_in[:, 4 * (s % 4):4 * (s % 4) + 4, ds(it * 2 * NB + s // 4 * NB, NB)])
                ada_chunk(8 * it + s + 8, 4, ((8 * it + s + 8) // 2 if isinstance(it, int) else 4 * it + s // 2 + 4, s % 2))
        for s in range(RING):
            slab(0, "A", 16, s, w_in[:, 4 * s:4 * s + 4, 0:NB])
        for j in range(6):
            ada_chunk(j, 4, j)
        for s in range(RING, 8):
            slab(0, "A", 16, s, w_in[:, 4 * (s % 4):4 * (s % 4) + 4, NB:2 * NB])
            for j in range(2):
                ada_chunk(6 + 2 * (s - RING) + j, 4, 6 + 2 * (s - RING) + j)
        for j in range(14, 16):
            ada_chunk(j, 4, j)
        with sp.Fori(1, 3) as it:
            a_body(it)
        sp.wait_ge(sem("erow_held"), 1)
        sp.dma_start(e_dram, erow[:]).then_inc(sem("e_out"), 16)
        sp.wait_ge(sem("e_out"), 16)
        sp.wait_ge(sem("tt_T"), KT // 2)
        for h in range(NH):
            src = e_dram[h:h + 1, 0:P]
            sp.dma_start(hank1[:, h, :], bass.AP(tensor=src.tensor, offset=src.offset, ap=[[1, P], [1, S]])).then_inc(sem("hank_in"), 16)
            src = e_dram[h:h + 1, P:2 * P]
            sp.dma_start(hank0[:, h, :], bass.AP(tensor=src.tensor, offset=src.offset, ap=[[1, P], [1, P]])).then_inc(sem("hank_in"), 16)

        def cols_body(it, phase, col0, chunk0, piece, k0, every=1):
            for s in range(8):
                slab(it, phase, 16, s, w_in[:, 4 * (s % 4):4 * (s % 4) + 4, ds(it * 2 * NB + (col0 + s // 4 * NB), NB)])
                if s % every == 0:
                    c, kts = s // every, 4 // every
                    ada_chunk(chunk0 + 2 * kts * it + c, piece, (k0 + kts * it + c // 2, c % 2))
        with sp.Fori(0, 4) as it:
            cols_body(it, "B", 6 * NB, 32, 3, 0, 2)
        with sp.Fori(0, 2) as it:
            cols_body(it, "C1", C_GATE, 48, 3, 8)
        with sp.Fori(0, 2) as it:
            cols_body(it, "C2", C_GATE + D, 64, 2, 0)

        with sp.Fori(0, 2) as it:
            for s in range(8):
                slab(it, "O", 16, s, w_o[s % 4 // 2][:, 4 * (s % 2):4 * (s % 2) + 4, ds(it * 2 * NB + s // 4 * NB, NB)])
                ada_chunk(80 + 8 * it + s, 2, (8 + 4 * it + s // 2, s % 2))
        sp.wait_ge(half_used, H0["O"])
        sp.dma_start(X[:], tokens(A["x"][0])).then_inc(sem("x_in"), 16)
        for it in range(2):
            for s in range(8):
                slab(it, "U", 16, s, w_out[:, 4 * (s % 4):4 * (s % 4) + 4, (2 * it + s // 4) * NB:(2 * it + s // 4 + 1) * NB])
                if it == 1:
                    ada_chunk(96 + s, 5, s)
                if (it, s) == (0, 3):
                    sp.wait_ge(sem("merge_done"), 1)
                    sp.dma_start(gt_bias[:], A["b_ada"][0:1, 2 * D:3 * D].to_broadcast([P, D])).then_inc(sem("gtb_in"), 16)

        def ffn(n):
            w_g, g0, w_u, u0, w_d = w_ffn[n]
            name = f"F{n + 1}"

            def gate_up(it, phase, per, first, j, w, c0):
                for s in range(4):
                    slab(it, phase, per, first + s, w[:, 4 * s:4 * s + 4, ds(j * NB + c0, NB)])
                    if (phase, first) == ("F1p", 0):
                        ada_chunk(104 + s, 5, 8 + s)

            def down(it, phase, per, first, j):
                for s in range(4):
                    slab(it, phase, per, first + s, w_d[:, ds(4 * j, 4), s * NB:(s + 1) * NB])

            gate_up(0, name + "p", 16, 0, 0, w_g, g0)
            gate_up(0, name + "p", 16, 4, 0, w_u, u0)
            if n == 0:
                sp.wait_ge(sem("gt_used"), 2)
                sp.dma_start(gt_bias[:], A["b_ada"][0:1, 5 * D:6 * D].to_broadcast([P, D])).then_inc(sem("gtb_in"), 16)
                sp.dma_start(gfin[:], A["g_final"].rearrange("(a n) -> a n", a=1).to_broadcast([P, D])).then_inc(sem("late_in"), 16)
                sp.dma_start(gn[:], A["gla_g_norm_2"][0:1, :].to_broadcast([P, GV])).then_inc(sem("late_in"), 16)
                sp.dma_start(alr_raw[:].rearrange("p (k n) -> p k n", k=KT), w_gla[:, :, 2 * D + 2 * GH * GK:]).then_inc(sem("late_in"), 16)
            with sp.Fori(0, FB - 1) as it:
                gate_up(it, name, 24, 0, it + 1, w_g, g0)
                if n == 0:
                    for half in range(2):
                        ada_chunk(108 + 2 * it + half, 5, (6 + it, half))
                down(it, name, 24, 4, it)
                gate_up(it, name, 24, 8, it + 1, w_u, u0)
            down(0, name + "e", 8, 0, FB - 1)

        ffn(0)

        def gla_body(it, phase, col0, w=w_gla):
            for s in range(8):
                slab(it, phase, 16, s, w[:, 4 * (s % 4):4 * (s % 4) + 4, ds(it * 2 * NB + (col0 + s // 4 * NB), NB)])
        for phase, col0 in (("GQ", 0), ("GV", D), ("GR", 2 * D)):
            with sp.Fori(0, 2) as it:
                gla_body(it, phase, col0)
            if phase == "GQ":
                sp.wait_ge(sem("xfin"), 1)
                sp.dma_start(wa2[:], A["gla_w_a2_2"][0]).then_inc(sem("gla_in"), 16)
                sp.dma_start(gmask[:], A["k_levels"]).then_inc(sem("gla_in"), 16)
        with sp.Fori(0, 2) as it:
            gla_body(it, "GO", 0, w_gla_out)
        ffn(1)
        for c in range(4):
            sp.wait_ge(free1, 2 + G0["F2e"] + c + 1)
            sp.wait_ge(sem("dstage_free"), 2 + 4 * (2 * FB - 1) + c + 1)
            sp.dma_start(tokens(out[0])[:, :, c * NB:(c + 1) * NB], X[:, :, c * NB:(c + 1) * NB]).then_inc(sem("out_done"), 16)
        sp.wait_ge(sem("out_done"), 4 * 16)
    @block.tensor
    def _(pe):
        pairs = [0]

        def half(it, phase, per, idx, gi, kt, first, last, x_hi=hi, x_lo=lo, halves_before=0):
            pe.wait_ge(lo_made, H0[phase] + it * per + idx + 1)
            for q in range(2):
                w = slice(idx % RING * HALF + q * NB, idx % RING * HALF + (q + 1) * NB)
                for tb in range(TB):
                    o, t = lin[gi % 2][tb][:], slice(tb * P, (tb + 1) * P)
                    pe.matmul(o, x_hi[:, kt + q, t], whi[:, w], start=first and q == 0, stop=False)
                    pe.matmul(o, x_hi[:, kt + q, t], wlo[:, w], start=False, stop=False)
                    m = pe.matmul(o, x_lo[:, kt + q, t], whi[:, w], start=False, stop=last and q == 1)
            m.then_inc(half_used, 1)

        def group(it, phase, per, gper, idx0, gi, n, hooks, kt0=0, x_hi=hi, x_lo=lo, lead=None, parts=None):
            pe.wait_ge(free0, G0[phase] + it * gper + gi + 1)
            pe.wait_ge(free1, G0[phase] + it * gper + gi + 1)
            for i in range(n):
                if parts is not None and i % 2 == 0:
                    pe.wait_ge(sem("oT_split"), parts + i // 2 + 1)
                if lead is not None:
                    pe.wait_ge(sem("tt_lo"), pairs[0] - 3 if i < 4 else pairs[0] - 7 + i)
                half(it, phase, per, idx0 + i, gi, kt0 + 2 * i, i == 0, i == n - 1, x_hi, x_lo)
                if lead is not None and i < 4:
                    turn(lead, 4 + i)
                hooks(idx0 + i)

        def turn(src, g, ready=None):
            n = pairs[0]
            if n >= 4:
                pe.wait_ge(sem("tt_free"), n - 3)
            if ready is not None:
                pe.wait_ge(*ready)
            for q in range(2):
                for tb in range(TB):
                    m = pe.transpose(aux[n % 4][:, q * S + tb * P:q * S + (tb + 1) * P],
                                     src[:, tb, (2 * g + q) * P:(2 * g + q + 1) * P], ident)
            m.then_inc(sem("tt_T"), 1)
            pairs[0] += 1

        def first_features(src):
            for g in range(KT // 4):
                turn(src, g)

        def ada_columns(n):
            pe.wait_ge(sem("ada_sum"), 32 * (n + 1))
            for j in range(KT):
                m = pe.matmul(aux[3][:, j:j + 1], ada_acc[:, j * P:(j + 1) * P], ones[:, 0:1], start=True, stop=True)
            m.then_inc(sem("ada_T"), 1)

        def ada_rows(n):
            pe.wait_ge(sem("ada_sum"), 32 * (n + 1))
            for j in range(4):
                m = pe.matmul(aux[j][:], ones, ada_acc[:, j * NB:(j + 1) * NB], start=True, stop=True)
            m.then_inc(sem("ada_T"), 1)

        none = lambda idx: None

        pe.wait_ge(sem("par_in"), 13 * 16)
        for n, rws in enumerate((112, 120, 96)):
            m = pe.transpose(aux[n][:, 0:rws], parr[0:rws, n, :], ident[0:rws, 0:rws])
        m.then_inc(sem("par_T"), 1)
        pe.wait_ge(sem("rel_in"), 32)
        pe.matmul(aux[3][0:NH, :], relb[:], onehot[:], start=True, stop=True).then_inc(sem("erow_T"), 1)
        pe.wait_ge(sem("par_cols"), 1)
        pe.wait_ge(sem("ada0_sum"), KT)
        for j in range(2 * KT):
            m = pe.matmul(aux[0][:, j:j + 1], acc0[:, j * P:(j + 1) * P], ones[:, 0:1], start=True, stop=True)
        m.then_inc(sem("ada0_T"), 1)
        pe.wait_ge(sem("gs_made"), 1)
        pe.wait_ge(sem("erow_held"), 1)
        pe.wait_ge(sem("xs_made"), 2)
        first_features(X)

        def project_ix():
            pe.wait_ge(sem("ixw_split"), 1)
            for tb in range(TB):
                t = slice(tb * P, (tb + 1) * P)
                for kt in range(KT):
                    o, w = aux[1 + tb][:, 0:NIXW], slice(kt * NIXW, (kt + 1) * NIXW)
                    pe.matmul(o, hi[:, kt, t], ixw_hi[:, w], start=kt == 0, stop=False)
                    pe.matmul(o, hi[:, kt, t], ixw_lo[:, w], start=False, stop=False)
                    m = pe.matmul(o, lo[:, kt, t], ixw_hi[:, w], start=False, stop=kt == KT - 1)
            m.then_inc(sem("ixw_done"), 1)

        group(0, "A", 16, 2, 0, 0, 8, none, lead=X)
        group(0, "A", 16, 2, 8, 1, 8, none)
        project_ix()
        with pe.Fori(1, 3) as it:
            for k in range(2):
                group(it, "A", 16, 2, 8 * k, k, 8, none)
        pe.wait_ge(sem("kdup_made"), 1)
        for tb in range(TB):
            m = pe.transpose(aux[0][:, tb * P:(tb + 1) * P], kdup[:, tb, :], ident)
        m.then_inc(sem("kix_T"), 1)
        ada_columns(0)

        def sb_turn(h, u):
            pe.wait_ge(sem("sb_staged"), h + 1)
            for w in range(2):
                for tb in range(TB):
                    m = pe.transpose(aux[0][:, w * S + tb * P:w * S + (tb + 1) * P], st_sb[:, u, w, tb, :], ident)
            m.then_inc(sem("sb_T"), 1)

        def sb_scores(h, u):
            pe.wait_ge(sem("sb_qk"), h + 1)
            pe.matmul(aux[1][:, 0:S], qk_sb[:, S:S + P], qk_sb[:, 0:S], start=True, stop=True)
            pe.matmul(aux[1][:, S:S + P], qk_sb[:, S + P:2 * S], qk_sb[:, P:S], start=True, stop=True).then_inc(sem("sb_z"), 1)

        def sb_suffix(h, u):
            pe.wait_ge(sem("sb_lk"), h + 1)
            pe.matmul(aux[2][:, 0:S], later, lk[:, 0:S], start=True, stop=False)
            pe.matmul(aux[2][:, P:S], ones, lk[:, S:S + P], start=False, stop=True)
            pe.matmul(aux[2][:, S:S + P], later, lk[:, S:S + P], start=True, stop=True).then_inc(sem("sb_suf"), 1)

        def sb_values(h, u):
            pe.wait_ge(sem("sb_a"), h + 1)
            pe.wait_ge(sem("sb_out"), h)
            pe.matmul(aux[3][:, 0:S], st_sb[:, u, 2, 0, :], lb[:, 0:S], start=True, stop=False)
            pe.matmul(aux[3][:, P:S], st_sb[:, u, 2, 1, :], lb[:, S:S + P], start=False, stop=True).then_inc(sem("sb_o"), 1)

        def sb_hooks(it):
            def run(idx):
                for off, step in ((0, sb_turn), (2, sb_scores), (5, sb_suffix), (7, sb_values)):
                    if idx % 8 == off:
                        step(2 * it + idx // 8, idx // 8)
            return run
        pe.wait_ge(sem("kix_made"), 1)
        pe.wait_ge(sem("mod_made"), 1)
        def b_body(it):
            for k in range(2):
                group(it, "B", 16, 2, 8 * k, k, 8, sb_hooks(it))
        with pe.Fori(0, 3) as it:
            b_body(it)
        b_body(3)
        pe.wait_ge(sem("sb_out"), NH)

        def ix_turn(p, u):
            pe.wait_ge(sem("ix_staged"), p + 1)
            for tb in range(TB):
                m = pe.transpose(aux[0][:, tb * P:(tb + 1) * P], st_ix[:, u % 2, tb, :], ident)
            m.then_inc(sem("ix_T"), 1)

        def ix_scores(p, u):
            pe.wait_ge(sem("ix_q"), p + 1)
            pe.wait_ge(sem("ix_relu"), 2 * p)
            for e in range(2):
                r = slice(e * DIX, (e + 1) * DIX)
                pe.matmul(aux[1 + e][:, 0:P], q_ixT[r, 0:P], k_ixT[r, 0:P], start=True, stop=True)
                m = pe.matmul(aux[1 + e][:, P:3 * P], q_ixT[r, P:S], k_ixT[r, :], start=True, stop=True)
            m.then_inc(sem("ix_z"), 1)

        def ix_hooks(it):
            def run(idx):
                if idx % 4 == 0:
                    ix_turn(4 * it + idx // 4, idx // 4)
                if idx % 4 == 2:
                    ix_scores(4 * it + idx // 4, idx // 4)
            return run
        with pe.Fori(0, 2) as it:
            for k in range(2):
                group(it, "C1", 16, 2, 8 * k, k, 8, ix_hooks(it))
        ada_columns(1)

        def ds_turn(h, u):
            pe.wait_ge(sem("ds_qk_staged"), h + 1)
            for w in range(2):
                for tb in range(TB):
                    m = pe.transpose(aux[0][:, w * S + tb * P:w * S + (tb + 1) * P], st_qk[:, u % 2, w, tb, :], ident)
            m.then_inc(sem("ds_T"), 1)

        def ds_logits(h, u):
            pe.wait_ge(sem("ds_k"), h + 1)
            pe.wait_ge(sem("ds_lg"), h)
            pe.matmul(aux[1][:, 0:P], qk_ds[:, 0:P], qk_ds[:, S:S + P], start=True, stop=False)
            pe.matmul(aux[1][:, 0:P], flip, hank0[:, ds(h, 1), :].rearrange("p a s -> p (a s)"), start=False, stop=True)
            pe.matmul(aux[1][:, P:3 * P], qk_ds[:, P:S], qk_ds[:, S:2 * S], start=True, stop=False)
            pe.matmul(aux[1][:, P:3 * P], flip, hank1[:, ds(h, 1), :].rearrange("p a s -> p (a s)"), start=False, stop=True).then_inc(sem("ds_L"), 1)

        def ds_probs(h, u):
            pe.wait_ge(sem("ds_p"), h + 1)
            for j in range(3):
                m = pe.transpose(aux[2][:, j * P:(j + 1) * P], lg[:, u % 2, j * P:(j + 1) * P], ident)
            m.then_inc(sem("ds_PT"), 1)

        def ds_values(h, u):
            pe.wait_ge(sem("ds_pt"), h + 1)
            pe.wait_ge(sem("ds_v_staged"), h + 1)
            pe.wait_ge(sem("ds_out"), h)
            pe.matmul(aux[3][:, 0:S], st_v[:, u % 2, 0, :], PT[:, 0:S], start=True, stop=False)
            pe.matmul(aux[3][:, P:S], st_v[:, u % 2, 1, :], PT[:, S:3 * P], start=False, stop=True).then_inc(sem("ds_o"), 1)

        def ds_hooks(it):
            def run(idx):
                for step, offs in ((ds_values, DS_O), (ds_probs, DS_P), (ds_logits, DS_L), (ds_turn, DS_T)):
                    if idx in offs:
                        u = offs.index(idx)
                        step(4 * it + u, u)
            return run
        pe.wait_ge(sem("mod_made"), 2)
        pe.wait_ge(sem("ix_relu"), 2 * NIX // 2)
        pe.wait_ge(sem("hank_in"), 2 * NH * 16)
        with pe.Fori(0, 2) as it:
            for k in range(2):
                group(it, "C2", 16, 2, 8 * k, k, 8, ds_hooks(it))

        for gi in range(4):
            group(0, "O", 16, 4, 4 * gi, gi, 4, none, kt0=8 * (gi % 2), parts=2 * gi if gi < 2 else None)
        for gi in range(4):
            group(1, "O", 16, 4, 4 * gi, gi, 4, none, kt0=8 * (gi % 2))
        pe.wait_ge(sem("ds_out"), NH)
        pe.wait_ge(sem("merge_done"), 1)
        first_features(merged)
        for g in range(4):
            group(g // 2, "U", 16, 2, 8 * (g % 2), g % 2, 8, none, lead=None if g else merged)
            if g == 0:
                pe.wait_ge(sem("tt_free"), pairs[0])
                ada_rows(2)

        def ffn(n):
            name = f"F{n + 1}"
            base = n * FB

            def turn_up(j):
                g = G0[name + "p"] + 6 * j + 4
                pe.wait_ge(free0 if n == 0 else sem("up_mul"), g if n == 0 else j + 1)
                pe.wait_ge(free1, g)
                pe.wait_ge(sem("hid_made"), base + j)
                src = ubuf
                for f in range(4):
                    for tb in range(TB):
                        m = pe.transpose(aux[f // 2][:, f % 2 * S + tb * P:f % 2 * S + (tb + 1) * P],
                                         src[:, tb, f * P:(f + 1) * P], ident)
                m.then_inc(sem("up_T"), 1)

            def turn_gate(j):
                g = G0[name + "p"] + (3 if isinstance(j, int) else 6 * j - 1)
                pe.wait_ge(free0, g)
                pe.wait_ge(free1, g)
                pe.wait_ge(sem("gpad_made"), j)
                for f in range(4):
                    for tb in range(TB):
                        m = pe.transpose(aux[2 + f // 2][:, f % 2 * S + tb * P:f % 2 * S + (tb + 1) * P],
                                         gbuf[:, tb, f * P:(f + 1) * P], ident)
                m.then_inc(sem("gate_T"), 1)

            def hooks(j, at_gate, at_up):
                def run(idx):
                    if idx == at_up:
                        turn_up(j - 1)
                    if idx == at_gate and n == 0:
                        turn_gate(j)
                return run

            def down(it, phase, per, gper, idx0, gi, j, run):
                pe.wait_ge(sem("hid_made"), base + j + 1)
                for c in range(4):
                    group(it, phase, per, gper, idx0 + 2 * c, gi + c, 2, run, 0, hid_hi, hid_lo)

            run = hooks(0, 9, -1)
            group(0, name + "p", 16, 2, 0, 0, 8, run, lead=xs)
            group(0, name + "p", 16, 2, 8, 1, 8, run)
            with pe.Fori(0, FB - 1) as it:
                run = hooks(it + 1, 9, 1)
                group(it, name, 24, 6, 0, 0, 8, run)
                down(it, name, 24, 6, 8, 1, it, run)
                group(it, name, 24, 6, 16, 5, 8, run)
            turn_up(FB - 1)

            def rows_now(idx):
                if idx == 1 and n == 0:
                    pe.wait_ge(sem("gpad_made"), FB)
                    ada_rows(3)
            down(0, name + "e", 8, 4, 0, 0, FB - 1, rows_now)

        pe.wait_ge(sem("gt_made"), 1)
        pe.wait_ge(sem("xs_made"), 4)
        first_features(xs)
        ffn(0)
        pe.wait_ge(sem("gt_made"), 2)

        pe.wait_ge(sem("xs_made"), 6)
        first_features(xs)

        def project_ranks():
            pe.wait_ge(sem("alr_split"), 1)
            for kt in range(KT):
                o, w = aux[0][0:GR, 0:S], slice(kt * GR, (kt + 1) * GR)
                pe.matmul(o, alr_hi[:, w], hi[:, kt, :], start=kt == 0, stop=False)
                pe.matmul(o, alr_hi[:, w], lo[:, kt, :], start=False, stop=False)
                m = pe.matmul(o, alr_lo[:, w], hi[:, kt, :], start=False, stop=kt == KT - 1)
            m.then_inc(sem("alr_done"), 1)

        def gq_hooks(it):
            def run(idx):
                if idx in (5, 13):
                    turn_block(2 * it + idx // 8 - 1)
            return run

        def turn_block(b):
            pe.wait_ge(free0, G0["GQ"] + b + 3)
            pe.wait_ge(free1, G0["GQ"] + b + 3)
            pe.wait_ge(sem("gq_turned"), b)
            for f in range(4):
                for tb in range(TB):
                    m = pe.transpose(aux[2 + f // 2][:, f % 2 * S + tb * P:f % 2 * S + (tb + 1) * P],
                                     gstage[:, tb, f * P:(f + 1) * P], ident)
            m.then_inc(sem("gq_T"), 1)

        group(0, "GQ", 16, 2, 0, 0, 8, none, lead=xs)
        project_ranks()
        group(0, "GQ", 16, 2, 8, 1, 8, lambda idx: turn_block(0) if idx == 13 else None)
        for k in range(2):
            group(1, "GQ", 16, 2, 8 * k, k, 8, gq_hooks(1))
        pe.wait_ge(sem("alrT_made"), 1)
        pe.wait_ge(sem("gla_in"), 32)
        for f in range(8):
            if f >= 2:
                pe.wait_ge(sem("gu_made"), f - 1)
            pe.matmul(aux[f % 2][:, 0:S], wa2[:, f * P:(f + 1) * P], alrT[:], start=True, stop=True).then_inc(sem("gu_T"), 1)
        for k in range(2):
            group(0, "GV", 16, 2, 8 * k, k, 8, lambda idx: turn_block(3) if idx == 5 else None)
        group(1, "GV", 16, 2, 0, 0, 8, none)
        group(1, "GV", 16, 2, 8, 1, 8, none)
        with pe.Fori(0, 2) as it:
            for k in range(2):
                group(it, "GR", 16, 2, 8 * k, k, 8, none)

        pe.wait_ge(sem("gb_made"), 1)
        pe.wait_ge(sem("gq_turned"), 4)
        pe.wait_ge(free0, 2 + G0["GO"])
        pe.wait_ge(free1, 2 + G0["GO"])

        def level(h, lv):
            n = 7 * h + lv
            if lv:
                pe.wait_ge(sem("gl_m"), 7 * h + GL_ITEMS.index(lv) + 1)
            if n >= 2:
                pe.wait_ge(sem("gl_picked"), n - 1)
            j = (6 * h + lv - 1) % 3
            l, r = (gla_k(h), gla_q(h)) if lv == 0 else (gm[:, j, :], gm[:, j, :])
            for tb in range(TB):
                for e in range(2):
                    c = slice(e * S + tb * P, e * S + (tb + 1) * P)
                    m = pe.matmul(aux[n % 2][:, tb * P:(tb + 1) * P], l[:, c], r[:, c], start=e == 0, stop=e == 1)
            m.then_inc(sem("gl_z"), 1)

        def turn_keys(h):
            pe.wait_ge(sem("gk_dec"), h + 1)
            if h:
                pe.wait_ge(sem("go_held"), 2 * h)
            for tb in range(TB):
                for e in range(2):
                    m = pe.transpose(aux[2][:, (2 * tb + e) * P:(2 * tb + e + 1) * P], gkd[:, h % 2, e * S + tb * P:e * S + (tb + 1) * P], ident)
            m.then_inc(sem("gk_T"), 1)

        def state(h, n):
            c, e, i = n // 2, n % 2, 6 * h + n
            pe.wait_ge(sem("gk_turned"), h + 1)
            if i >= 4:
                pe.wait_ge(sem("gs_added"), i - 3)
            r = slice(c % 2 * GC, (c % 2 + 1) * GC)
            pe.matmul(lin[i % 4 // 2][i % 2][:], gkdT[r, c // 2, e * P:(e + 1) * P], gla_v(h, c // 2)[r, :], start=True, stop=True).then_inc(sem("gs_T"), 1)

        def values(h, tb):
            pe.wait_ge(sem("gl_picked"), 7 * h + 7)
            pe.wait_ge(sem("gq_made"), h + 1)
            pe.wait_ge(sem("gs_added"), 6 * h + (2 if tb == 0 else 6))
            if tb == 0 and h:
                pe.wait_ge(sem("go_held"), 2 * h - 1)
            o = aux[3 - tb][:]
            pe.matmul(o, gsc[:, h % 2, tb * P:(tb + 1) * P], gla_v(h, tb), start=True, stop=False)
            cs = (0,) if tb == 0 else (1, 2)
            for c in cs:
                for e in range(2):
                    m = pe.matmul(o, gq[:, h % 2, c, e, :], sts[:, c, e, :], start=False, stop=c == cs[-1] and e == 1)
            m.then_inc(sem("go_T"), 1)

        for h in range(GH + 1):
            for lv in range(7):
                if h < GH:
                    level(h, lv)
                if h:
                    for step, n in {0: [(turn_keys, None)], 1: [(state, 0), (state, 1)], 2: [(state, 2), (state, 3)],
                                    3: [(state, 4), (state, 5)], 4: [(values, 0)], 5: [(values, 1)]}.get(lv, ()):
                        step(h - 1) if n is None else step(h - 1, n)
        for g in range(KT // 4):
            turn(gv, g, (sem("go_done"), g // 2 + 1))
        pe.wait_ge(sem("go_done"), GH)
        for g in range(4):
            group(g // 2, "GO", 16, 2, 8 * (g % 2), g % 2, 8, none, lead=None if g else gv)
        pe.wait_ge(sem("xs_made"), 8)
        first_features(xs)
        ffn(1)

    @block.scalar
    def _(act):
        pairs, affine, squared = [0], [0], [0]

        def split(it, phase, per, idx):
            act.wait_ge(slab_in[idx // 2 % RING], 2 * (H0[phase] + it * per) + 16 * (idx // 8 + 1))
            if not (phase == "A" and idx < RING):
                act.wait_ge(half_used, H0[phase] + it * per + idx - RING + 1)
            act.activation(whi[:, idx % RING * HALF:(idx % RING + 1) * HALF],
                           raw[:, idx // 2 % RING, idx % 2 * HALF:(idx % 2 + 1) * HALF], ACT.Copy).then_inc(hi_made, 1)

        def body(it, phase, per, hooks, upto=None, start=RING):
            for idx in range(start, per + RING if upto is None else upto):
                split(it, phase, per, idx)
                for step in hooks.get(idx, ()):
                    step()

        def drain(it, phase, gper, gi, upto, dst, **how):
            per = dict((p[0], p[2]) for p in PHASES)[phase]
            act.wait_ge(half_used, H0[phase] + it * per + upto)
            act.activation(dst, lin[gi % 2][0][:], ACT.Copy, **how).then_inc(free0, 1)

        def squares(src, dst, combined=0):
            if combined:
                act.activation(small[:, 160:161], ones[:, 0:1], ACT.Sqrt).then_inc(sem("warm"), 1)
            for tb in (1, 0):
                if combined:
                    act.wait_ge(sem(f"xcomb{tb}"), combined)
                if squared[0]:
                    act.wait_ge(sem("ss_made"), squared[0])
                act.activation(junk[:], src[:, tb, :], ACT.Square, accum_out=dst[:, tb:tb + 1]).then_inc(sem("ss_made"), 1)
                squared[0] += 1

        def norm_stats(n, combined=0):
            squares(X, ss, combined)
            act.wait_ge(sem("ms_made"), n + 1)
            act.activation(rstd, ss, ACT.Sqrt).then_inc(sem("sd_made"), 1)

        def norm_rows(n, dst):
            act.wait_ge(sem("rstd_made"), n + 1)
            act.activation(dst[:, 0, :], X[:, 0, :], ACT.Copy, scale=rstd[:, 0:1]).then_inc(sem("xs_made"), 1)

        def features(phase, plain, scale=None, shift=None):
            for g in range(KT // 2):
                n = pairs[0]
                act.wait_ge(sem("tt_T"), n + 1)
                if plain:
                    act.activation(hi[:, 2 * g:2 * g + 2, :].rearrange("p k t -> p (k t)"), aux[n % 4][:], ACT.Copy).then_inc(sem("tt_hi"), 1)
                else:
                    if affine[0] >= 2:
                        act.wait_ge(sem("tt_lo"), n - 1)
                    for q in range(2):
                        kt = 2 * g + q
                        m = act.activation(aff[:, n % 2, q * S:(q + 1) * S], aux[n % 4][:, q * S:(q + 1) * S], ACT.Identity,
                                           scale=scale[:, kt:kt + 1], bias=0.0 if shift is None else shift[:, kt:kt + 1])
                    m.then_inc(sem("tt_aff"), 1)
                    affine[0] += 1
                pairs[0] += 1
                if g >= RING:
                    split(0, phase, 16, g)

        act.wait_ge(sem("par_cols"), 1)
        act.activation(csg, c_col, ACT.Sigmoid).then_inc(sem("csg_made"), 1)
        act.wait_ge(sem("x_in"), 16)
        norm_stats(0)
        norm_rows(0, X)
        act.wait_ge(sem("gs_made"), 1)
        act.nop().then_inc(free0, 1)
        act.wait_ge(free0, 1)
        act.nop().then_inc(free0, 1)
        for idx in range(RING):
            split(0, "A", 16, idx)
        features("A", False, gs_mix, sh_mix)

        def drains2(it, phase, dst, extra=None, second=19):
            hooks = dict(extra or {})
            for k, idx in ((0, 11), (1, second)):
                hooks[idx] = list(hooks.get(idx, [])) + [lambda k=k: drain(it, phase, 2, k, 8 * (k + 1), dst(k))]
            return hooks

        cols = lambda it, k: ds(it * 2 * NB + k * NB, NB)

        def split_ix():
            act.wait_ge(sem("ixw_in"), 16)
            act.activation(ixw_hi[:], ixw_raw[:], ACT.Copy).then_inc(sem("ixw_hi"), 1)

        def hold_ix():
            act.wait_ge(sem("ixw_done"), 1)
            act.activation(ixw[:, 0, :], aux[1][:, 0:NIXW], ACT.Copy).then_inc(sem("ixw_held"), 1)
        body(0, "A", 16, drains2(0, "A", lambda k: sbz[:, 0, k * NB:(k + 1) * NB], {9: [split_ix]}), start=8)
        with act.Fori(1, 3) as it:
            body(it, "A", 16, drains2(it, "A", lambda k: sbz[:, 0, cols(it, k)]))
        hold_ix()
        act.wait_ge(sem("kix_T"), 1)
        act.activation(k_ixT[:], aux[0][:, 0:S], ACT.Copy).then_inc(sem("kix_made"), 1)

        def sb_act(it):
            def hold_qk(u):
                h = 2 * it + u
                act.wait_ge(sem("sb_T"), h + 1)
                act.activation(qk_sb[:], aux[0][:], ACT.Copy).then_inc(sem("sb_qk"), 1)

            def softplus(u):
                h = 2 * it + u
                act.wait_ge(sem("sb_az"), h + 1)
                act.activation(az[:], az[:], ACT.Exp, scale=HD ** -0.5).then_inc(sem("sb_e"), 1)
                act.wait_ge(sem("sb_e"), h + 1)
                act.activation(az[:], az[:], ACT.Ln, bias=1.0).then_inc(sem("sb_L"), 1)

            def weights(u):
                h = 2 * it + u
                act.wait_ge(sem("sb_sm"), h + 1)
                act.activation(lb[:], lb[:], ACT.Exp).then_inc(sem("sb_ex"), 1)

            def hold_out(u):
                h = 2 * it + u
                act.wait_ge(sem("sb_o"), h + 1)
                act.activation(oT_sb[:, ds(h, 1), :].rearrange("p a t -> p (a t)"), aux[3][:, 0:S], ACT.Copy).then_inc(sem("sb_out"), 1)
            hooks = {}
            for u in range(2):
                for off, step in ((4, hold_qk), (6, softplus), (9, weights), (11, hold_out)):
                    hooks.setdefault(8 * u + off, []).append(lambda u=u, step=step: step(u))
            return hooks

        with act.Fori(0, 3) as it:
            body(it, "B", 16, drains2(it, "B", lambda k: dsz[:, 0, cols(it, k)], sb_act(it)))
        body(3, "B", 16, drains2(3, "B", lambda k: qix[:, 0, k * NB:(k + 1) * NB], sb_act(3)))

        def ix_act(it):
            def hold_q(u):
                p = 4 * it + u
                act.wait_ge(sem("ix_T"), p + 1)
                act.activation(q_ixT[:], aux[0][:, 0:S], ACT.Copy).then_inc(sem("ix_q"), 1)

            def relu(u):
                p = 4 * it + u
                act.wait_ge(sem("ix_z"), p + 1)
                act.wait_ge(sem("ix_sum"), 2 * p)
                for e in range(2):
                    act.activation(r_ix[:, e, :], aux[1 + e][:, 0:3 * P], ACT.Relu, scale=DIX ** -0.5).then_inc(sem("ix_relu"), 1)
            hooks = {}
            for u in range(4):
                hooks.setdefault(4 * u + 4, []).append(lambda u=u: hold_q(u))
                hooks.setdefault(4 * u + 6, []).append(lambda u=u: relu(u))
            return hooks
        with act.Fori(0, 2) as it:
            body(it, "C1", 16, drains2(it, "C1", lambda k: gate_sb[:, 0, cols(it, k)], ix_act(it)))

        def ds_act(it):
            def hold_q(u):
                h = 4 * it + u
                act.wait_ge(sem("ds_T"), h + 1)
                act.activation(qk_ds[:, 0:S], aux[0][:, 0:S], ACT.Copy, scale=HD ** -0.5).then_inc(sem("ds_q"), 1)

            def soft(u):
                h = 4 * it + u
                act.wait_ge(sem("ds_mx"), h + 1)
                for tb, c in ((0, slice(0, P)), (1, slice(P, 3 * P))):
                    n = 2 * (u % 2) + tb
                    m = act.activation(lg[:, u % 2, c], lg[:, u % 2, c], ACT.Exp, bias=nmax[:, n:n + 1], accum_out=ssum[:, n:n + 1])
                    m.then_inc(sem("ds_ex"), 1)

            def hold_p(u):
                h = 4 * it + u
                act.wait_ge(sem("ds_PT"), h + 1)
                act.activation(PT[:], aux[2][:, 0:3 * P], ACT.Copy).then_inc(sem("ds_pt"), 1)

            def hold_out(u):
                h = 4 * it + u
                act.wait_ge(sem("ds_o"), h + 1)
                act.activation(oT_ds[:, ds(h, 1), :].rearrange("p a t -> p (a t)"), aux[3][:, 0:S], ACT.Copy).then_inc(sem("ds_out"), 1)
            hooks = {}
            for offs, step in ((DS_O, hold_out), (DS_P, hold_p), (DS_L, soft), (DS_T, hold_q)):
                for u in range(4):
                    hooks.setdefault(offs[u] + AHEAD, []).append(lambda u=u, step=step: step(u))
            return hooks
        act.wait_ge(sem("tk_in"), 1)
        with act.Fori(0, 2) as it:
            body(it, "C2", 16, drains2(it, "C2", lambda k: gate_ds[:, 0, cols(it, k)], ds_act(it)))

        act.wait_ge(half_used, H0["O"])
        for n in range(4):
            if n == 3:
                act.wait_ge(sem("ds_out"), NH)
            src = (oT_sb, oT_ds)[n // 2][:, n % 2 * 4:n % 2 * 4 + 4, :]
            act.activation(hi[:, 4 * n:4 * n + 4, :], src, ACT.Copy).then_inc(sem("oT_hi"), 1)

        def o_hooks(it):
            hooks = {}

            def gate(gi):
                g = (gate_sb, gate_ds)[gi % 2][:, :, cols(it, gi // 2)]
                act.activation(g, g, ACT.Sigmoid).then_inc(sem("og_sig"), 1)

            for gi in range(4):
                hooks.setdefault(4 * gi + 5, []).append(lambda gi=gi: gate(gi))
            return hooks
        act.wait_ge(free0, G0["O"] + 2)
        act.wait_ge(free1, G0["O"] + 2)
        with act.Fori(0, 2) as it:
            body(it, "O", 16, o_hooks(it))
        act.wait_ge(half_used, H0["U"])
        features("U", True)
        for it in range(2):
            body(it, "U", 16, drains2(it, "U", lambda k: y1[:, 0, (2 * it + k) * NB:(2 * it + k + 1) * NB], second=19 - it), start=4 if it else 8)

        def ffn(n):
            name = f"F{n + 1}"
            base = n * FB

            def hid_high(j):
                if n == 0:
                    act.wait_ge(sem("hidf_made"), j + 1)
                    act.activation(hid_hi[:], hidf[:], ACT.Copy).then_inc(sem("hid_h"), 1)
                else:
                    act.wait_ge(sem("up_T"), base + j + 1)
                    for e in range(2):
                        act.activation(hid_hi[:, 2 * e:2 * e + 2, :].rearrange("p k t -> p (k t)"), aux[e][:], ACT.Copy).then_inc(sem("hid_h"), 1)

            def gate_pad(j):
                act.wait_ge(sem("gate_T"), j + 1)
                for e in range(2):
                    m = act.activation(gpad[:, 2 * e:2 * e + 2, 2:], aux[2 + e][:].rearrange("p (k t) -> p k t", k=2), ACT.Copy)
                m.then_inc(sem("gpad_made"), 1)

            def sigmoid(j):
                if n == 0:
                    act.wait_ge(sem("conv_made"), 6 * j + 6)
                    act.activation(csig[:], cacc[:], ACT.Sigmoid).then_inc(sem("csig_made"), 1)
                else:
                    g = G0[name + "p"] + (3 if isinstance(j, int) else 6 * j - 1)
                    act.wait_ge(free0, g)
                    act.wait_ge(free1, g)
                    act.activation(csig[:].rearrange("p a t -> p (a t)"), gbuf[:].rearrange("p a t -> p (a t)"), ACT.Sigmoid).then_inc(sem("csig_made"), 1)

            def down(it, phase, gper, gi, c, upto):
                k = (0 if phase == name else 4 * (FB - 1)) + (4 * it + c)
                act.wait_ge(sem("dstage_free"), n * 4 * FB + k + 1)
                drain(it, phase, gper, gi, upto, dstage[:, c % 2, :])

            def hooks(it, phase, gper, j, ups):
                hk = {}
                add = lambda idx, f: hk.setdefault(idx, []).append(f)
                add(11, lambda: drain(it, phase, gper, 0, 8, gbuf[:, 0, :]))
                if n == 0:
                    add(13, lambda: gate_pad(j))
                add(18 if n == 0 else 12, lambda: sigmoid(j))
                if phase == name:
                    add(5, lambda: hid_high(it))
                    for c in range(4):
                        add(13 + 2 * c, lambda c=c: down(it, phase, gper, 1 + c, c, 10 + 2 * c))
                up = 1 if phase != name else 5
                add(ups, lambda: drain(it, phase, gper, up, ups - AHEAD + 1, ubuf[:, 0, :]))
                return hk
            body(0, name + "p", 16, hooks(0, name + "p", 2, 0, 19), start=8)
            with act.Fori(0, FB - 1) as it:
                body(it, name, 24, hooks(it, name, 6, it + 1, 27))
            hid_high(FB - 1)
            hk = {5 + 2 * c - (c == 3 and n == 0): [lambda c=c: down(0, name + "e", 4, c, c, 2 * c + 2)] for c in range(4)}
            if n == 0:
                body(0, name + "e", 8, hk)
            else:
                for idx in range(4, 8):
                    split(0, name + "e", 8, idx)
                    for step in hk.get(idx, ()):
                        step()
                for idx in (9, 11):
                    hk[idx][0]()

        norm_stats(1, 1)
        norm_rows(1, xs)
        features("F1p", False, gs_ffn, sh_ffn)
        ffn(0)

        squares(X, ss, 2)
        act.wait_ge(sem("xy_made"), 2)
        squares(xs, ssy)
        act.wait_ge(sem("ms_made"), 3)
        act.activation(small[:, 116:120], small[:, 112:116], ACT.Sqrt).then_inc(sem("sd_made"), 1)
        act.wait_ge(sem("rstd_made"), 3)
        act.activation(xs[:, 0, :], xs[:, 0, :], ACT.Copy, scale=ry[:, 0:1]).then_inc(sem("xs_made"), 1)
        act.wait_ge(sem("late_in"), 48)
        act.activation(alr_hi[:], alr_raw[:], ACT.Copy).then_inc(sem("alr_hi_made"), 1)
        features("GQ", False, g_n0)

        def hold_ranks():
            act.wait_ge(sem("alr_done"), 1)
            act.activation(alrT[:], aux[0][0:GR, 0:S], ACT.Copy).then_inc(sem("alrT_made"), 1)

        def turned(b):
            scale = GK ** -0.5 if b < 2 else 1.0
            act.wait_ge(sem("gq_T"), b + 1)
            for e in range(2):
                m = act.activation(gqk[:, 4 * b + 2 * e:4 * b + 2 * e + 2, :].rearrange("p k t -> p (k t)"), aux[2 + e][:], ACT.Copy, scale=scale)
            m.then_inc(sem("gq_turned"), 1)

        def gq_drain(b):
            if b:
                act.wait_ge(sem("gq_T"), b)
            drain(b // 2, "GQ", 2, b % 2, 8 * (b % 2 + 1), gstage[:, 0, :])
        body(0, "GQ", 16, {11: [lambda: gq_drain(0)], 13: [hold_ranks], 17: [lambda: turned(0)], 19: [lambda: gq_drain(1)]}, start=8)
        body(1, "GQ", 16, {9: [lambda: turned(1)], 11: [lambda: gq_drain(2)], 17: [lambda: turned(2)], 19: [lambda: gq_drain(3)]})
        gvd = lambda it: drains2(it, "GV", lambda k: gv[:, 0, cols(it, k)])
        hk = gvd(0)
        hk.setdefault(9, []).append(lambda: turned(3))
        body(0, "GV", 16, hk)
        act.wait_ge(sem("gabs"), 1)
        act.activation(gt1[:], gt1[:], ACT.Exp).then_inc(sem("gexp"), 1)
        act.wait_ge(sem("gexp"), 1)
        act.activation(gt1[:], gt1[:], ACT.Ln, bias=1.0).then_inc(sem("gln"), 1)
        body(1, "GV", 16, gvd(1))

        def gate(it, k):
            act.wait_ge(free0, 2 + G0["GR"] + 2 * it + k + 1)
            act.wait_ge(free1, 2 + G0["GR"] + 2 * it + k + 1)
            act.wait_ge(sem("gr_gated"), 2 * it + k)
            act.activation(gsig[:], gr[:, :, cols(it, k)], ACT.Sigmoid).then_inc(sem("gsig_made"), 1)

        def gr_body(it):
            hooks = drains2(it, "GR", lambda k: gr[:, 0, cols(it, k)])
            hooks[13] = [lambda: gate(it, 0)]
            hooks[19].append(lambda: gate(it, 1))
            body(it, "GR", 16, hooks)
        act.wait_ge(sem("gb_made"), 1)
        for it in range(2):
            gr_body(it)
        def decays(h, i):
            n = 7 * h + i
            act.wait_ge(sem("gl_d"), n + 1)
            act.activation(ge[:, n % 4, :], ge[:, n % 4, :], ACT.Exp).then_inc(sem("gl_e"), 1)
            if GL_ITEMS[i] == 0:
                if h >= 2:
                    act.wait_ge(sem("gs_added"), 6 * (h - 1))
                act.activation(geb[:, h % 2, :], gla_sums(h), ACT.Exp).then_inc(sem("geb_made"), 1)

        for h in range(GH + 1):
            for i in range(7):
                if h < GH:
                    decays(h, i)
                if i == 1 and h:
                    act.wait_ge(sem("gk_T"), h)
                    act.activation(gkdT[:].rearrange("p a t -> p (a t)"), aux[2][:], ACT.Copy).then_inc(sem("gk_turned"), 1)
            for tb in range(TB if h else 0):
                act.wait_ge(sem("go_T"), 2 * (h - 1) + tb + 1)
                n = 2 * (h - 1) + tb
                if n:
                    act.wait_ge(sem("go_held"), n)
                act.activation(gjunk[:], aux[3 - tb][:], ACT.Square, accum_out=gss[:, tb * GH + h - 1:tb * GH + h]).then_inc(sem("gss_made"), 1)
                act.activation(gla_v(h - 1, tb), aux[3 - tb][:], ACT.Copy).then_inc(sem("go_held"), 1)
        act.wait_ge(sem("gms_made"), 1)
        act.activation(grs, gss[:], ACT.Sqrt).then_inc(sem("gsd_made"), 1)
        act.wait_ge(half_used, H0["GO"])
        features("GO", True)
        for it in range(2):
            body(it, "GO", 16, drains2(it, "GO", lambda k: y1[:, 0, (2 * it + k) * NB:(2 * it + k + 1) * NB], second=19 - it), start=4 if it else 8)
        norm_stats(3, 3)
        norm_rows(3, xs)
        features("F2p", False, g_n1)
        ffn(1)

    @block.vector
    def _(dve):
        pairs, affine, links = [0], [0], [0]

        def link(op):
            links[0] += 1
            op.then_inc(sem("dve_link"), 1)
            dve.wait_ge(sem("dve_link"), links[0])

        def split(it, phase, per, idx):
            dve.wait_ge(hi_made, H0[phase] + it * per + idx + 1)
            c = slice(idx % RING * HALF, (idx % RING + 1) * HALF)
            dve.tensor_tensor(wlo[:, c], raw[:, idx // 2 % RING, idx % 2 * HALF:(idx % 2 + 1) * HALF],
                              whi[:, c].bitcast(fp32), ALU.subtract).then_inc(lo_made, 1)

        def body(it, phase, per, hooks, upto=None, start=RING):
            for idx in range(start, per + RING if upto is None else upto):
                split(it, phase, per, idx)
                for step in hooks.get(idx, ()):
                    step()

        pers = dict((p[0], p[2]) for p in PHASES)

        def drained(it, phase, upto):
            dve.wait_ge(half_used, H0[phase] + it * pers[phase] + upto)

        def drain(it, phase, gi, upto, dst):
            drained(it, phase, upto)
            dve.tensor_copy(dst, lin[gi % 2][1][:]).then_inc(free1, 1)

        def norm_stats(n):
            dve.wait_ge(sem("ss_made"), 2 * (n + 1) if n < 2 else 10)
            dve.tensor_scalar(ss, ss, 1.0 / D, EPS, ALU.mult, ALU.add).then_inc(sem("ms_made"), 1)
            dve.wait_ge(sem("sd_made"), n + 1)
            dve.reciprocal(rstd, rstd).then_inc(sem("rstd_made"), 1)
            dve.wait_ge(sem("rstd_made"), n + 1)

        def norm_rows(dst):
            dve.tensor_scalar(dst[:, 1, :], X[:, 1, :], rstd[:, 1:2], None, ALU.mult).then_inc(sem("xs_made"), 1)

        def features(phase, plain):
            for g in range(KT // 2):
                n = pairs[0]
                h = hi[:, 2 * g:2 * g + 2, :].rearrange("p k t -> p (k t)")
                if plain:
                    src = aux[n % 4][:]
                else:
                    dve.wait_ge(sem("tt_aff"), affine[0] + 1)
                    dve.nop().then_inc(sem("tt_free"), 1)
                    src = aff[:, n % 2, :]
                    affine[0] += 1
                    dve.tensor_copy(h, src).then_inc(sem("tt_hi"), 1)
                dve.wait_ge(sem("tt_hi"), n + 1)
                dve.tensor_tensor(lo[:, 2 * g:2 * g + 2, :].rearrange("p k t -> p (k t)"), src, h.bitcast(fp32), ALU.subtract).then_inc(sem("tt_lo"), 1)
                if plain:
                    dve.wait_ge(sem("tt_lo"), n + 1)
                    dve.nop().then_inc(sem("tt_free"), 1)
                pairs[0] += 1
                if g >= RING:
                    split(0, phase, 16, g)

        link(dve.memset(acc0[:], 0.0))
        dve.wait_ge(sem("par_T"), 1)
        dve.tensor_copy(par2[:], aux[1][:, 0:120])
        dve.tensor_copy(par3[:], aux[2][:, 0:96])
        dve.tensor_copy(par1[:], aux[0][:, 0:112]).then_inc(sem("par_cols"), 1)
        dve.wait_ge(sem("par_cols"), 1)
        dve.wait_ge(sem("csg_made"), 1)
        dve.tensor_tensor(cact, c_col, csg, ALU.mult).then_inc(sem("cact_made"), 1)
        dve.wait_ge(sem("cact_made"), 1)
        norm_stats(0)
        norm_rows(X)
        with dve.Fori(0, KT // 4) as it:
            for u in range(4):
                dve.wait_ge(sem(f"ada0_in{u}"), 16 * it + 16)
                dve.wait_ge(sem("ada0_sum"), 4 * it + u)
                dve.scalar_tensor_tensor(acc0[:], ada0[:, u, :], cact[:, ds(4 * it + u, 1)], acc0[:], ALU.mult, ALU.add).then_inc(sem("ada0_sum"), 1)
        dve.wait_ge(sem("ada0_T"), 1)
        link(dve.tensor_tensor(sh_mix, aux[0][:, 0:KT], b_sh1, ALU.add))
        link(dve.tensor_tensor(gs_mix, aux[0][:, KT:2 * KT], b_sc1, ALU.add))
        dve.scalar_tensor_tensor(gs_mix, gs_mix, 1.0, g_mix, ALU.add, ALU.mult).then_inc(sem("gs_made"), 1)
        dve.wait_ge(sem("erow_T"), 1)
        dve.tensor_copy(erow[:], aux[3][0:NH, :]).then_inc(sem("erow_held"), 1)
        dve.wait_ge(sem("gs_made"), 1)
        dve.nop().then_inc(free1, 1)
        dve.wait_ge(free1, 1)
        dve.nop().then_inc(free1, 1)
        for idx in range(RING):
            split(0, "A", 16, idx)
        features("A", False)

        cols = lambda it, k: ds(it * 2 * NB + k * NB, NB)

        def drains2(it, phase, dst, extra=None):
            hooks = dict(extra or {})
            for k, idx in ((0, 11), (1, 19)):
                hooks[idx] = list(hooks.get(idx, [])) + [lambda k=k: drain(it, phase, k, 8 * (k + 1), dst(k))]
            return hooks

        def split_ix():
            dve.wait_ge(sem("ixw_hi"), 1)
            dve.tensor_tensor(ixw_lo[:], ixw_raw[:], ixw_hi[:].bitcast(fp32), ALU.subtract).then_inc(sem("ixw_split"), 1)
        body(0, "A", 16, drains2(0, "A", lambda k: sbz[:, 1, k * NB:(k + 1) * NB], {9: [split_ix]}), start=8)
        with dve.Fori(1, 3) as it:
            body(it, "A", 16, drains2(it, "A", lambda k: sbz[:, 1, cols(it, k)]))
        dve.wait_ge(sem("ixw_done"), 1)
        link(dve.tensor_copy(ixw[:, 1, :], aux[2][:, 0:NIXW]))
        dve.wait_ge(sem("ixw_held"), 1)
        dve.tensor_copy(kdup[:, :, 0:DIX], ixw[:, :, 0:DIX])
        dve.tensor_copy(kdup[:, :, DIX:P], ixw[:, :, 0:DIX]).then_inc(sem("kdup_made"), 1)
        link(dve.tensor_scalar(wix[:], ixw[:, :, DIX:NIXW], NIX ** -0.5, None, ALU.mult))
        dve.wait_ge(sem("ada_T"), 1)
        link(dve.tensor_tensor(sc_ffn, aux[3][:, 0:KT], b_sc2, ALU.add))
        link(dve.scalar_tensor_tensor(gs_ffn, sc_ffn, 1.0, g_ffn, ALU.add, ALU.mult))
        dve.nop().then_inc(sem("mod_made"), 1)

        SC = HD ** -0.5

        def sb_dve(it):
            def log_keep(u):
                h = 2 * it + u
                z = aux[1][:, 0:3 * P]
                dve.wait_ge(sem("sb_z"), h + 1)
                dve.tensor_scalar(lb[:], z, SC, 0.0, ALU.mult, ALU.min).then_inc(sem("sb_own"), 1)
                dve.wait_ge(sem("sb_own"), 3 * h + 1)
                dve.scalar_tensor_tensor(az[:], lb[:], 2.0 / SC, z, ALU.mult, ALU.subtract).then_inc(sem("sb_az"), 1)
                dve.wait_ge(sem("sb_L"), h + 1)
                dve.tensor_tensor(lb[:], lb[:], az[:], ALU.subtract).then_inc(sem("sb_own"), 1)
                dve.wait_ge(sem("sb_own"), 3 * h + 2)
                dve.scalar_tensor_tensor(lk[:], z, -SC, lb[:], ALU.mult, ALU.add).then_inc(sem("sb_own"), 1)
                dve.wait_ge(sem("sb_own"), 3 * h + 3)
                dve.tensor_tensor(lk[:], lk[:], sbmask, ALU.mult).then_inc(sem("sb_lk"), 1)

            def weights(u):
                h = 2 * it + u
                dve.wait_ge(sem("sb_suf"), h + 1)
                dve.tensor_tensor(lb[:], lb[:], aux[2][:, 0:3 * P], ALU.add).then_inc(sem("sb_sm"), 1)
                dve.wait_ge(sem("sb_ex"), h + 1)
                dve.tensor_tensor(lb[:], lb[:], sbmask, ALU.mult).then_inc(sem("sb_a"), 1)
            hooks = {}
            for u in range(2):
                hooks.setdefault(8 * u + 6, []).append(lambda u=u: log_keep(u))
                hooks.setdefault(8 * u + 9, []).append(lambda u=u: weights(u))
            return hooks
        with dve.Fori(0, 3) as it:
            body(it, "B", 16, drains2(it, "B", lambda k: dsz[:, 1, cols(it, k)], sb_dve(it)))
        body(3, "B", 16, drains2(3, "B", lambda k: qix[:, 1, k * NB:(k + 1) * NB], sb_dve(3)))

        link(dve.memset(score[:], 0.0))

        def ix_dve(it):
            def add(u):
                p = 4 * it + u
                for e in range(2):
                    dve.wait_ge(sem("ix_relu"), 2 * p + e + 1)
                    dve.wait_ge(sem("ix_sum"), 2 * p + e)
                    for tb, c in ((0, slice(0, P)), (1, slice(P, 3 * P))):
                        m = dve.scalar_tensor_tensor(score[:, c], r_ix[:, e, c], wix[:, tb, ds(2 * p + e, 1)], score[:, c], ALU.mult, ALU.add)
                    m.then_inc(sem("ix_sum"), 1)
            return {4 * u + 6: [lambda u=u: add(u)] for u in range(4)}
        with dve.Fori(0, 2) as it:
            body(it, "C1", 16, drains2(it, "C1", lambda k: gate_sb[:, 1, cols(it, k)], ix_dve(it)))
        dve.wait_ge(sem("ada_T"), 2)
        link(dve.tensor_tensor(sh_ffn, aux[3][:, 0:KT], b_sh2, ALU.add))
        dve.nop().then_inc(sem("mod_made"), 1)
        dve.wait_ge(sem("ix_sum"), NIX)
        dve.tensor_tensor(selneg[:], score[:], cneg, ALU.add).then_inc(sem("tk_in"), 1)
        dve.wait_ge(sem("tk_in"), 1)
        for r in range(TOPK // 8):
            for tb, c in ((0, slice(0, P)), (1, slice(P, 3 * P))):
                link(dve.max(top8[:], selneg[:, c]))
                link(dve.match_replace(selneg[:, c], top8[:], selneg[:, c], TAKEN))
        link(dve.tensor_scalar(selneg[:], selneg[:], TAKEN / 2, NEG, ALU.is_gt, ALU.mult))
        link(dve.tensor_tensor(selneg[:], selneg[:], cneg, ALU.add))

        def ds_dve(it):
            def hold_k(u):
                h = 4 * it + u
                dve.wait_ge(sem("ds_q"), h + 1)
                dve.tensor_copy(qk_ds[:, S:2 * S], aux[0][:, S:2 * S]).then_inc(sem("ds_k"), 1)

            def soft(u):
                h = 4 * it + u
                s = u % 2
                dve.wait_ge(sem("ds_L"), h + 1)
                dve.tensor_tensor(lg[:, s, :], aux[1][:, 0:3 * P], selneg[:], ALU.add).then_inc(sem("ds_lg"), 1)
                dve.wait_ge(sem("ds_lg"), h + 1)
                parts = ((0, slice(0, P)), (1, slice(P, 3 * P)))
                for tb, c in parts:
                    m = dve.tensor_reduce(nmax[:, 2 * s + tb:2 * s + tb + 1], lg[:, s, c], AX.X, ALU.max, negate=True)
                m.then_inc(sem("ds_mx"), 1)
                dve.wait_ge(sem("ds_ex"), 2 * h + 2)
                dve.reciprocal(ssum[:, 2 * s:2 * s + 2], ssum[:, 2 * s:2 * s + 2]).then_inc(sem("ds_rs"), 1)
                dve.wait_ge(sem("ds_rs"), h + 1)
                for tb, c in parts:
                    m = dve.tensor_scalar(lg[:, s, c], lg[:, s, c], ssum[:, 2 * s + tb:2 * s + tb + 1], None, ALU.mult)
                m.then_inc(sem("ds_p"), 1)
            hooks = {}
            for offs, step in ((DS_L, soft), (DS_T, hold_k)):
                for u in range(4):
                    hooks.setdefault(offs[u] + AHEAD, []).append(lambda u=u, step=step: step(u))
            return hooks
        with dve.Fori(0, 2) as it:
            body(it, "C2", 16, drains2(it, "C2", lambda k: gate_ds[:, 1, cols(it, k)], ds_dve(it)))

        for n in range(4):
            dve.wait_ge(sem("oT_hi"), n + 1)
            src = (oT_sb, oT_ds)[n // 2][:, n % 2 * 4:n % 2 * 4 + 4, :]
            dve.tensor_tensor(lo[:, 4 * n:4 * n + 4, :], src, hi[:, 4 * n:4 * n + 4, :].bitcast(fp32), ALU.subtract).then_inc(sem("oT_split"), 1)

        def o_hooks(it):
            def take(gi):
                c = cols(it, gi // 2)
                drained(it, "O", 4 * (gi + 1))
                dve.wait_ge(sem("og_sig"), 4 * it + gi + 1)
                n, last = gi % 2, 2 + G0["O"] + 4 * it + gi + 1
                for tb, free in ((0, free0), (1, free1)):
                    to, gated = (gate_ds if n else merged)[:, tb, c], (gate_ds if n else gate_sb)[:, tb, c]
                    dve.tensor_tensor(to, lin[n][tb][:], gated, ALU.mult).then_inc(free, 1)
                if n:
                    for tb, free in ((0, free0), (1, free1)):
                        dve.wait_ge(free, last)
                        m = dve.tensor_tensor(merged[:, tb, c], merged[:, tb, c], gate_ds[:, tb, c], ALU.add)
                    m.then_inc(sem("og_add1"), 1)
            return {4 * gi + 7: [lambda gi=gi: take(gi)] for gi in range(4)}
        with dve.Fori(0, 2) as it:
            body(it, "O", 16, o_hooks(it))
        dve.wait_ge(sem("og_add1"), 4)
        dve.nop().then_inc(sem("merge_done"), 1)

        def modulation_row(n):
            if n:
                dve.wait_ge(sem("gt_used"), 2)
            dve.wait_ge(sem("ada_T"), n + 3)
            dve.wait_ge(sem("gtb_in"), 16 * (n + 1))
            for j in range(4):
                c = slice(j * NB, (j + 1) * NB)
                m = dve.tensor_tensor(gt_row[:, c], aux[j][:], gt_bias[:, c], ALU.add)
            m.then_inc(sem("gt_made"), 1)
            dve.wait_ge(sem("gt_made"), n + 1)

        features("U", True)

        def combine(y, c, scaled, last=False):
            s = slice(c * NB, (c + 1) * NB)
            if not scaled:
                link(dve.tensor_tensor(y[:, 1, s], y[:, 1, s], gt_row[:, s], ALU.mult))
            m = dve.tensor_tensor(X[:, 1, s], X[:, 1, s], y[:, 1, s], ALU.add)
            if last:
                m.then_inc(sem("xcomb1"), 1)

        def u_drain(g):
            if g == 0:
                modulation_row(0)
            s = slice(g * NB, (g + 1) * NB)
            drained(g // 2, "U", 8 * (g % 2 + 1))
            dve.tensor_tensor(y1[:, 1, s], lin[g % 2][1][:], gt_row[:, s], ALU.mult).then_inc(free1, 1)
            dve.wait_ge(free1, 2 + G0["U"] + g + 1)
            combine(y1, g, True, g == 3)
        dve.wait_ge(sem("x_in"), 32)
        for it in range(2):
            body(it, "U", 16, {11: [lambda it=it: u_drain(2 * it)], 19 - it: [lambda it=it: u_drain(2 * it + 1)]}, start=4 if it else 8)
        dve.wait_ge(sem("xcomb1"), 1)
        dve.nop().then_inc(sem("gt_used"), 1)

        def ffn(n, y):
            name = f"F{n + 1}"
            base = n * FB
            flat = lambda t: t[:].rearrange("p a t -> p (a t)")

            def hidden(j):
                dve.wait_ge(sem("up_T"), base + j + 1)
                if n == 0:
                    dve.wait_ge(sem("act_made"), j + 1)
                    for e in range(2):
                        m = dve.tensor_tensor(hidf[:, 2 * e:2 * e + 2, :].rearrange("p k t -> p (k t)"), aux[e][:],
                                              cacc[:, 2 * e:2 * e + 2, :].rearrange("p k t -> p (k t)"), ALU.mult)
                    m.then_inc(sem("hidf_made"), 1)
                    dve.wait_ge(sem("hid_h"), j + 1)
                    dve.tensor_tensor(hid_lo[:], hidf[:], hid_hi[:].bitcast(fp32), ALU.subtract).then_inc(sem("hid_made"), 1)
                else:
                    dve.wait_ge(sem("hid_h"), FB + 2 * j + 2)
                    for e in range(2):
                        m = dve.tensor_tensor(hid_lo[:, 2 * e:2 * e + 2, :].rearrange("p k t -> p (k t)"), aux[e][:],
                                              hid_hi[:, 2 * e:2 * e + 2, :].rearrange("p k t -> p (k t)").bitcast(fp32), ALU.subtract)
                    m.then_inc(sem("hid_made"), 1)

            def conv(j, e):
                if e == 0:
                    dve.wait_ge(sem("gpad_made"), j + 1)
                fs = (2 * e, 2 * e + 1)
                col = lambda w, f: w[:, ds(4 * j + f, 1)]
                for f in fs:
                    m = dve.tensor_scalar(cacc[:, f, :], gpad[:, f, 2:], col(conv_w2, f), col(conv_b, f), ALU.mult, ALU.add)
                m.then_inc(sem("conv_made"), 1)
                for k, w in ((1, conv_w1), (2, conv_w0)):
                    dve.wait_ge(sem("conv_made"), 6 * j + 3 * e + k)
                    for f in fs:
                        m = dve.scalar_tensor_tensor(cacc[:, f, :], gpad[:, f, 2 - k:2 - k + S], col(w, f), cacc[:, f, :], ALU.mult, ALU.add)
                    m.then_inc(sem("conv_made"), 1)

            def activate(j):
                dve.wait_ge(sem("csig_made"), base + j + 1)
                g = cacc if n == 0 else gbuf
                dve.tensor_tensor(flat(cacc), flat(g), flat(csig), ALU.mult).then_inc(sem("act_made"), 1)

            def up(it, phase, gi, upto, j):
                if n == 0:
                    drain(it, phase, gi, upto, ubuf[:, 1, :])
                else:
                    drained(it, phase, upto)
                    dve.wait_ge(sem("act_made"), base + j + 1)
                    dve.tensor_tensor(ubuf[:, 1, :], lin[gi % 2][1][:], flat(cacc)[:, NB:2 * NB], ALU.mult).then_inc(free1, 1)

            def down(it, phase, gper, gi, c, upto):
                drained(it, phase, upto)
                dve.wait_ge(free1, 2 + G0[phase] + it * gper + gi)
                s = slice(c * NB, (c + 1) * NB)
                dve.tensor_tensor(y[:, 1, s], y[:, 1, s], lin[gi % 2][1][:], ALU.add).then_inc(free1, 1)

            def hooks(it, phase, gper, j, ups):
                hk = {}
                add = lambda idx, f: hk.setdefault(idx, []).append(f)
                add(11, lambda: drain(it, phase, 0, 8, gbuf[:, 1, :]))
                if n == 0 and phase != name:
                    add(9, lambda: (dve.wait_ge(sem("tt_T"), 3 * KT // 2), link(dve.memset(gpad[:, :, 0:2], 0.0)),
                                    link(dve.memset(yacc[:, 1, :], 0.0))))
                if n == 0:
                    add(14, lambda: conv(j, 0))
                    add(16, lambda: conv(j, 1))
                add(18 if n == 0 else 16, lambda: activate(j))
                if phase == name:
                    add(5, lambda: hidden(it))
                    for c in range(4):
                        add(13 + 2 * c, lambda c=c: down(it, phase, gper, 1 + c, c, 10 + 2 * c))
                add(ups, lambda: up(it, phase, 1 if phase != name else 5, ups - AHEAD + 1, j))
                return hk
            body(0, name + "p", 16, hooks(0, name + "p", 2, 0, 19), start=8)
            with dve.Fori(0, FB - 1) as it:
                body(it, name, 24, hooks(it, name, 6, it + 1, 27))
            hidden(FB - 1)
            hk = {5 + 2 * c - (c == 3 and n == 0): [lambda c=c: down(0, name + "e", 4, c, c, 2 * c + 2)] for c in range(4)}
            if n == 0:
                def join(c):
                    dve.wait_ge(free1, 2 + G0["F1e"] + c + 1)
                    combine(y, c, False, c == 3)

                def first_two():
                    join(0)
                    join(1)
                hk[6] = [lambda: modulation_row(1)]
                hk[7].append(first_two)
                hk[9].append(lambda: join(2))
                hk[10].append(lambda: join(3))
                body(0, name + "e", 8, hk)
            else:
                for idx in range(4, 8):
                    split(0, name + "e", 8, idx)
                    for step in hk.get(idx, ()):
                        step()
                for idx in (9, 11):
                    hk[idx][0]()

        norm_stats(1)
        norm_rows(xs)
        features("F1p", False)
        ffn(0, yacc)

        dve.wait_ge(sem("late_in"), 48)
        for tb in (1, 0):
            dve.wait_ge(sem(f"xcomb{tb}"), 2)
            dve.tensor_tensor(xs[:, tb, :], X[:, tb, :], gfin[:], ALU.mult).then_inc(sem("xy_made"), 1)
        dve.wait_ge(sem("ss_made"), 8)
        link(dve.tensor_scalar(ss, ss, 1.0 / D, EPS, ALU.mult, ALU.add))
        link(dve.reciprocal(ry, ss))
        link(dve.tensor_tensor(ssy, ssy, ry, ALU.mult))
        dve.tensor_scalar(ssy, ssy, 1.0 / D, EPS, ALU.mult, ALU.add).then_inc(sem("ms_made"), 1)
        dve.wait_ge(sem("sd_made"), 3)
        link(dve.reciprocal(small[:, 116:120], small[:, 116:120]))
        dve.tensor_tensor(ry, rstd, rstdy, ALU.mult).then_inc(sem("rstd_made"), 1)
        dve.wait_ge(sem("rstd_made"), 3)
        dve.tensor_scalar(xs[:, 1, :], xs[:, 1, :], ry[:, 1:2], None, ALU.mult).then_inc(sem("xs_made"), 1)
        dve.wait_ge(sem("alr_hi_made"), 1)
        dve.tensor_tensor(alr_lo[:], alr_raw[:], alr_hi[:].bitcast(fp32), ALU.subtract).then_inc(sem("alr_split"), 1)
        features("GQ", False)
        def gq_drain(b):
            if b:
                dve.wait_ge(sem("gq_T"), b)
            drain(b // 2, "GQ", b % 2, 8 * (b % 2 + 1), gstage[:, 1, :])
        body(0, "GQ", 16, {11: [lambda: gq_drain(0)], 19: [lambda: gq_drain(1)]}, start=8)
        body(1, "GQ", 16, {11: [lambda: gq_drain(2)], 19: [lambda: gq_drain(3)]})
        for f in range(8):
            dve.wait_ge(sem("gu_T"), f + 1)
            dve.tensor_scalar(gu[:, f * S:(f + 1) * S], aux[f % 2][:, 0:S], gla_b[:, f:f + 1], None, ALU.add).then_inc(sem("gu_made"), 1)
        dve.wait_ge(sem("gu_made"), 8)
        dve.scalar_tensor_tensor(gt1[:], gu[:], -1.0, gu[:], ALU.mult, ALU.min).then_inc(sem("gabs"), 1)
        link(dve.tensor_scalar(gu[:], gu[:], 0.0, 1.0 / 16, ALU.min, ALU.mult))
        gvd = lambda it: drains2(it, "GV", lambda k: gv[:, 1, cols(it, k)])
        body(0, "GV", 16, gvd(0))
        dve.wait_ge(sem("gln"), 1)
        link(dve.scalar_tensor_tensor(gu[:], gt1[:], -1.0 / 16, gu[:], ALU.mult, ALU.add))
        dve.wait_ge(sem("greset_made"), 1)
        dve.tensor_tensor_scan(gb[:], greset[:], gu[:], 0.0, ALU.mult, ALU.add).then_inc(sem("gb_made"), 1)
        body(1, "GV", 16, gvd(1))
        dve.wait_ge(sem("late_in"), 48)

        def gate(it, k):
            n, g = 2 * it + k, gr[:, :, cols(it, k)]
            dve.wait_ge(sem("gsig_made"), n + 1)
            dve.tensor_tensor(g, g, gsig[:], ALU.mult).then_inc(sem("gr_gated"), 1)
            dve.wait_ge(sem("gr_gated"), n + 1)
            dve.tensor_tensor(g, g, gn[:].rearrange("p (a v) -> p a v", a=1).to_broadcast([P, TB, NB]), ALU.mult)

        def gr_body(it):
            hooks = drains2(it, "GR", lambda k: gr[:, 1, cols(it, k)])
            hooks[14] = [lambda: gate(it, 0)]
            hooks[19].append(lambda: gate(it, 1))
            body(it, "GR", 16, hooks)
        for it in range(2):
            gr_body(it)
        dve.wait_ge(half_used, H0["GO"])
        dve.wait_ge(free0, 2 + G0["GO"])
        dve.wait_ge(free1, 2 + G0["GO"])
        link(dve.memset(gq[:], 0.0))

        def zero(h):
            if h >= 2:
                dve.wait_ge(sem("go_T"), 2 * (h - 1))
            dve.memset(gsc[:, h % 2, :], 0.0).then_inc(sem("gsc_zero"), 1)

        def pick(h, lv):
            n = 7 * h + lv
            if lv == 0:
                dve.wait_ge(sem("gla_in"), 32)
                dve.wait_ge(sem("gsc_zero"), h + 1)
            dve.wait_ge(sem("gl_z"), n + 1)
            dve.wait_ge(sem("gl_picked"), n)
            dve.copy_predicated(gsc[:, h % 2, :], gmask[:, lv, :].bitcast(u32), aux[n % 2][:, 0:S]).then_inc(sem("gl_picked"), 1)

        def decayed(h, i):
            n, lv = 7 * h + i, GL_ITEMS[i]
            dve.wait_ge(sem("gl_e"), n + 1)
            if lv == 0:
                if h >= 2:
                    dve.wait_ge(sem("gk_T"), h - 1)
                dve.tensor_tensor(gkd[:, h % 2, :], gla_k(h), ge[:, n % 4, :], ALU.mult).then_inc(sem("gk_dec"), 1)
                dve.wait_ge(sem("gk_dec"), h + 1)
                dve.nop().then_inc(sem("gl_m"), 1)
                return
            j = 6 * h + lv - 1
            if j >= 3:
                dve.wait_ge(sem("gl_z"), 7 * ((j - 3) // 6) + (j - 3) % 6 + 2)
            m = LEVELS[lv - 1]
            e, o = pairs_by(ge[:, n % 4, :], m), pairs_by(gm[:, j % 3, :], m)
            dve.tensor_tensor(o[:, :, 1, :], pairs_by(gla_q(h), m)[:, :, 1, :], e[:, :, 1, :], ALU.mult)
            dve.tensor_tensor(o[:, :, 0, :], pairs_by(gla_k(h), m)[:, :, 0, :], e[:, :, 0, :], ALU.mult).then_inc(sem("gl_m"), 1)

        def queries(h):
            dve.wait_ge(sem("geb_made"), h + 1)
            if h >= 2:
                dve.wait_ge(sem("go_T"), 2 * (h - 1))
            q3, e3 = (t.rearrange("p (e t) -> p e t", e=2) for t in (gla_q(h), geb[:, h % 2, :]))
            for c in range(3):
                t, o = slice((c + 1) * GC, (c + 2) * GC), (c + 1) % 2 * GC
                m = dve.tensor_tensor(gq[:, h % 2, c, :, o:o + GC], q3[:, :, t], e3[:, :, t], ALU.mult)
            m.then_inc(sem("gq_made"), 1)

        def state(h, n):
            c, e, i = n // 2, n % 2, 6 * h + n
            dve.wait_ge(sem("gs_T"), i + 1)
            bank = lin[i % 4 // 2][i % 2][:]
            if c == 0:
                if h and e == 0:
                    dve.wait_ge(sem("go_T"), 2 * h)
                dve.tensor_copy(sts[:, 0, e, :], bank).then_inc(sem("gs_added"), 1)
            else:
                dve.wait_ge(sem("gs_added"), i - 1)
                last = e * S + (c + 1) * GC - 1
                dve.scalar_tensor_tensor(sts[:, c, e, :], sts[:, c - 1, e, :], geb[:, h % 2, last:last + 1], bank,
                                         ALU.mult, ALU.add).then_inc(sem("gs_added"), 1)

        for h in range(GH + 1):
            for i in range(7):
                if h < GH:
                    if i == 0:
                        zero(h)
                    decayed(h, i)
                    lv = GL_ITEMS[i]
                    if lv:
                        pick(h, lv - 1)
                    if i == 3:
                        queries(h)
                    if i == 6:
                        pick(h, 6)
                if h and i in (1, 3, 4):
                    for e in range(2):
                        state(h - 1, 2 * (1, 3, 4).index(i) + e)
        dve.wait_ge(sem("gss_made"), TB * GH)
        dve.tensor_scalar(gss[:], gss[:], 1.0 / GV, EPS, ALU.mult, ALU.add).then_inc(sem("gms_made"), 1)
        dve.wait_ge(sem("gsd_made"), 1)
        link(dve.reciprocal(grs, grs))
        dve.wait_ge(sem("go_held"), TB * GH)
        for h in range(GH):
            for tb in range(TB):
                n = tb * GH + h
                m = dve.scalar_tensor_tensor(gla_v(h, tb), gla_v(h, tb), grs[:, n:n + 1], gr[:, tb, h * GV:(h + 1) * GV], ALU.mult, ALU.mult)
            m.then_inc(sem("go_done"), 1)
        features("GO", True)

        def go_drain(g):
            s = slice(g * NB, (g + 1) * NB)
            drained(g // 2, "GO", 8 * (g % 2 + 1))
            dve.tensor_tensor(X[:, 1, s], X[:, 1, s], lin[g % 2][1][:], ALU.add).then_inc(free1, 1)
        for it in range(2):
            body(it, "GO", 16, {11: [lambda it=it: go_drain(2 * it)], 19 - it: [lambda it=it: go_drain(2 * it + 1)]}, start=4 if it else 8)
        dve.wait_ge(free1, 2 + G0["F2p"])
        dve.nop().then_inc(sem("xcomb1"), 1)
        norm_stats(3)
        norm_rows(xs)
        features("F2p", False)
        ffn(1, X)

    @block.gpsimd
    def _(pool):
        steps = [0]

        def link(op):
            steps[0] += 1
            op.then_inc(sem("pool_link"), 1)
            pool.wait_ge(sem("pool_link"), steps[0])

        def ada(n, kt, half, col):
            c = slice(half * (D // 2), (half + 1) * (D // 2))
            pool.wait_ge(ada_come[half], 8 * (n - half) + 16)
            pool.wait_ge(sem("ada_sum"), n)
            pool.tensor_tensor(ada_in[:, half, :], ada_in[:, half, :], col.to_broadcast([P, D // 2]), ALU.mult).then_inc(sem("ada_mul"), 1)
            pool.wait_ge(sem("ada_mul"), n + 1)
            pool.tensor_tensor(ada_acc[:, c], ada_acc[:, c], ada_in[:, half, :], ALU.add).then_inc(sem("ada_sum"), 1)
            pool.wait_ge(sem("ada_sum"), n + 1)
            pool.nop().then_inc(ada_left, 1)

        def pairs_of(n, kt, count):
            pool.tensor_copy(acol, cact[:, ds(kt, 1)]).then_inc(sem("acol_made"), 1)
            pool.wait_ge(sem("acol_made"), count + 1)
            for half in range(2):
                ada(n + half, kt, half, acol)

        def clear(piece):
            if piece:
                pool.wait_ge(sem("ada_T"), piece)
            link(pool.memset(ada_acc[:], 0.0))

        pool.wait_ge(sem("cact_made"), 1)
        clear(0)
        for k in range(8):
            pairs_of(2 * k, k, k)
        with pool.Fori(0, 2) as it:
            for k in range(4):
                pairs_of(8 * it + 2 * k + 16, 4 * it + k + 8, 4 * it + k + 8)

        def sb_stage(h, u):
            pool.tensor_copy(st_sb[:, u, :, :, :],
                             sbz[:].rearrange("p t (w h d) -> p w t h d", w=3, h=NH)[:, :, :, ds(h, 1), :].rearrange("p w t a d -> p w t (a d)")).then_inc(sem("sb_staged"), 1)
        pool.wait_ge(free0, 2 + G0["B"])
        pool.wait_ge(free1, 2 + G0["B"])
        sb_stage(0, 0)
        sb_stage(1, 1)
        clear(1)

        def b_pool(it, more):
            for u in range(2):
                kk = 2 * it + u
                pairs_of(32 + 2 * kk, kk, 16 + kk)
                if more:
                    pool.wait_ge(sem("sb_o"), 2 * it + u + 1)
                    sb_stage(2 * it + u + 2, u)
        with pool.Fori(0, 3) as it:
            b_pool(it, True)
        b_pool(3, False)

        def ix_stage(p, u):
            pool.tensor_copy(st_ix[:, u % 2, :, :], qix[:, :, ds(p * P, P)]).then_inc(sem("ix_staged"), 1)
        pool.wait_ge(free0, 2 + G0["C1"])
        pool.wait_ge(free1, 2 + G0["C1"])
        pool.wait_ge(sem("sb_o"), NH)
        ix_stage(0, 0)
        ix_stage(1, 1)

        def c_pool(it, n0, k0, stages):
            for u in range(4):
                kk = 4 * it + u + k0
                pairs_of(n0 + 2 * kk, kk, n0 // 2 + kk)
                for st in stages[u]:
                    st()

        def ix_next(it, u):
            pool.wait_ge(sem("ix_T"), 4 * it + u + 1)
            ix_stage(4 * it + u + 2, u)
        c_pool(0, 32, 8, [[lambda u=u: ix_next(0, u)] for u in range(4)])
        c_pool(1, 32, 8, [[lambda u=u: ix_next(1, u)] if u < 2 else [] for u in range(4)])

        def qk_stage(h, u):
            src = dsz[:].rearrange("p t (w h d) -> p w t h d", w=3, h=NH)[:, 0:2, :, ds(h, 1), :].rearrange("p w t a d -> p w t (a d)")
            pool.tensor_copy(st_qk[:, u % 2, :, :, :], src).then_inc(sem("ds_qk_staged"), 1)

        def v_stage(h, u):
            pool.tensor_copy(st_v[:, u % 2, :, :], dsz[:, :, ds(h * HD + 2 * W, HD)]).then_inc(sem("ds_v_staged"), 1)

        for u in range(2):
            qk_stage(u, u)
            v_stage(u, u)

        def qk_next(it, u):
            pool.wait_ge(sem("ds_T"), 4 * it + u - 1)
            qk_stage(4 * it + u, u)

        def v_next(it, u):
            pool.wait_ge(sem("ds_o"), 4 * it + u - 1)
            v_stage(4 * it + u, u)

        clear(2)

        def ds_pool(it, more):
            q, v = (lambda u: lambda: qk_next(it, u)), (lambda u: lambda: v_next(it, u))
            after = [[q(2), q(3)], [v(2)], [q(4), q(5)] if more else [], [v(3)] + ([v(4), v(5)] if more else [])]
            if more:
                after = [[q(2), q(3)], [v(2), q(4)], [q(5), v(3)], [v(4), v(5)]]
            c_pool(it, 64, 0, after)
        ds_pool(0, True)
        ds_pool(1, False)

        for kk in range(8, 16):
            pairs_of(64 + 2 * kk, kk, 32 + kk)

        def combine(y, c, row, last=False):
            s = slice(c * NB, (c + 1) * NB)
            if row is not None:
                pool.wait_ge(sem("gt_made"), row + 1)
                link(pool.tensor_tensor(y[:, 0, s], y[:, 0, s], gt_row[:, s], ALU.mult))
            m = pool.tensor_tensor(X[:, 0, s], X[:, 0, s], y[:, 0, s], ALU.add)
            if last:
                m.then_inc(sem("xcomb0"), 1)
        clear(3)
        pool.wait_ge(sem("x_in"), 32)
        for g in range(4):
            pool.wait_ge(free0, 2 + G0["U"] + g + 1)
            combine(y1, g, 0, g == 3)
            if g < 3:
                for k in ((), (0, 1), (2, 3))[g]:
                    pairs_of(96 + 2 * k, k, 48 + k)
        pool.wait_ge(sem("xcomb0"), 1)
        pool.nop().then_inc(sem("gt_used"), 1)

        def ffn(n, y):
            name = f"F{n + 1}"
            base = n * FB

            def down(it, phase, gper, gi, c):
                k = n * 4 * FB + (0 if phase == name else 4 * (FB - 1)) + 4 * it + c
                pool.wait_ge(free0, 2 + G0[phase] + it * gper + gi + 1)
                pool.wait_ge(sem("dstage_free"), 2 + k)
                s = slice(c * NB, (c + 1) * NB)
                pool.tensor_tensor(y[:, 0, s], y[:, 0, s], dstage[:, c % 2, :], ALU.add).then_inc(sem("dstage_free"), 1)

            def up(g, j):
                if n == 1:
                    pool.wait_ge(free0, g)
                    pool.wait_ge(sem("act_made"), base + j + 1)
                    pool.tensor_tensor(ubuf[:, 0, :], ubuf[:, 0, :], cacc[:].rearrange("p a t -> p (a t)")[:, 0:NB], ALU.mult).then_inc(sem("up_mul"), 1)

            if n == 0:
                for k in range(4, 6):
                    pairs_of(96 + 2 * k, k, 48 + k)
            up(2 + G0[name + "p"] + 2, 0)
            with pool.Fori(0, FB - 1) as it:
                if n == 0:
                    pairs_of(108 + 2 * it, 6 + it, 54 + it)
                for c in range(4):
                    down(it, name, 6, 1 + c, c)
                up(2 + G0[name] + 6 * it + 6, it + 1)
            for c in range(4):
                down(0, name + "e", 4, c, c)
                if n == 0:
                    pool.wait_ge(sem("dstage_free"), 2 + 4 * (FB - 1) + c + 1)
                    combine(y, c, 1, c == 3)

        link(pool.memset(yacc[:, 0, :], 0.0))
        pool.nop().then_inc(sem("dstage_free"), 1)
        pool.nop().then_inc(sem("dstage_free"), 1)
        ffn(0, yacc)
        pool.wait_ge(sem("rstd_made"), 3)
        for tb in (0, 1):
            link(pool.tensor_scalar(X[:, tb, :], X[:, tb, :], rstd[:, tb:tb + 1], None, ALU.mult))
            m = pool.tensor_tensor(X[:, tb, :], X[:, tb, :], gfin[:], ALU.mult)
        m.then_inc(sem("xfin"), 1)
        link(pool.memset(greset[:], 1.0))
        pool.memset(greset[:].rearrange("p (c t) -> p c t", t=GC)[:, :, 0:1], 0.0).then_inc(sem("greset_made"), 1)
        pool.wait_ge(sem("gb_made"), 1)
        pool.wait_ge(half_used, H0["GO"])
        for h in range(GH):
            for i, lv in enumerate(GL_ITEMS):
                n = 7 * h + i
                if n >= 4:
                    pool.wait_ge(sem("gl_m"), n - 3)
                if lv:
                    m = LEVELS[lv - 1]
                    b, e = pairs_by(gla_sums(h), m), pairs_by(ge[:, n % 4, :], m)
                    ref = b[:, :, 0, m - 1:m].to_broadcast([P, 2 * S // (2 * m), m])
                    pool.tensor_tensor(e[:, :, 1, :], b[:, :, 1, :], ref, ALU.subtract)
                    pool.tensor_tensor(e[:, :, 0, :], ref, b[:, :, 0, :], ALU.subtract).then_inc(sem("gl_d"), 1)
                else:
                    b, e = (t.rearrange("p (c t) -> p c t", t=GC) for t in (gla_sums(h), ge[:, n % 4, :]))
                    pool.tensor_tensor(e, b[:, :, GC - 1:GC].to_broadcast([P, 8, GC]), b, ALU.subtract).then_inc(sem("gl_d"), 1)
        for g in range(4):
            pool.wait_ge(free0, 2 + G0["GO"] + g + 1)
            combine(y1, g, None, g == 3)
        ffn(1, X)

    ctx.close()


INPUTS = ("x", "c", "w_ada", "b_ada", "g_mix", "w_in", "w_o_sb", "w_o_dsa", "w_out", "rel_bias", "g_ffn", "w_gate", "w_up",
          "conv_w", "conv_b", "w_down", "g_final", "norm_g_2", "gla_w_in_2", "gla_w_a2_2", "gla_b_a_2", "gla_g_norm_2",
          "gla_w_out_2", "ffn_w_gu_2", "ffn_w_down_2")


def constants():
    import numpy as np
    i = np.arange(P)
    key, query = i[:, None], i[None, :]
    con = np.zeros((P, 10, P), np.float32)
    con[:, 0] = key == query
    con[:, 1] = key + query == P - 1
    con[:, 2] = 1
    con[:, 3] = key > query
    con[:, 4] = con[:, 6] = key < query
    con[:, 5] = 1
    con[:, 7] = con[:, 9] = np.where(query > key, NEG, 0)
    dist = np.maximum(S - 1 - np.arange(2 * S), 0)
    exact = BUCKETS // 2
    far = exact + (np.log(np.maximum(dist, 1).astype(np.float32) / np.float32(exact))
                   / np.float32(np.log(128 / exact)) * np.float32(BUCKETS - exact)).astype(np.int32)
    bucket = np.where(dist < exact, dist, np.minimum(far, BUCKETS - 1))
    onehot = (np.arange(BUCKETS)[:, None] == bucket[None, :]).astype(np.float32)
    levels = np.zeros((P, 7, TB, P), np.float32)
    levels[:, 0] = (key == query)[:, None]
    for n, m in enumerate(LEVELS):
        levels[:, n + 1] = ((key // (2 * m) == query // (2 * m)) & (key // m < query // m))[:, None]
    return {"k_con": con.reshape(P, 10 * P), "k_onehot": onehot, "k_levels": levels.reshape(P, 7, S)}


def kernel(**inputs):
    import numpy as np
    import concourse.bacc as bacc
    from concourse.bass_utils import run_bass_kernel_spmd

    nc = bacc.Bacc("TRN2", target_bir_lowering=False, num_devices=1, dynamic_dma_scratch_size=1024)
    arrays, A = {}, {}
    given = {name: np.ascontiguousarray(inputs[name]) for name in INPUTS}
    for name, a in list(given.items()) + list(constants().items()):
        arrays[f"in_{name}_dram"] = a
        A[name] = nc.dram_tensor(f"in_{name}_dram", a.shape, mybir.dt.from_np(a.dtype), kind="ExternalInput").ap()
    out = nc.dram_tensor("out_0_dram", (1, S, D), mybir.dt.float32, kind="ExternalOutput").ap()
    build_program(nc, A, out)
    r = run_bass_kernel_spmd(nc, [arrays], core_ids=[0])
    return r.results[0]["out_0_dram"]
```
